# Optimizing a Trainium2 kernel written in Bass

```python
import jax, jax.numpy as jnp
from jax import lax
import numpy as np
import math

D_MODEL = 1024
BATCH = 1
SEQ = 256
DEPTH = 1

D_FF = 2816
A_HEADS = 8
A_HEAD_DIM = 64
A_WIDTH = A_HEADS * A_HEAD_DIM
MOBA_BLOCK = 256
MOBA_TOPK = 3
Q_CHUNK = 64
G_GROUPS = 8
G_CHUNK = 128
G_WIDTH = 512
G_GROUP_DIM = G_WIDTH // G_GROUPS
IN_WIDTH = 3 * A_WIDTH + 2 * G_WIDTH
N_BRANCHES = 2
EPS = 1e-6


def rmsnorm(x, g):
    xf = x.astype(jnp.float32)
    y = xf * lax.rsqrt(jnp.mean(xf * xf, axis=-1, keepdims=True) + EPS)
    return (y * g.astype(jnp.float32)).astype(x.dtype)

def layernorm(x, g, b):
    xf = x.astype(jnp.float32)
    mu = jnp.mean(xf, axis=-1, keepdims=True)
    var = jnp.mean(jnp.square(xf - mu), axis=-1, keepdims=True)
    y = (xf - mu) * lax.rsqrt(var + EPS)
    return (y * g.astype(jnp.float32) + b.astype(jnp.float32)).astype(x.dtype)

def swiglu(x, w_gate, w_up, w_down):
    return (jax.nn.silu(x @ w_gate) * (x @ w_up)) @ w_down

def moba_attention(q, k, v):
    B, H, S, Dh = q.shape
    n_blocks = -(-S // MOBA_BLOCK)
    s_pad = n_blocks * MOBA_BLOCK
    k_sel = min(MOBA_TOPK, n_blocks)
    pad = ((0, 0), (0, 0), (0, s_pad - S), (0, 0))
    kp = jnp.pad(k, pad)
    vp = jnp.pad(v, pad)
    kb = kp.reshape(B, H, n_blocks, MOBA_BLOCK, Dh)
    vb = vp.reshape(B, H, n_blocks, MOBA_BLOCK, Dh)
    k_mean = jnp.mean(kb.astype(jnp.float32), axis=3)
    scale = Dh ** -0.5
    b_idx = jnp.arange(B)[:, None, None, None]
    h_idx = jnp.arange(H)[None, :, None, None]
    block_ids = jnp.arange(n_blocks)

    def one_chunk(c):
        start = c * Q_CHUNK
        qc = lax.dynamic_slice_in_dim(q, start, Q_CHUNK, axis=2) * scale
        own = start // MOBA_BLOCK
        gate = jnp.einsum('bhqd,bhnd->bhqn', qc.astype(jnp.float32), k_mean)
        gate = jnp.where(block_ids < own, gate, -jnp.inf)
        top_s, top_i = lax.top_k(gate, k_sel)
        valid = jnp.isfinite(top_s)
        kg = kb[b_idx, h_idx, top_i]
        vg = vb[b_idx, h_idx, top_i]
        s_sel = jnp.einsum('bhqd,bhqkpd->bhqkp', qc, kg).astype(jnp.float32)
        s_sel = jnp.where(valid[..., None], s_sel, -jnp.inf)
        k_own = lax.dynamic_slice_in_dim(kp, own * MOBA_BLOCK, MOBA_BLOCK, axis=2)
        v_own = lax.dynamic_slice_in_dim(vp, own * MOBA_BLOCK, MOBA_BLOCK, axis=2)
        s_own = jnp.einsum('bhqd,bhpd->bhqp', qc, k_own).astype(jnp.float32)
        q_pos = start + jnp.arange(Q_CHUNK)
        k_pos = own * MOBA_BLOCK + jnp.arange(MOBA_BLOCK)
        s_own = jnp.where(k_pos[None, :] <= q_pos[:, None], s_own, -jnp.inf)
        logits = jnp.concatenate([s_sel.reshape(B, H, Q_CHUNK, k_sel * MOBA_BLOCK), s_own], axis=-1)
        p = jax.nn.softmax(logits, axis=-1)
        p_sel = p[..., :k_sel * MOBA_BLOCK].reshape(B, H, Q_CHUNK, k_sel, MOBA_BLOCK).astype(v.dtype)
        p_own = p[..., k_sel * MOBA_BLOCK:].astype(v.dtype)
        return (jnp.einsum('bhqkp,bhqkpd->bhqd', p_sel, vg)
                + jnp.einsum('bhqp,bhpd->bhqd', p_own, v_own))

    outs = lax.map(one_chunk, jnp.arange(S // Q_CHUNK))
    return outs.transpose(1, 2, 0, 3, 4).reshape(B, H, S, Dh)

def chunked_spatial_gating(u, v, ln_g, ln_b, w_s, b_s):
    B, S, _ = v.shape
    v = layernorm(v, ln_g, ln_b)
    n_chunks = S // G_CHUNK
    vc = v.reshape(B, n_chunks, G_CHUNK, G_GROUPS, G_GROUP_DIM)
    causal = jnp.tril(jnp.ones((G_CHUNK, G_CHUNK), dtype=bool))
    w = jnp.where(causal[None], w_s, jnp.zeros((), w_s.dtype))
    mixed = jnp.einsum('gij,bcjgd->bcigd', w, vc) + b_s.T[None, None, :, :, None]
    return u * mixed.reshape(B, S, G_WIDTH)

def first_inputs(seed: int = 0) -> dict:
    key = jax.random.key(seed)
    ks = jax.random.split(key, 24)
    L, D = DEPTH, D_MODEL

    def w(k, shape, fan_in, mult=1.0):
        return jax.random.normal(k, shape, jnp.float32) * (mult * fan_in ** -0.5)

    def gain(k, shape):
        return 1.0 + 0.05 * jax.random.normal(k, shape, jnp.float32)

    def bias(k, shape, s=0.02):
        return s * jax.random.normal(k, shape, jnp.float32)

    return {
        "x": jax.random.normal(ks[0], (BATCH, SEQ, D), jnp.float32),
        "ffn1_norm": gain(ks[1], (L, D)),
        "ffn1_w_gate": w(ks[2], (L, D, D_FF), D),
        "ffn1_w_up": w(ks[3], (L, D, D_FF), D),
        "ffn1_w_down": w(ks[4], (L, D_FF, D), D_FF),
        "mix_norm": gain(ks[5], (L, D)),
        "w_in": w(ks[6], (L, D, IN_WIDTH), D),
        "gmlp_ln_g": gain(ks[7], (L, G_WIDTH)),
        "gmlp_ln_b": bias(ks[8], (L, G_WIDTH)),
        "gmlp_w_s": w(ks[9], (L, G_GROUPS, G_CHUNK, G_CHUNK), G_CHUNK, 0.5),
        "gmlp_b_s": 1.0 + bias(ks[10], (L, G_GROUPS, G_CHUNK), 0.05),
        "w_branch_attn": w(ks[11], (L, A_WIDTH, D), A_WIDTH),
        "w_branch_gmlp": w(ks[12], (L, G_WIDTH, D), G_WIDTH),
        "w_gate": w(ks[13], (L, D, N_BRANCHES * D), D),
        "b_gate": bias(ks[14], (L, N_BRANCHES * D)),
        "w_out": w(ks[15], (L, D, D), D),
        "ffn2_norm": gain(ks[16], (L, D)),
        "ffn2_w_gate": w(ks[17], (L, D, D_FF), D),
        "ffn2_w_up": w(ks[18], (L, D, D_FF), D),
        "ffn2_w_down": w(ks[19], (L, D_FF, D), D_FF),
        "final_norm": gain(ks[20], (D,)),
    }

def first_block(x, ffn1_norm, ffn1_w_gate, ffn1_w_up, ffn1_w_down, mix_norm, w_in,
              gmlp_ln_g, gmlp_ln_b, gmlp_w_s, gmlp_b_s, w_branch_attn, w_branch_gmlp,
              w_gate, b_gate, w_out, ffn2_norm, ffn2_w_gate, ffn2_w_up, ffn2_w_down,
              final_norm):
    B, S, D = x.shape
    h = x
    for l in range(DEPTH):
        h = h + 0.5 * swiglu(rmsnorm(h, ffn1_norm[l]), ffn1_w_gate[l], ffn1_w_up[l], ffn1_w_down[l])

        n = rmsnorm(h, mix_norm[l])
        z = n @ w_in[l]
        q = z[..., :A_WIDTH]
        k = z[..., A_WIDTH:2 * A_WIDTH]
        v = z[..., 2 * A_WIDTH:3 * A_WIDTH]
        to_heads = lambda t: t.reshape(B, S, A_HEADS, A_HEAD_DIM).transpose(0, 2, 1, 3)
        attn = moba_attention(to_heads(q), to_heads(k), to_heads(v))
        attn = attn.transpose(0, 2, 1, 3).reshape(B, S, A_WIDTH)

        zg = jax.nn.gelu(z[..., 3 * A_WIDTH:])
        gm = chunked_spatial_gating(zg[..., :G_WIDTH], zg[..., G_WIDTH:],
                                    gmlp_ln_g[l], gmlp_ln_b[l], gmlp_w_s[l], gmlp_b_s[l])

        y_attn = attn @ w_branch_attn[l]
        y_gmlp = gm @ w_branch_gmlp[l]
        gates = jax.nn.sigmoid(n @ w_gate[l] + b_gate[l])
        merged = gates[..., :D] * y_attn + gates[..., D:] * y_gmlp
        h = h + merged @ w_out[l]

        h = h + 0.5 * swiglu(rmsnorm(h, ffn2_norm[l]), ffn2_w_gate[l], ffn2_w_up[l], ffn2_w_down[l])
    return rmsnorm(h, final_norm)


N_META = 16
NORM_EPS = 1e-6
HG_HEADS = 8
HG_DK = D_MODEL // HG_HEADS
HG_DV = D_MODEL // HG_HEADS
HG_WIDTH = HG_HEADS * HG_DK
HG_CHUNK = 16
MLA_HEADS = 8
QK_NOPE = 128
QK_ROPE = 64
V_HEAD = 128
Q_LORA = 256
KV_LORA = 256
ROPE_THETA = 10000.0
ATTN_BLOCK = 128
FFN_HIDDEN = ((8 * D_MODEL + 3 * 256 - 1) // (3 * 256)) * 256
IN_SIZES = (HG_WIDTH, HG_WIDTH, HG_WIDTH, HG_WIDTH,
            Q_LORA, KV_LORA, QK_ROPE,
            D_MODEL, D_MODEL)
IN_COLS = sum(IN_SIZES)


def rms_norm(x, g):
    xf = x.astype(jnp.float32)
    y = xf * lax.rsqrt(jnp.mean(xf * xf, axis=-1, keepdims=True) + NORM_EPS)
    return (y * g.astype(jnp.float32)).astype(x.dtype)

def rope_tables(length):
    pos = jnp.arange(length, dtype=jnp.float32)
    inv_freq = 1.0 / (ROPE_THETA ** (jnp.arange(0, QK_ROPE, 2, dtype=jnp.float32) / QK_ROPE))
    ang = pos[:, None] * inv_freq[None, :]
    return jnp.cos(ang), jnp.sin(ang)

def apply_rope(t, cos, sin):
    t32 = t.astype(jnp.float32)
    t1, t2 = jnp.split(t32, 2, axis=-1)
    return jnp.concatenate([t1 * cos - t2 * sin, t2 * cos + t1 * sin], axis=-1).astype(t.dtype)

def hgrn2_chunk_scan(q, k, v, logf):
    B, L, H, _ = q.shape
    n = L // HG_CHUNK

    def to_chunks(t):
        return t.reshape(B, n, HG_CHUNK, H, t.shape[-1]).transpose(1, 0, 3, 2, 4)

    xs = (to_chunks(q), to_chunks(k), to_chunks(v), to_chunks(logf))
    causal = jnp.tril(jnp.ones((HG_CHUNK, HG_CHUNK), dtype=bool))[:, :, None]

    def step(S, inp):
        qb, kb, vb, gb = inp
        b = jnp.cumsum(gb, axis=2)
        o_inter = jnp.einsum('bhtk,bhkv->bhtv', qb * jnp.exp(b), S)
        diff = b[:, :, :, None, :] - b[:, :, None, :, :]
        decay = jnp.exp(jnp.where(causal, diff, -jnp.inf))
        A = jnp.einsum('bhtsk,bhsk->bhts', decay * qb[:, :, :, None, :], kb)
        o_intra = jnp.einsum('bhts,bhsv->bhtv', A, vb)
        b_last = b[:, :, -1:, :]
        S_new = jnp.exp(b_last[:, :, 0, :])[..., None] * S + jnp.einsum(
            'bhsk,bhsv->bhkv', kb * jnp.exp(b_last - b), vb)
        return S_new, o_inter + o_intra

    S0 = jnp.zeros((B, H, q.shape[-1], v.shape[-1]), jnp.float32)
    _, ys = lax.scan(step, S0, xs)
    return ys.transpose(1, 0, 3, 2, 4).reshape(B, L, H, v.shape[-1])

def hgrn2_mixer(q, f_pre, i, g, lb, norm_g):
    B, L, _ = q.shape
    split = lambda t: t.reshape(B, L, HG_HEADS, -1).astype(jnp.float32)
    qh = jax.nn.silu(split(q))
    lbh = lb.astype(jnp.float32).reshape(HG_HEADS, HG_DK)
    fgate = lbh + (1.0 - lbh) * jax.nn.sigmoid(split(f_pre))
    o = hgrn2_chunk_scan(qh, 1.0 - fgate, split(i), jnp.log(fgate))
    o = rms_norm(o, norm_g) * jax.nn.silu(split(g))
    return o.reshape(B, L, HG_WIDTH).astype(q.dtype)

def mla_mixer(c_q, c_kv, k_pe, q_norm_g, w_q_b, kv_norm_g, w_kv_b, cos, sin):
    B, L, _ = c_q.shape
    q = (rms_norm(c_q, q_norm_g) @ w_q_b).reshape(B, L, MLA_HEADS, QK_NOPE + QK_ROPE)
    q_nope = q[..., :QK_NOPE]
    q_pe = apply_rope(q[..., QK_NOPE:], cos[:, None, :], sin[:, None, :])
    kv = (rms_norm(c_kv, kv_norm_g) @ w_kv_b).reshape(B, L, MLA_HEADS, QK_NOPE + V_HEAD)
    k_nope, v = kv[..., :QK_NOPE], kv[..., QK_NOPE:]
    k_pe = apply_rope(k_pe, cos, sin)
    scale = (QK_NOPE + QK_ROPE) ** -0.5
    bounds = [(0, N_META)] + [(N_META + s, min(N_META + s + ATTN_BLOCK, L))
                              for s in range(0, L - N_META, ATTN_BLOCK)]
    outs = []
    for start, end in bounds:
        s = (jnp.einsum('bqhd,bkhd->bhqk', q_nope[:, start:end], k_nope[:, :end])
             + jnp.einsum('bqhr,bkr->bhqk', q_pe[:, start:end], k_pe[:, :end]))
        s = s.astype(jnp.float32) * scale
        qpos = jnp.arange(start, end)[:, None]
        kpos = jnp.arange(end)[None, :]
        s = jnp.where(kpos <= qpos, s, -jnp.inf)
        p = jax.nn.softmax(s, axis=-1).astype(v.dtype)
        outs.append(jnp.einsum('bhqk,bkhd->bqhd', p, v[:, :end]))
    o = jnp.concatenate(outs, axis=1)
    return o.reshape(B, L, MLA_HEADS * V_HEAD)

def second_inputs(seed: int = 0) -> dict:
    key = jax.random.key(seed)
    ks = jax.random.split(key, 20)
    nrm = lambda k, shape, scale: jax.random.normal(k, shape, jnp.float32) * scale
    gain = lambda k, shape: 1.0 + 0.02 * jax.random.normal(k, shape, jnp.float32)
    return {
        "x": nrm(ks[0], (BATCH, SEQ, D_MODEL), 1.0),
        "meta_tokens": nrm(ks[1], (N_META, D_MODEL), 1.0),
        "w_in": nrm(ks[2], (DEPTH, D_MODEL, IN_COLS), D_MODEL ** -0.5),
        "b_gate": nrm(ks[3], (DEPTH, 2 * D_MODEL), 0.01),
        "lb_logits": nrm(ks[4], (DEPTH + 1, HG_WIDTH), 0.1),
        "hg_norm_g": gain(ks[5], (DEPTH, HG_DV)),
        "w_hg_o": nrm(ks[6], (DEPTH, HG_WIDTH, D_MODEL), HG_WIDTH ** -0.5),
        "q_a_norm_g": gain(ks[7], (DEPTH, Q_LORA)),
        "w_q_b": nrm(ks[8], (DEPTH, Q_LORA, MLA_HEADS * (QK_NOPE + QK_ROPE)), Q_LORA ** -0.5),
        "kv_a_norm_g": gain(ks[9], (DEPTH, KV_LORA)),
        "w_kv_b": nrm(ks[10], (DEPTH, KV_LORA, MLA_HEADS * (QK_NOPE + V_HEAD)), KV_LORA ** -0.5),
        "w_mla_o": nrm(ks[11], (DEPTH, MLA_HEADS * V_HEAD, D_MODEL), (MLA_HEADS * V_HEAD) ** -0.5),
        "w_out": nrm(ks[12], (DEPTH, D_MODEL, D_MODEL), D_MODEL ** -0.5),
        "mix_pre_g": gain(ks[13], (DEPTH, D_MODEL)),
        "mix_post_g": gain(ks[14], (DEPTH, D_MODEL)),
        "ffn_pre_g": gain(ks[15], (DEPTH, D_MODEL)),
        "ffn_post_g": gain(ks[16], (DEPTH, D_MODEL)),
        "w_ffn_in": nrm(ks[17], (DEPTH, D_MODEL, 2 * FFN_HIDDEN), D_MODEL ** -0.5),
        "w_ffn_out": nrm(ks[18], (DEPTH, FFN_HIDDEN, D_MODEL), FFN_HIDDEN ** -0.5),
    }

def second_block(x, meta_tokens, w_in, b_gate, lb_logits, hg_norm_g, w_hg_o, q_a_norm_g, w_q_b,
              kv_a_norm_g, w_kv_b, w_mla_o, w_out, mix_pre_g, mix_post_g, ffn_pre_g, ffn_post_g,
              w_ffn_in, w_ffn_out):
    B = x.shape[0]
    meta = jnp.broadcast_to(meta_tokens[None].astype(x.dtype), (B, N_META, D_MODEL))
    h = jnp.concatenate([meta, x], axis=1)
    L = h.shape[1]
    cos, sin = rope_tables(L)
    lower_bounds = jnp.cumsum(jax.nn.softmax(lb_logits.astype(jnp.float32), axis=0), axis=0)
    splits = []
    acc = 0
    for sz in IN_SIZES[:-2]:
        acc += sz
        splits.append(acc)
    for l in range(DEPTH):
        u = rms_norm(h, mix_pre_g[l])
        proj = u @ w_in[l]
        hq, hf, hi, hg, cq, ckv, kpe, gates = jnp.split(proj, splits, axis=-1)
        y_a = hgrn2_mixer(hq, hf, hi, hg, lower_bounds[l], hg_norm_g[l]) @ w_hg_o[l]
        y_b = mla_mixer(cq, ckv, kpe, q_a_norm_g[l], w_q_b[l], kv_a_norm_g[l], w_kv_b[l],
                        cos, sin) @ w_mla_o[l]
        gate_a, gate_b = jnp.split(jax.nn.sigmoid(gates + b_gate[l]), 2, axis=-1)
        mixed = (gate_a * y_a + gate_b * y_b) @ w_out[l]
        h = h + rms_norm(mixed, mix_post_g[l])
        u = rms_norm(h, ffn_pre_g[l])
        gt, up = jnp.split(u @ w_ffn_in[l], 2, axis=-1)
        h = h + rms_norm((jax.nn.silu(gt) * up) @ w_ffn_out[l], ffn_post_g[l])
    return h[:, N_META:, :]


def setup_inputs(seed=0):
    out = dict(first_inputs(seed))
    for name, value in second_inputs(seed + 1).items():
        if name != "x":
            out[name + "_2"] = value
    return out


def reference(
    x, ffn1_norm, ffn1_w_gate, ffn1_w_up, ffn1_w_down, mix_norm, w_in, gmlp_ln_g, gmlp_ln_b,
    gmlp_w_s, gmlp_b_s, w_branch_attn, w_branch_gmlp, w_gate, b_gate, w_out, ffn2_norm,
    ffn2_w_gate, ffn2_w_up, ffn2_w_down, final_norm, meta_tokens_2, w_in_2, b_gate_2,
    lb_logits_2, hg_norm_g_2, w_hg_o_2, q_a_norm_g_2, w_q_b_2, kv_a_norm_g_2, w_kv_b_2,
    w_mla_o_2, w_out_2, mix_pre_g_2, mix_post_g_2, ffn_pre_g_2, ffn_post_g_2, w_ffn_in_2,
    w_ffn_out_2,
):
    x = first_block(
        x, ffn1_norm, ffn1_w_gate, ffn1_w_up, ffn1_w_down, mix_norm, w_in, gmlp_ln_g, gmlp_ln_b,
        gmlp_w_s, gmlp_b_s, w_branch_attn, w_branch_gmlp, w_gate, b_gate, w_out, ffn2_norm,
        ffn2_w_gate, ffn2_w_up, ffn2_w_down, final_norm,
    )
    return second_block(
        x, meta_tokens_2, w_in_2, b_gate_2, lb_logits_2, hg_norm_g_2, w_hg_o_2, q_a_norm_g_2,
        w_q_b_2, kv_a_norm_g_2, w_kv_b_2, w_mla_o_2, w_out_2, mix_pre_g_2, mix_post_g_2,
        ffn_pre_g_2, ffn_post_g_2, w_ffn_in_2, w_ffn_out_2,
    )


_drawn_inputs = setup_inputs


def setup_inputs(seed=0):
    import zlib

    import numpy as np

    out = dict(_drawn_inputs(seed))
    spreads = {}
    factors = {'gmlp_ln_g': 6.617,
     'gmlp_ln_b': 8.0,
     'b_gate': 8.0,
     'b_gate_2': 8.0,
     'lb_logits_2': 16.969,
     'hg_norm_g_2': 26.184,
     'q_a_norm_g_2': 8.0,
     'kv_a_norm_g_2': 8.0,
     'mix_post_g_2': 3.463,
     'ffn_pre_g_2': 3.474,
     'ffn_post_g_2': 16.215}
    for name, (base, spread) in spreads.items():
        noise = np.random.default_rng([zlib.crc32(name.encode()), seed]).standard_normal(out[name].shape)
        drawn = base * np.exp(spread * noise) if base else spread * noise
        out[name] = __import__('jax').numpy.asarray(drawn.astype(out[name].dtype))
    for name, factor in factors.items():
        out[name] = (out[name] * factor).astype(out[name].dtype)
    return out
```

```python
from contextlib import ExitStack

import numpy as np

import concourse.bass as bass
from concourse import mybir

F32 = mybir.dt.float32
F32R = mybir.dt.float32r
ALU = mybir.AluOpType
ACT = mybir.ActivationFunctionType
AX_X = mybir.AxisListType.X

P = 128
D = 1024
DC = D // P
SEQ = 256
META = 16
L2 = SEQ + META
X0 = META
FF = 2816
PAIRS = FF // 256
NT = SEQ // P
EPS = 1e-6

AH, AD = 8, 64
AW = AH * AD
GG, GC, GW = 8, 128, 512
GD = GW // GG
HH, HC = 8, 16
NOPE, ROPE, VH = 128, 64, 128
QL = 256
MLA_SCALE = float(NOPE + ROPE) ** -0.5
LEVELS = [0, 1, 2, 4, 8, 16, 32, 64]

RING = 3
SLAB = 2048

FFN_SLABS = 3 * PAIRS
N_FFN = [0, FFN_SLABS + 26, 2 * FFN_SLABS + 26 + 43]
N_MIX1 = FFN_SLABS
N_MIX2 = 2 * FFN_SLABS + 26
N_ALL = 3 * FFN_SLABS + 26 + 43
assert N_FFN[1] == N_MIX1 + 26 and N_FFN[2] == N_MIX2 + 43

VEC_ROWS = [("ffn1_norm", 8), ("mix_norm", 8), ("ffn2_norm", 8), ("final_norm", 8), ("mix_pre_g_2", 8),
            ("mix_post_g_2", 8), ("ffn_pre_g_2", 8), ("ffn_post_g_2", 8), ("b_gate", 16), ("b_gate_2", 16),
            ("lb_logits_2", 16), ("hg_norm_g_2", 1), ("q_a_norm_g_2", 2), ("kv_a_norm_g_2", 2)]
VEC = {}
_at = 0
for _name, _k in VEC_ROWS:
    VEC[_name] = _at
    _at += _k
NVEC = _at

T_ID, T_MASK, T_COS, T_SIN = 0, P, P + L2, P + 2 * L2
T_LVL = P + 3 * L2
TAB = T_LVL + P * 8
NEG = -1e30


def constants():
    tab = np.zeros((P, TAB), np.float32)
    tab[:, T_ID:T_ID + P] = np.eye(P, dtype=np.float32)
    q, k = np.arange(P)[:, None], np.arange(P)[None, :]
    tab[:, T_MASK + L2 - P:T_MASK + L2] = np.where(k <= q, 0.0, NEG)
    inv_freq = (1.0 / (np.float32(10000.0) ** (np.arange(0, ROPE, 2, dtype=np.float32) / np.float32(ROPE)))).astype(np.float32)
    ang = (np.arange(L2, dtype=np.float32)[:, None] * inv_freq[None, :]).astype(np.float32)
    row = np.arange(P)
    sign = np.where(row % ROPE < ROPE // 2, -1.0, 1.0).astype(np.float32)
    tab[:, T_COS:T_COS + L2] = np.cos(ang).T[row % (ROPE // 2)]
    tab[:, T_SIN:T_SIN + L2] = np.sin(ang).T[row % (ROPE // 2)] * sign[:, None]
    s, t = np.arange(P)[:, None], np.arange(P)[None, :]
    for i, h in enumerate(LEVELS):
        keep = (s == t) if h == 0 else ((s // (2 * h) == t // (2 * h)) & (s % (2 * h) < h) & (t % (2 * h) >= h))
        tab[:, T_LVL + P * i:T_LVL + P * i + P] = keep
    return tab


SEMS = """slab_used hi_ready lo_ready
x_loaded vec_loaded tab_loaded ws_loaded gm_loaded meta_loaded store_done
vec_T x_T meta_T ws_T vec_ready ones_ready gfp_ready ws_masked ws_T_copied lb_exp lb_ready
h_new xhi_done xlo_done sq_done ss_ready mean_done rec_ready rstd_ready meta_hi meta_lo
y_bank y_zeroed gate_scaled silu_done up_scaled hidden hid_hi_done hid_lo_done
evac out_T out_copied dve_chain act_chain
""".split()
SEMS1 = """gelu_done gsig_done s1_mm s1_masked s1_biased exp1_done p1_ready p1_T p1_copied pv1_mm  attn_hi attn_lo
vln_ready mixed_mm gm_ready gm_hi gm_lo merged1 m_hi m_lo""".split()
SEMS2 = """sq2_done x2_done c_ready csq_done ac_hi ac_lo cmean_done silu2_done rope_done s2_mm s2_masked s2_biased exp2_done
p2_ready p2_T p2_copied pv2_mm mla_hi mla_lo fsig_done f_ready at_zero hg_ready lvl_mm lvl_done gsigb_done vT vm_T v_copied
vm_copied cross_mm cross_copied am_mm am_copied o_mm o_ready osq_done osum_mm ostd_done o_final o_hi o_lo gsiga_done
dve_chain2 css_ready cmean_mm merged2 m2_hi m2_lo mg_done msq_done yg_done ysq_done """.split()


def program(nc, a, tab_d, out):
    ctx = ExitStack()
    with ctx:
        def sb(name, shape, dt):
            return ctx.enter_context(nc.sbuf_tensor(name, shape, dt))

        s = {}
        for name in SEMS + SEMS1 + SEMS2:
            s[name] = ctx.enter_context(nc.semaphore(name))
        slab_in = [ctx.enter_context(nc.semaphore(f"slab_in{i}")) for i in range(RING)]

        ps = ctx.enter_context(nc.psum_tensor("ps", [P, 8, 512], F32))
        stage = sb("stage", [P, RING, SLAB], F32)
        w_hi = sb("w_hi", [P, RING, SLAB], F32R)
        w_lo = sb("w_lo", [P, RING, SLAB], F32R)
        x_hi = sb("x_hi", [P, DC, L2], F32R)
        x_lo = sb("x_lo", [P, DC, L2], F32R)
        a_hi = sb("a_hi", [P, DC, SEQ], F32R)
        a_lo = sb("a_lo", [P, DC, SEQ], F32R)
        h = sb("h", [P, DC, SEQ], F32)
        sq = sb("sq", [P, DC, SEQ], F32)
        ar = sb("ar", [P, 17408], F32)
        tab = sb("tab", [P, TAB], F32)
        vec = sb("vec", [P, NVEC], F32)
        gfp = sb("gfp", [P, DC], F32)
        lb = sb("lb", [P, 6, DC], F32)
        ones = sb("ones", [P, P], F32)
        ss = sb("ss", [P, 2, L2], F32)
        rec = sb("rec", [P, 2, L2], F32)
        rstd = sb("rstd", [P, 2, L2], F32)
        rcol = sb("rcol", [P, 2, 8], F32)

        ident = tab[:, T_ID:T_ID + P]
        mask = tab[:, T_MASK:T_MASK + L2]
        lvl = tab[:, T_LVL:].bitcast(mybir.dt.int32).rearrange("p (l t) -> p l t", t=P)

        def view(at, *dims):
            n = int(np.prod(dims))
            v = ar[:, at:at + n]
            if len(dims) == 1:
                return v
            names = "abcd"[:len(dims)]
            return v.rearrange("p (" + " ".join(names) + ") -> p " + " ".join(names),
                               **dict(zip(names, dims)))

        x_tok = view(0, NT, D)
        vrows = view(2048, P)
        ws = view(14336, GG, GC)
        meta_tok = view(2304, D)
        ga_s, ga_a = view(0, 512), view(512, 512)
        up_s, hid = view(1024, 512), view(1536, 512)

        def ffn_input(f):
            return (x_hi[:, :, X0:], x_lo[:, :, X0:]) if f == 0 else (a_hi[:], a_lo[:])

        def hidden_part(f, part, J):
            c = 2 * (J % 2)
            return (a_hi, a_lo)[part][:, c:c + 2, :] if f == 0 else (x_hi, x_lo)[part][:, 4 + c:6 + c, X0:]

        def pair(v):
            return v.rearrange("p (c t) -> p c t", c=2)
        qT, kT = view(2048, 4, SEQ), view(3072, 4, SEQ)
        V1 = view(4096, NT, AW)
        uT = view(5120, 4, SEQ)
        vg = view(6144, NT, GW)
        gates = view(7168, 16, SEQ)
        S1 = view(11264, 4, 384)
        pT1 = view(12800, 4, 384)
        wsT = view(15360, GG, GC)
        gbias = view(16384, 4, GC)
        ln_g, ln_b = view(14336, GW), view(14848, GW)
        tA, tB = view(0, 1024), view(1024, 1024)
        meta = sb("meta", [P, 2, DC, META], F32)
        small = sb("small", [P, 96], F32)
        out_tok = view(2048, NT, D)

        q2, k2, f2 = view(0, HH, SEQ), view(2048, HH, L2), view(4224, HH, L2)
        gA = view(4224, DC, SEQ)
        Am = view(4224, HH, SEQ)
        cq, ckv, q_sw = view(4224, 2, SEQ), view(4736, 2, L2), view(5280, 4, SEQ)
        qn, hiT, hgs = view(6400, HH, SEQ), view(6400, HH, L2), view(6400, HH, SEQ)
        kn, yb, sq2 = view(8576, HH, L2), view(8576, DC, SEQ), view(8576, DC, SEQ)
        V2, V2m = view(10752, NT, D), view(12800, D)
        AT = view(13824, HH, 3, P)
        q_pe, k_pe, k_sw = view(13824, 4, SEQ), view(14848, L2), view(15120, L2)
        S2 = view(15120, 2, P + META + L2)
        pT2, pT2m = view(15952, 2, 384), view(16896, 2, SEQ)
        mT = view(13824, 2, 512)
        mg = view(0, DC, SEQ)
        yg = view(4096, DC, SEQ)
        K0 = P + META
        sq_flat = sq[:].rearrange("p c t -> p (c t)")
        cq_sq, ckv_sq = sq_flat[:, 0:2 * SEQ].rearrange("p (c t) -> p c t", c=2), sq_flat[:, 512:512 + 2 * L2].rearrange("p (c t) -> p c t", c=2)
        r_q, r_kv = sq_flat[:, 1056:1056 + SEQ], sq_flat[:, 1312:1312 + L2]
        def kv_part(v):
            return v[:].rearrange("p c t -> p (c t)")[:, 512:512 + 2 * L2].rearrange("p (c t) -> p c t", c=2)
        R2 = rstd[:, 1, :]
        gB = sq
        TILES = (0, X0, X0 + P)
        FULL = (1, 2, 11, 12, 13, 14, 19, 20, 21, 22)
        LSLOT = {18: 0, 19: 1, 20: 2, 21: 3, 22: 4, 24: 5, 25: 6, 26: 7}
        MLA_S = {9: 0, 11: 1, 13: 2, 15: 3}
        MLA_T = {10: 0, 12: 1, 14: 2, 16: 3}
        MLA_PV = {11: 0, 13: 1, 15: 2, 17: 3}
        E2 = 22

        def slab_words(n):
            i = n - N_MIX2
            return 1536 if i in (5, 6) else SLAB

        def q_parts(v, n):
            nope, rope = 4 * NOPE, 4 * ROPE
            w = wview(v, n, 2, 768)
            if v is stage:
                w = w.rearrange("p k (h c) -> p k h c", h=4)
                return [(w[:, k, :, 0:NOPE], w[:, k, :, NOPE:]) for k in range(2)]
            return [(w[:, k, 0:nope].rearrange("p (h c) -> p h c", h=4), w[:, k, nope:].rearrange("p (h c) -> p h c", h=4))
                    for k in range(2)]

        def wait_slab(eng, n, it):
            base = 16 * (n // RING + 1)
            eng.wait_ge(slab_in[n % RING], base if it is None else it * (16 * 2) + base)

        def up(n, it, per=6):
            return n if it is None else it * per + n

        def wview(w, n, k, width=None):
            v = w[:, n % RING, :] if width is None else w[:, n % RING, 0:k * width]
            return v.rearrange("p (k c) -> p k c", k=k)

        def mixer1_act(act, split_hi, input_hi):
            n = N_MIX1

            def exps(g):
                act.wait_ge(s["s1_biased"], g + 1)
                for t in range(NT):
                    for o in range(4):
                        v = S1[:, o, P:] if t else S1[:, o, 0:P]
                        k = 4 * t + o
                        nc.scalar.activation(v, v, ACT.Exp, bias=small[:, 8 + k:9 + k],
                                             accum_out=small[:, 16 + k:17 + k]).then_inc(s["exp1_done"], 1)

            def copy_probs(g):
                for o in range(4):
                    act.wait_ge(s["p1_T"], 4 * g + o + 1)
                    nc.scalar.copy(pT1[:, o, :], ps[:, 4 + o, 0:384]).then_inc(s["p1_copied"], 1)

            def attn_hi(g):
                act.wait_ge(s["pv1_mm"], g + 1)
                nc.scalar.activation(a_hi[:, 2 * g:2 * g + 2, :].rearrange("p c t -> p (c t)"), ps[:, 4, :],
                                     ACT.Copy).then_inc(s["attn_hi"], 1)

            for i in range(26):
                if i in (6, 7):
                    act.wait_ge(s["evac"], i + 1)
                    v = uT[:, 2 * (i - 6):2 * (i - 5), :]
                    nc.scalar.activation(v, v, ACT.Gelu_apprx_tanh).then_inc(s["gelu_done"], 1)
                if i in (8, 9):
                    act.wait_ge(s["evac"], i + 1)
                    v = vg[:, :, 256 * (i - 8):256 * (i - 7)]
                    nc.scalar.activation(v, v, ACT.Gelu_apprx_tanh).then_inc(s["gelu_done"], 1)
                if i in (19, 21):
                    q = (i - 19) // 2
                    act.wait_ge(s["merged1"], q + 1)
                    nc.scalar.activation(x_hi[:, 4 * q:4 * q + 4, X0:], tA.rearrange("p (c t) -> p c t", c=4),
                                         ACT.Copy).then_inc(s["m_hi"], 1)
                if i >= 22:
                    input_hi(a_hi, vec[:, VEC["ffn2_norm"]:], 8, [i - 22])
                split_hi(n + i + 3)
                if i == 5:
                    exps(0)
                if i == 7:
                    copy_probs(0)
                if i == 8:
                    attn_hi(0)
                if i == 9:
                    act.wait_ge(s["rec_ready"], 4)
                    nc.scalar.activation(small[:, 60:62], small[:, 58:60], ACT.Sqrt).then_inc(s["rstd_ready"], 1)
                if i == 10:
                    exps(1)
                if i == 12:
                    copy_probs(1)
                if i == 13:
                    attn_hi(1)
                if i == 15:
                    act.wait_ge(s["gm_ready"], 1)
                    nc.scalar.activation(a_hi[:, 4:8, :], tA.rearrange("p (c t) -> p c t", c=4), ACT.Copy).then_inc(s["gm_hi"], 1)
                if i == 17:
                    for c in range(16):
                        act.wait_ge(s["evac"], 10 + c // 2 + 1)
                        nc.scalar.activation(gates[:, c, :], gates[:, c, :], ACT.Sigmoid,
                                             bias=vec[:, VEC["b_gate"] + c:VEC["b_gate"] + c + 1]).then_inc(s["gsig_done"], 1)

        def mixer1_dve(dve, split_lo, seq, input_lo, residual, mean_to_rec):
            n = N_MIX1
            bc2 = rstd[:, 0, X0:].unsqueeze(1).to_broadcast([P, 2, SEQ])

            def acc(i):
                k = 2 * (i % 2)
                return ps[:, k:k + 2, 0:SEQ]

            def group_scores(g):
                dve.wait_ge(s["s1_mm"], g + 1)
                if g:
                    dve.wait_ge(s["p1_T"], 4)
                m0 = mask[:, L2 - P:].unsqueeze(1).to_broadcast([P, 2, P])
                m1 = mask[:, L2 - SEQ:].unsqueeze(1).to_broadcast([P, 4, SEQ])
                for b in range(2):
                    nc.vector.scalar_tensor_tensor(out=S1[:, 2 * b:2 * b + 2, 0:P],
                                                   in0=ps[:, 6 + b, 0:SEQ].rearrange("p (h k) -> p h k", h=2),
                                                   scalar=AD ** -0.5, in1=m0, op0=ALU.mult, op1=ALU.add).then_inc(s["s1_masked"], 1)
                nc.vector.scalar_tensor_tensor(out=S1[:, :, P:], in0=ps[:, 4:6, :].rearrange("p b (h k) -> p (b h) k", h=2),
                                               scalar=AD ** -0.5, in1=m1, op0=ALU.mult, op1=ALU.add).then_inc(s["s1_masked"], 1)
                dve.wait_ge(s["s1_masked"], 3 * g + 3)
                nc.vector.reduce_max(small[:, 0:4], S1[:, :, 0:P], AX_X)
                seq(nc.vector.reduce_max(small[:, 4:8], S1[:, :, P:], AX_X))
                nc.vector.tensor_scalar(small[:, 8:16], small[:, 0:8], -1.0, None, ALU.mult).then_inc(s["s1_biased"], 1)

            def group_probs(g):
                dve.wait_ge(s["exp1_done"], 8 * (g + 1))
                seq(nc.vector.reciprocal(small[:, 24:32], small[:, 16:24]))
                r0 = small[:, 24:28].unsqueeze(2).to_broadcast([P, 4, P])
                r1 = small[:, 28:32].unsqueeze(2).to_broadcast([P, 4, SEQ])
                nc.vector.tensor_tensor(S1[:, :, 0:P], S1[:, :, 0:P], r0, ALU.mult).then_inc(s["p1_ready"], 1)
                nc.vector.tensor_tensor(S1[:, :, P:], S1[:, :, P:], r1, ALU.mult).then_inc(s["p1_ready"], 1)

            def attn_lo(g):
                dve.wait_ge(s["attn_hi"], g + 1)
                nc.vector.tensor_tensor(a_lo[:, 2 * g:2 * g + 2, :].rearrange("p c t -> p (c t)"), ps[:, 4, :],
                                        a_hi[:, 2 * g:2 * g + 2, :].rearrange("p c t -> p (c t)").bitcast(F32),
                                        ALU.subtract).then_inc(s["attn_lo"], 1)

            def layer_norm():
                dve.wait_ge(s["gelu_done"], 4)
                for t in range(NT):
                    st, mv = small[:, 32 + 8 * t:38 + 8 * t], small[:, 48 + 4 * t:50 + 4 * t]
                    seq(nc.vector.bn_stats(st, vg[:, t, :]))
                    seq(nc.vector.bn_aggr(mv, st))
                    seq(nc.vector.tensor_scalar(small[:, 56 + t:57 + t], mv[:, 1:2], EPS, None, ALU.add))
                nc.vector.reciprocal(small[:, 58:60], small[:, 56:58]).then_inc(s["rec_ready"], 1)

            def layer_norm_apply():
                dve.wait_ge(s["rstd_ready"], 4)
                dve.wait_ge(s["gm_loaded"], 64)
                for t in range(NT):
                    nc.vector.tensor_scalar(vg[:, t, :], vg[:, t, :], small[:, 48 + 4 * t:49 + 4 * t], small[:, 60 + t:61 + t],
                                            ALU.subtract, ALU.mult).then_inc(s["vln_ready"], 1)
                dve.wait_ge(s["vln_ready"], 2)
                lg = ln_g.unsqueeze(1).to_broadcast([P, NT, GW])
                lb_ = ln_b.unsqueeze(1).to_broadcast([P, NT, GW])
                seq(nc.vector.tensor_tensor(vg, vg, lg, ALU.mult))
                nc.vector.tensor_tensor(vg, vg, lb_, ALU.add).then_inc(s["vln_ready"], 1)

            def spatial_gate():
                dve.wait_ge(s["mixed_mm"], 1)
                t4 = tA.rearrange("p (c i t) -> p c i t", c=4, i=NT)
                mixed = ps[:, 5:7, :].rearrange("p b (c i t) -> p (b c) i t", c=2, i=NT)
                gb = gbias.unsqueeze(2).to_broadcast([P, 4, NT, P])
                seq(nc.vector.tensor_tensor(t4, mixed, gb, ALU.add))
                nc.vector.tensor_tensor(tA, tA, uT.rearrange("p c t -> p (c t)"), ALU.mult).then_inc(s["gm_ready"], 1)

            mean_to_rec(2, ps[:, 4, 0:SEQ])
            seq(nc.vector.tensor_scalar(rcol[:, 0, 0:2], ps[:, 4, 256:260].rearrange("p (i two) -> p i two", two=2)[:, :, 0],
                                        EPS, None, ALU.add))
            nc.vector.reciprocal(rcol[:, 0, 0:2], rcol[:, 0, 0:2]).then_inc(s["rec_ready"], 1)
            dve.wait_ge(s["rstd_ready"], 3)
            for i in range(26):
                dve.wait_ge(s["slab_used"], n + i + 1)
                if i < 4:
                    dst = (qT, kT)[i // 2][:, 2 * (i % 2):2 * (i % 2) + 2, :]
                    nc.vector.tensor_tensor(dst, acc(i), bc2, ALU.mult).then_inc(s["evac"], 1)
                elif i < 6 or i in (8, 9):
                    dst, j = (V1, i - 4) if i < 6 else (vg, i - 8)
                    for t in range(NT):
                        op = nc.vector.tensor_scalar(dst[:, t, 256 * j:256 * j + 256], ps[:, 2 * (i % 2) + t, 0:256],
                                                     rcol[:, 1, t:t + 1], None, ALU.mult)
                    op.then_inc(s["evac"], 1)
                elif i < 8:
                    nc.vector.tensor_tensor(uT[:, 2 * (i - 6):2 * (i - 5), :], acc(i), bc2, ALU.mult).then_inc(s["evac"], 1)
                elif i < 18:
                    nc.vector.tensor_tensor(gates[:, 2 * (i - 10):2 * (i - 9), :], acc(i), bc2, ALU.mult).then_inc(s["evac"], 1)
                elif i < 22:
                    q, b = (i - 18) // 2, i % 2
                    dve.wait_ge(s["gsig_done"], 16)
                    if q and not b:
                        dve.wait_ge(s["m_lo"], q)
                    y = ps[:, 2 * b:2 * b + 2, :].rearrange("p b t -> p (b t)")
                    gt = gates[:, 8 * b + 4 * q:8 * b + 4 * q + 4, :].rearrange("p c t -> p (c t)")
                    nc.vector.tensor_tensor((tA, tB)[b], y, gt, ALU.mult).then_inc(s["evac"], 1)
                    if b:
                        dve.wait_ge(s["evac"], i + 1)
                        nc.vector.tensor_tensor(tA, tA, tB, ALU.add).then_inc(s["merged1"], 1)
                        dve.wait_ge(s["merged1"], q + 1)
                        dve.wait_ge(s["m_hi"], q + 1)
                        nc.vector.tensor_tensor(x_lo[:, 4 * q:4 * q + 4, X0:], tA.rearrange("p (c t) -> p c t", c=4),
                                                x_hi[:, 4 * q:4 * q + 4, X0:].bitcast(F32), ALU.subtract).then_inc(s["m_lo"], 1)
                else:
                    residual(i - 22, 1.0)
                    dve.wait_ge(s["h_new"], 8 + i - 22 + 1)
                    input_lo(i - 22, vec[:, VEC["ffn2_norm"]:], 16, (a_hi, a_lo))
                split_lo(n + i + 3)
                if i == 5:
                    group_scores(0)
                if i == 6:
                    group_probs(0)
                if i == 8:
                    attn_lo(0)
                if i == 9:
                    layer_norm()
                    group_scores(1)
                if i == 10:
                    group_probs(1)
                    layer_norm_apply()
                if i == 13:
                    attn_lo(1)
                if i == 15:
                    spatial_gate()
                    dve.wait_ge(s["gm_hi"], 1)
                    nc.vector.tensor_tensor(a_lo[:, 4:8, :], tA.rearrange("p (c t) -> p c t", c=4),
                                            a_hi[:, 4:8, :].bitcast(F32), ALU.subtract).then_inc(s["gm_lo"], 1)

        def mixer2_act(act, split_hi):
            n = N_MIX2
            bg = vec[:, VEC["b_gate_2"]:]

            def pair_hi(p):
                act.wait_ge(s["pv2_mm"], p + 1)
                nc.scalar.activation(a_hi[:, 2 * p:2 * p + 2, :].rearrange("p c t -> p (c t)"), ps[:, 7, :],
                                     ACT.Copy).then_inc(s["mla_hi"], 1)

            for i in range(43):
                if i < 2:
                    src, sqs, dst, g = ((cq, cq_sq, a_hi[:, 0:2, :], "q_a_norm_g_2"), (ckv, ckv_sq, kv_part(a_hi), "kv_a_norm_g_2"))[i]
                    act.wait_ge(s["evac"], E2 + i + 1)
                    nc.scalar.activation(sqs, src, ACT.Square).then_inc(s["csq_done"], 1)
                    for c in range(2):
                        k = VEC[g] + c
                        nc.scalar.activation(dst[:, c, :], src[:, c, :], ACT.Copy, scale=vec[:, k:k + 1]).then_inc(s["ac_hi"], 1)
                if i in (3, 4, 9, 10):
                    j = i - 3 if i < 5 else i - 7
                    act.wait_ge(s["evac"], E2 + i + 1)
                    nc.scalar.activation(q2[:, 2 * j:2 * j + 2, :], q2[:, 2 * j:2 * j + 2, :], ACT.Silu).then_inc(s["silu2_done"], 1)
                if 11 <= i < 15:
                    j = i - 11
                    act.wait_ge(s["evac"], E2 + i + 1)
                    nc.scalar.activation(f2[:, 2 * j:2 * j + 2, :], f2[:, 2 * j:2 * j + 2, :], ACT.Sigmoid).then_inc(s["fsig_done"], 1)
                if 27 <= i < 31:
                    j = i - 27
                    act.wait_ge(s["evac"], E2 + i + 1)
                    nc.scalar.activation(hgs[:, 2 * j:2 * j + 2, :], hgs[:, 2 * j:2 * j + 2, :], ACT.Silu).then_inc(s["silu2_done"], 1)
                if 35 <= i < 39:
                    j = i - 35
                    act.wait_ge(s["merged2"], j + 1)
                    nc.scalar.activation(x_hi[:, 2 * j:2 * j + 2, X0:], pair(mT[:, j % 2, :]), ACT.Copy).then_inc(s["m2_hi"], 1)
                if i >= 39:
                    j = i - 39
                    act.wait_ge(s["slab_used"], n + i + 1)
                    for c in range(2):
                        k = VEC["mix_post_g_2"] + 2 * j + c
                        nc.scalar.activation(mg[:, 2 * j + c, :], ps[:, 4 + j, SEQ * c:SEQ * c + SEQ], ACT.Copy,
                                             scale=vec[:, k:k + 1]).then_inc(s["mg_done"], 1)
                    nc.scalar.activation(sq[:, 2 * j:2 * j + 2, :].rearrange("p c t -> p (c t)"), ps[:, 4 + j, :],
                                         ACT.Square).then_inc(s["msq_done"], 1)
                split_hi(n + i + 3)
                if i == 3:
                    act.wait_ge(s["c_ready"], 1)
                    nc.scalar.activation(r_q, rec[:, 0, X0:], ACT.Sqrt).then_inc(s["cmean_done"], 1)
                    nc.scalar.activation(r_kv, rec[:, 1, :], ACT.Sqrt).then_inc(s["cmean_done"], 1)
                    nc.scalar.activation(rcol[:, 1, 2:5], rcol[:, 0, 2:5], ACT.Sqrt).then_inc(s["cmean_done"], 1)
                if i in MLA_PV:
                    pair_hi(MLA_PV[i])
                if i in MLA_S:
                    p = MLA_S[i]
                    act.wait_ge(s["s2_biased"], p + 1)
                    for t in range(NT):
                        for hh in range(2):
                            v = S2[:, hh, K0:] if t else S2[:, hh, 0:K0]
                            k = 2 * t + hh
                            nc.scalar.activation(v, v, ACT.Exp, bias=small[:, 8 + k:9 + k],
                                                 accum_out=small[:, 16 + k:17 + k]).then_inc(s["exp2_done"], 1)
                if i in MLA_T:
                    p = MLA_T[i]
                    act.wait_ge(s["p2_T"], p + 1)
                    nc.scalar.copy(pT2, ps[:, 5:7, 0:384]).then_inc(s["p2_copied"], 1)
                    nc.scalar.copy(pT2m[0:META].rearrange("p c t -> p (c t)"), ps[0:META, 4, :]).then_inc(s["p2_copied"], 1)
                if i == 18:
                    for c in range(DC):
                        act.wait_ge(s["evac"], E2 + 15 + c // 2 + 1)
                        nc.scalar.activation(gB[:, c, :], gB[:, c, :], ACT.Sigmoid, bias=bg[:, DC + c:DC + c + 1]).then_inc(s["gsigb_done"], 1)
                if i == 23:
                    act.wait_ge(s["vm_T"], 1)
                    nc.scalar.copy(V2m[0:META], ps[0:META, 0:2, :].rearrange("p b c -> p (b c)")).then_inc(s["vm_copied"], 1)
                    act.wait_ge(s["vT"], 1)
                    for t in range(NT):
                        nc.scalar.copy(V2[:, t, :], ps[:, 4 + 2 * t:6 + 2 * t, :].rearrange("p b c -> p (b c)")).then_inc(s["v_copied"], 1)
                if i == 27:
                    act.wait_ge(s["cross_mm"], 1)
                    nc.scalar.copy(AT[:, :, 1, :], ps[:, 4:6, :].rearrange("p b (h t) -> p (b h) t", h=4)).then_inc(s["cross_copied"], 1)
                    nc.scalar.copy(Am[0:META, 0:4, :].rearrange("p h t -> p (h t)"),
                                   ps[0:META, 6:8, :].rearrange("p b t -> p (b t)")).then_inc(s["cross_copied"], 1)
                if i == 28:
                    act.wait_ge(s["am_mm"], 1)
                    nc.scalar.copy(Am[0:META, 4:8, :].rearrange("p h t -> p (h t)"),
                                   ps[0:META, 4:6, :].rearrange("p b t -> p (b t)")).then_inc(s["am_copied"], 1)
                if i == 29:
                    for b in range(2):
                        act.wait_ge(s["o_ready"], b + 1)
                        nc.scalar.activation(k2[:, 4 * b:4 * b + 4, 0:SEQ], q2[:, 4 * b:4 * b + 4, :], ACT.Square).then_inc(s["osq_done"], 1)
                if i == 30:
                    for b in range(2):
                        act.wait_ge(s["osum_mm"], 2 * b + 2)
                        nc.scalar.activation(k2[:, 4 * b:4 * b + 4, 0:SEQ], ps[:, 4 + 2 * b:6 + 2 * b, :].rearrange("p b (h t) -> p (b h) t", h=2),
                                             ACT.Sqrt, scale=float(D // P), bias=small[:, 64:65]).then_inc(s["ostd_done"], 1)
                if i == 32:
                    for b in range(2):
                        act.wait_ge(s["o_final"], b + 1)
                        nc.scalar.activation(a_hi[:, 4 * b:4 * b + 4, :], q2[:, 4 * b:4 * b + 4, :], ACT.Copy).then_inc(s["o_hi"], 1)
                if i == 34:
                    for c in range(DC):
                        act.wait_ge(s["evac"], E2 + 31 + c // 2 + 1)
                        nc.scalar.activation(gA[:, c, :], gA[:, c, :], ACT.Sigmoid, bias=bg[:, c:c + 1]).then_inc(s["gsiga_done"], 1)

        def mixer2_dve(dve, split_lo, seq, mean_to_rec):
            n = N_MIX2

            def bc(r, k):
                return r.unsqueeze(1).to_broadcast([P, k, r.shape[1]])

            def acc(i, width):
                k = 2 * (i % 2)
                return ps[:, k:k + 2, 0:width]

            def rope():
                x0 = tab[:, T_COS + X0:T_COS + L2].unsqueeze(1).to_broadcast([P, 4, SEQ])
                x1 = tab[:, T_SIN + X0:T_SIN + L2].unsqueeze(1).to_broadcast([P, 4, SEQ])
                dve.wait_ge(s["evac"], E2 + 7)
                for d, r in ((0, 32), (32, 0), (64, 96), (96, 64)):
                    seq(nc.vector.tensor_copy(q_sw[d:d + 32], q_pe[r:r + 32]))
                    seq(nc.vector.tensor_copy(k_sw[d:d + 32], k_pe[r:r + 32]))
                seq(nc.vector.tensor_tensor(q_pe, q_pe, x0, ALU.mult))
                seq(nc.vector.tensor_tensor(q_sw, q_sw, x1, ALU.mult))
                nc.vector.tensor_tensor(q_pe, q_pe, q_sw, ALU.add).then_inc(s["rope_done"], 1)
                seq(nc.vector.tensor_tensor(k_pe, k_pe, tab[:, T_COS:T_COS + L2], ALU.mult))
                seq(nc.vector.tensor_tensor(k_sw, k_sw, tab[:, T_SIN:T_SIN + L2], ALU.mult))
                nc.vector.tensor_tensor(k_pe, k_pe, k_sw, ALU.add).then_inc(s["rope_done"], 1)

            def pair_scores(p):
                dve.wait_ge(s["s2_mm"], p + 1)
                if p:
                    dve.wait_ge(s["p2_T"], p)
                else:
                    dve.wait_ge(s["rope_done"], 2)
                nc.vector.scalar_tensor_tensor(out=S2[:, :, 0:K0], in0=ps[:, 5:7, 0:K0],
                                               scalar=MLA_SCALE, in1=bc(mask[:, P:], 2), op0=ALU.mult, op1=ALU.add).then_inc(s["s2_masked"], 1)
                nc.vector.scalar_tensor_tensor(out=S2[:, :, K0:], in0=ps[:, 5:7, K0:K0 + L2],
                                               scalar=MLA_SCALE, in1=bc(mask, 2), op0=ALU.mult, op1=ALU.add).then_inc(s["s2_masked"], 1)
                dve.wait_ge(s["s2_masked"], 2 * p + 2)
                nc.vector.reduce_max(small[:, 0:2], S2[:, :, 0:K0], AX_X)
                seq(nc.vector.reduce_max(small[:, 2:4], S2[:, :, K0:], AX_X))
                nc.vector.tensor_scalar(small[:, 8:12], small[:, 0:4], -1.0, None, ALU.mult).then_inc(s["s2_biased"], 1)
                dve.wait_ge(s["exp2_done"], 4 * (p + 1))
                seq(nc.vector.reciprocal(small[:, 24:28], small[:, 16:20]))
                r0 = small[:, 24:26].unsqueeze(2).to_broadcast([P, 2, K0])
                r1 = small[:, 26:28].unsqueeze(2).to_broadcast([P, 2, L2])
                nc.vector.tensor_tensor(S2[:, :, 0:K0], S2[:, :, 0:K0], r0, ALU.mult).then_inc(s["p2_ready"], 1)
                nc.vector.tensor_tensor(S2[:, :, K0:], S2[:, :, K0:], r1, ALU.mult).then_inc(s["p2_ready"], 1)

            def pair_lo(p):
                dve.wait_ge(s["mla_hi"], p + 1)
                nc.vector.tensor_tensor(a_lo[:, 2 * p:2 * p + 2, :].rearrange("p c t -> p (c t)"), ps[:, 7, :],
                                        a_hi[:, 2 * p:2 * p + 2, :].rearrange("p c t -> p (c t)").bitcast(F32),
                                        ALU.subtract).then_inc(s["mla_lo"], 1)

            def forget(j):
                dve.wait_ge(s["fsig_done"], j + 1)
                for c in (2 * j, 2 * j + 1):
                    seq(nc.vector.tensor_scalar(f2[:, c, :], f2[:, c, :], lb[:, 5, c:c + 1], lb[:, 4, c:c + 1], ALU.mult, ALU.add))
                nc.vector.tensor_scalar(k2[:, 2 * j:2 * j + 2, :], f2[:, 2 * j:2 * j + 2, :], -1.0, 1.0, ALU.mult,
                                        ALU.add).then_inc(s["f_ready"], 1)

            def level(l):
                size = LEVELS[l]
                dve.wait_ge(s["lvl_mm"], l + 1)
                if size == 0:
                    nc.vector.tensor_tensor(q2, q2, f2[:, :, X0:], ALU.mult).then_inc(s["hg_ready"], 1)
                else:
                    nb = SEQ // (2 * size)
                    fx = f2[:, :, X0:].rearrange("p h (b two s) -> p h b two s", two=2, s=size)
                    qx = q2.rearrange("p h (b two s) -> p (h b) two s", two=2, s=size)
                    if size < META:
                        kk, ff = k2, f2
                    else:
                        kk, ff = k2[:, :, X0:], f2[:, :, X0:]
                    kx = kk.rearrange("p h (b two s) -> p h b two s", two=2, s=size)
                    fk = ff.rearrange("p h (b two s) -> p h b two s", two=2, s=size)
                    nk = kk.shape[2] // (2 * size)
                    o = kx[:, :, :, 0, :]
                    nc.vector.tensor_tensor(o, o, fk[:, :, :, 1, 0:1].to_broadcast([P, HH, nk, size]), ALU.mult).then_inc(s["dve_chain2"], 1)
                    qv = q2.rearrange("p h (b two s) -> p h b two s", two=2, s=size)[:, :, :, 1, :]
                    nc.vector.tensor_tensor(qv, qv, fx[:, :, :, 0, 0:1].to_broadcast([P, HH, nb, size]), ALU.mult).then_inc(s["dve_chain2"], 1)
                    dve.wait_ge(s["dve_chain2"], 3 * l - 1)
                    t0 = fk[:, :, :, 0, 0]
                    nc.vector.tensor_tensor(t0, t0, fk[:, :, :, 1, 0], ALU.mult).then_inc(s["dve_chain2"], 1)
                    dve.wait_ge(s["dve_chain2"], 3 * l)
                    if l == len(LEVELS) - 1:
                        tot = f2[:, :, X0:X0 + 1].to_broadcast([P, HH, META])
                        nc.vector.tensor_tensor(meta[:, 0], k2[:, :, 0:META], tot, ALU.mult).then_inc(s["hg_ready"], 1)
                    else:
                        nc.vector.tensor_copy(meta[:, 1, 0, 0:1], f2[:, 0, 0:1]).then_inc(s["hg_ready"], 1)
                if l == 0:
                    dve.wait_ge(s["at_zero"], 1)
                else:
                    dve.wait_ge(s["lvl_done"], 4 * l)
                for b in range(4):
                    for hd in range(2):
                        op = nc.vector.copy_predicated(AT[:, 2 * b + hd, 0:3:2, :], lvl[:, l, :].unsqueeze(1).to_broadcast([P, 2, P]),
                                                       ps[:, 4 + b, 256 * hd:256 * hd + 256].rearrange("p (t q) -> p t q", t=2))
                    op.then_inc(s["lvl_done"], 1)

            mean_to_rec(4, ps[:, 4, 0:SEQ])
            dve.wait_ge(s["rec_ready"], 6)
            seq(nc.vector.tensor_tensor(rec[:, 1, X0:], ps[:, 5, X0:L2], rec[:, 0, X0:], ALU.mult))
            seq(nc.vector.tensor_copy(rec[:, 1, 0:META], ps[:, 5, 0:META]))
            seq(nc.vector.tensor_scalar(rec[:, 1, :], rec[:, 1, :], EPS, None, ALU.add))
            nc.vector.reciprocal(rec[:, 1, :], rec[:, 1, :]).then_inc(s["rec_ready"], 1)
            dve.wait_ge(s["rstd_ready"], 7)
            seq(nc.vector.tensor_tensor(R2[:, X0:], R2[:, X0:], rstd[:, 0, X0:], ALU.mult))
            seq(nc.vector.memset(small[:, 64:65], EPS))
            for i in range(43):
                if i < 39:
                    dve.wait_ge(s["slab_used"], n + i + 1)
                if i < 2:
                    dst, w = ((cq, SEQ), (ckv, L2))[i]
                    nc.vector.tensor_tensor(dst, acc(i, w), bc(R2[:, L2 - w:], 2), ALU.mult).then_inc(s["evac"], 1)
                    src, sqs, hi, lo, g, o = ((cq, cq_sq, a_hi[:, 0:2, :], a_lo[:, 0:2, :], "q_a_norm_g_2", ss[:, 0, X0:]),
                                              (ckv, ckv_sq, kv_part(a_hi), kv_part(a_lo), "kv_a_norm_g_2", ss[:, 1, :]))[i]
                    dve.wait_ge(s["csq_done"], i + 1)
                    nc.vector.tensor_tensor(o, sqs[:, 0, :], sqs[:, 1, :], ALU.add).then_inc(s["css_ready"], 1)
                    dve.wait_ge(s["evac"], E2 + i + 1)
                    for c in range(2):
                        dve.wait_ge(s["ac_hi"], 2 * i + c + 1)
                        k = VEC[g] + c
                        nc.vector.scalar_tensor_tensor(out=lo[:, c, :], in0=src[:, c, :], scalar=vec[:, k:k + 1],
                                                       in1=hi[:, c, :].bitcast(F32), op0=ALU.mult, op1=ALU.subtract).then_inc(s["ac_lo"], 1)
                elif i == 2:
                    nc.vector.tensor_tensor(k_pe, ps[:, 0, 0:L2], R2, ALU.mult).then_inc(s["evac"], 1)
                elif i in (3, 4, 9, 10):
                    j = i - 3 if i < 5 else i - 7
                    nc.vector.tensor_tensor(q2[:, 2 * j:2 * j + 2, :], acc(i, SEQ), bc(R2[:, X0:], 2), ALU.mult).then_inc(s["evac"], 1)
                elif i in (5, 6):
                    k, j = 2 * (i % 2), i - 5
                    dve.wait_ge(s["cmean_done"], 3)
                    nc.vector.tensor_tensor(qn[:, 4 * j:4 * j + 4, :], ps[:, k:k + 2, :].rearrange("p b (h t) -> p (b h) t", h=2),
                                            bc(r_q, 4), ALU.mult)
                    nc.vector.tensor_tensor(q_pe[:, 2 * j:2 * j + 2, :], pair(ps[:, 7, :]), bc(r_q, 2), ALU.mult).then_inc(s["evac"], 1)
                elif i in (7, 8):
                    k, j = 2 * (i % 2), i - 7
                    nc.vector.tensor_tensor(kn[:, 4 * j:4 * j + 2, :], ps[:, k:k + 2, 0:L2], bc(r_kv, 2), ALU.mult)
                    nc.vector.tensor_tensor(kn[:, 4 * j + 2:4 * j + 4, :], ps[:, 4:6, 0:L2], bc(r_kv, 2), ALU.mult)
                    for t in range(NT):
                        nc.vector.tensor_scalar(V2[:, t, 512 * j:512 * j + 512], ps[:, 6 + t, :], rcol[:, 1, 3 + t:4 + t], None, ALU.mult)
                    nc.vector.tensor_scalar(V2m[0:META, 512 * j:512 * j + 512], ps[0:META, 2 - k, :], rcol[0:META, 1, 2:3], None,
                                            ALU.mult).then_inc(s["evac"], 1)
                elif 11 <= i < 15:
                    j = i - 11
                    nc.vector.tensor_tensor(f2[:, 2 * j:2 * j + 2, :], acc(i, L2), bc(R2, 2), ALU.mult).then_inc(s["evac"], 1)
                elif 15 <= i < 19:
                    j = i - 15
                    nc.vector.tensor_tensor(gB[:, 2 * j:2 * j + 2, :], acc(i, SEQ), bc(R2[:, X0:], 2), ALU.mult).then_inc(s["evac"], 1)
                elif 19 <= i < 23:
                    j = i - 19
                    nc.vector.tensor_tensor(hiT[:, 2 * j:2 * j + 2, :], acc(i, L2), bc(R2, 2), ALU.mult).then_inc(s["evac"], 1)
                elif 23 <= i < 27:
                    j = i - 23
                    dve.wait_ge(s["gsigb_done"], 2 * j + 2)
                    nc.vector.tensor_tensor(yb[:, 2 * j:2 * j + 2, :], acc(i, SEQ), gB[:, 2 * j:2 * j + 2, :], ALU.mult).then_inc(s["evac"], 1)
                elif 27 <= i < 31:
                    j = i - 27
                    if j == 0:
                        dve.wait_ge(s["v_copied"], 2)
                    nc.vector.tensor_tensor(hgs[:, 2 * j:2 * j + 2, :], acc(i, SEQ), bc(R2[:, X0:], 2), ALU.mult).then_inc(s["evac"], 1)
                elif 31 <= i < 35:
                    j = i - 31
                    nc.vector.tensor_tensor(gA[:, 2 * j:2 * j + 2, :], acc(i, SEQ), bc(R2[:, X0:], 2), ALU.mult).then_inc(s["evac"], 1)
                elif 35 <= i < 39:
                    j = i - 35
                    dve.wait_ge(s["gsiga_done"], 2 * j + 2)
                    if j >= 2:
                        dve.wait_ge(s["m2_lo"], j - 1)
                    m = pair(mT[:, j % 2, :])
                    nc.vector.tensor_tensor(m, acc(i, SEQ), gA[:, 2 * j:2 * j + 2, :], ALU.mult).then_inc(s["evac"], 1)
                    dve.wait_ge(s["evac"], E2 + i + 1)
                    nc.vector.tensor_tensor(m, m, yb[:, 2 * j:2 * j + 2, :], ALU.add).then_inc(s["merged2"], 1)
                    dve.wait_ge(s["merged2"], j + 1)
                    dve.wait_ge(s["m2_hi"], j + 1)
                    nc.vector.tensor_tensor(x_lo[:, 2 * j:2 * j + 2, X0:], m, x_hi[:, 2 * j:2 * j + 2, X0:].bitcast(F32),
                                            ALU.subtract).then_inc(s["m2_lo"], 1)
                split_lo(n + i + 3)
                if i == 3:
                    dve.wait_ge(s["cmean_mm"], 1)
                    seq(nc.vector.tensor_scalar(rec[:, 0, X0:], ps[:, 4, 0:SEQ], float(D // QL), EPS, ALU.mult, ALU.add))
                    seq(nc.vector.tensor_scalar(rec[:, 1, :], ps[:, 5, 0:L2], float(D // QL), EPS, ALU.mult, ALU.add))
                    seq(nc.vector.tensor_scalar(rcol[:, 0, 2:5], ps[:, 6, 0:6].rearrange("p (t two) -> p t two", two=2)[:, :, 0],
                                                float(D // QL), EPS, ALU.mult, ALU.add))
                    nc.vector.reciprocal(rec[:, 0, X0:], rec[:, 0, X0:])
                    nc.vector.reciprocal(rec[:, 1, :], rec[:, 1, :])
                    nc.vector.reciprocal(rcol[:, 0, 2:5], rcol[:, 0, 2:5]).then_inc(s["c_ready"], 1)
                if i == 6:
                    rope()
                if i in MLA_PV:
                    pair_lo(MLA_PV[i])
                if i in MLA_S:
                    pair_scores(MLA_S[i])
                if 12 <= i < 16:
                    forget(i - 12)
                if i in LSLOT:
                    level(LSLOT[i])
                if i == 29:
                    for b in range(2):
                        dve.wait_ge(s["o_mm"], 2 * b + 2)
                        nc.vector.tensor_copy(q2[:, 4 * b:4 * b + 4, :], ps[:, 4 + 2 * b:6 + 2 * b, :].rearrange("p b (h t) -> p (b h) t", h=2)).then_inc(s["o_ready"], 1)
                if i in (31, 32):
                    b = i - 31
                    dve.wait_ge(s["ostd_done"], b + 1)
                    dve.wait_ge(s["silu2_done"], 8)
                    o = q2[:, 4 * b:4 * b + 4, :]
                    k = VEC["hg_norm_g_2"]
                    rms = k2[:, 4 * b:4 * b + 4, 0:SEQ]
                    seq(nc.vector.reciprocal(rms, rms))
                    seq(nc.vector.tensor_tensor(o, o, rms, ALU.mult))
                    nc.vector.scalar_tensor_tensor(out=o, in0=o, scalar=vec[:, k:k + 1], in1=hgs[:, 4 * b:4 * b + 4, :],
                                                   op0=ALU.mult, op1=ALU.mult).then_inc(s["o_final"], 1)
                if i == 33:
                    for b in range(2):
                        dve.wait_ge(s["o_hi"], b + 1)
                        nc.vector.tensor_tensor(a_lo[:, 4 * b:4 * b + 4, :], q2[:, 4 * b:4 * b + 4, :],
                                                a_hi[:, 4 * b:4 * b + 4, :].bitcast(F32), ALU.subtract).then_inc(s["o_lo"], 1)
            dve.wait_ge(s["msq_done"], 4)
            nc.vector.tensor_reduce(ss[:, 0, X0:], sq[:].rearrange("p c t -> p t c"), AX_X, ALU.add).then_inc(s["ss_ready"], 1)
            mean_to_rec(5, ps[:, 0, 0:SEQ])
            dve.wait_ge(s["rstd_ready"], 8)
            dve.wait_ge(s["mg_done"], 8)
            dve.wait_ge(s["x2_done"], 2 * DC)
            for b in range(4):
                v, hb = mg[:, 2 * b:2 * b + 2, :], h[:, 2 * b:2 * b + 2, :]
                seq(nc.vector.tensor_tensor(v, v, bc(rstd[:, 0, X0:], 2), ALU.mult))
                nc.vector.tensor_tensor(hb, hb, v, ALU.add).then_inc(s["h_new"], 1)

        block = ctx.enter_context(nc.Block())

        @block.sync
        def _(sp):
            sp.dma_start(x_tok, a["x"][0].rearrange("(i p) d -> p i d", p=P)).then_inc(s["x_loaded"], 16)
            sp.dma_start(tab[:], tab_d).then_inc(s["tab_loaded"], 16)

            def load(n, src, dst=None, it=None):
                if n >= RING or it is not None:
                    sp.wait_ge(s["lo_ready"], up(max(n - RING + 1, 1), it))
                if dst is None:
                    dst = wview(stage, n, src.shape[1])
                sp.dma_start(dst, src).then_inc(slab_in[n % RING], 16)

            def cols(w, c0, width=256):
                return w.rearrange("(k p) c -> p k c", p=P)[:, :, bass.ds(c0, width)]

            def rows(w, r0):
                return w[bass.ds(r0, 256), :].rearrange("(k p) c -> p k c", p=P)

            def ffn_loads(f, wg, g0, wu, u0, wd):
                n = N_FFN[f]
                load(n, cols(wg, g0))
                load(n + 1, cols(wu, u0))
                with sp.Fori(0, (PAIRS - 1) // 2) as it:
                    for b in range(2):
                        load(n + 2 + 3 * b, cols(wg, it * 512 + (g0 + 256 * (b + 1))), it=it)
                        load(n + 3 + 3 * b, cols(wu, it * 512 + (u0 + 256 * (b + 1))), it=it)
                        load(n + 4 + 3 * b, rows(wd, it * 512 + 256 * b), it=it)
                load(n + FFN_SLABS - 1, rows(wd, 256 * (PAIRS - 1)))

            ffn_loads(0, a["ffn1_w_gate"][0], 0, a["ffn1_w_up"][0], 0, a["ffn1_w_down"][0])
            n = N_MIX1
            for i in range(10):
                load(n + i, cols(a["w_in"][0], 256 * i))
            for i in range(8):
                load(n + 10 + i, cols(a["w_gate"][0], 256 * i))
            for i in range(2):
                load(n + 18 + 2 * i, cols(a["w_branch_attn"][0], 512 * i, 512))
                load(n + 19 + 2 * i, cols(a["w_branch_gmlp"][0], 512 * i, 512))
            for i in range(4):
                load(n + 22 + i, cols(a["w_out"][0], 256 * i))
            ffn_loads(1, a["ffn2_w_gate"][0], 0, a["ffn2_w_up"][0], 0, a["ffn2_w_down"][0])
            n, w = N_MIX2, a["w_in_2"][0]
            q0, f0, i0, g0, cq0, ckv0, kpe0 = 0, 1024, 2048, 3072, 4096, 4096 + QL, 4096 + 2 * QL
            ga0 = kpe0 + ROPE
            gb0 = ga0 + D
            load(n, cols(w, cq0))
            load(n + 1, cols(w, ckv0))
            load(n + 2, cols(w, kpe0, ROPE), wview(stage, n + 2, DC, ROPE))
            for i in range(2):
                load(n + 3 + i, cols(w, q0 + 256 * i))
            for i in range(2):
                load(n + 5 + i, cols(a["w_q_b_2"][0], 768 * i, 768), wview(stage, n + 5 + i, 2, 768))
            for i in range(2):
                load(n + 7 + i, cols(a["w_kv_b_2"][0], 1024 * i, 1024))
            for i in range(2, 4):
                load(n + 7 + i, cols(w, q0 + 256 * i))
            for j, src, c0 in ((11, w, f0), (15, w, gb0), (19, w, i0), (23, a["w_mla_o_2"][0], 0), (27, w, g0),
                               (31, w, ga0), (35, a["w_hg_o_2"][0], 0), (39, a["w_out_2"][0], 0)):
                for i in range(4):
                    load(n + j + i, cols(src, c0 + 256 * i))
            ffn_loads(2, a["w_ffn_in_2"][0], 0, a["w_ffn_in_2"][0], FF, a["w_ffn_out_2"][0])
            for i in range(NT):
                sp.wait_ge(s["out_copied"], 2 * (i + 1))
                sp.dma_start(out[0, P * i:P * (i + 1), :], out_tok[:, i, :]).then_inc(s["store_done"], 16)
            sp.wait_ge(s["store_done"], 16 * NT)

        @block.gpsimd
        def _(pool):
            nc.gpsimd.memset(ones[:], 1.0 / D).then_inc(s["ones_ready"], 1)
            pool.wait_ge(s["ws_loaded"], 16)
            nc.gpsimd.affine_select(out=ws, in_=ws, compare_op=ALU.is_ge, fill=0.0, base=0,
                                    pattern=[[0, GG], [-1, GC]], channel_multiplier=1).then_inc(s["ws_masked"], 1)
            pool.wait_ge(s["ws_T"], 1)
            nc.gpsimd.dma_start(ln_g, a["gmlp_ln_g"].partition_broadcast(P)).then_inc(s["gm_loaded"], 16)
            nc.gpsimd.dma_start(ln_b, a["gmlp_ln_b"].partition_broadcast(P)).then_inc(s["gm_loaded"], 16)
            for half in range(2):
                src = a["gmlp_b_s"].rearrange("l (c two) i -> l two c i", two=2)[:, half]
                nc.gpsimd.dma_start(gbias[64 * half:64 * half + 64], src.partition_broadcast(64)).then_inc(s["gm_loaded"], 16)

            pool.wait_ge(s["rstd_ready"], 6)
            pool.wait_ge(s["xlo_done"], 32)
            pool.wait_ge(s["sq2_done"], 8)
            fg = vec[:, VEC["final_norm"]:]
            for c in range(DC):
                nc.gpsimd.tensor_scalar(h[:, c, :], h[:, c, :], fg[:, c:c + 1], None, ALU.mult).then_inc(s["x2_done"], 1)
            pool.wait_ge(s["x2_done"], DC)
            for c in range(DC):
                nc.gpsimd.tensor_tensor(h[:, c, :], h[:, c, :], rstd[:, 0, X0:], ALU.mult).then_inc(s["x2_done"], 1)
            pool.wait_ge(s["mla_lo"], 4)
            nc.gpsimd.memset(AT, 0.0).then_inc(s["at_zero"], 1)

        @block.scalar
        def _(act):
            chain = [0]

            def seq(ins):
                chain[0] += 1
                ins.then_inc(s["act_chain"], 1)
                act.wait_ge(s["act_chain"], chain[0])

            for name, k in VEC_ROWS:
                r = VEC[name]
                src = a[name]
                src = src.rearrange("(k p) -> k p", p=P) if len(src.shape) == 1 else src.rearrange("l (k p) -> (l k) p", p=P)
                act.dma_start(vrows[r:r + k, :], src).then_inc(s["vec_loaded"], 16)
            act.dma_start(meta_tok[0:META, :], a["meta_tokens_2"]).then_inc(s["meta_loaded"], 16)
            act.dma_start(ws, a["gmlp_w_s"][0].rearrange("g i j -> i g j")).then_inc(s["ws_loaded"], 16)

            def split_hi(n, it=None):
                if it is None and n >= N_ALL:
                    return
                wait_slab(act, n, it)
                if n >= RING:
                    act.wait_ge(s["slab_used"], up(n - RING + 1, it))
                if it is None and n in (N_MIX2 + 5, N_MIX2 + 6):
                    for dst, src in zip(q_parts(w_hi, n), q_parts(stage, n)):
                        for o, i in zip(dst, src):
                            last = nc.scalar.activation(o, i, ACT.Copy)
                    last.then_inc(s["hi_ready"], 1)
                    return
                if it is None and n == N_MIX2 + 2:
                    o = w_hi[:, n % RING, 0:D].rearrange("p (k two c) -> p k two c", k=DC, two=2)
                    i = wview(stage, n, DC, ROPE).unsqueeze(2).to_broadcast([P, DC, 2, ROPE])
                else:
                    o, i = w_hi[:, n % RING, 0:slab_words(n)], stage[:, n % RING, 0:slab_words(n)]
                nc.scalar.activation(o, i, ACT.Copy).then_inc(s["hi_ready"], 1)

            def input_hi(dst, g, base, bs=range(4)):
                for b in bs:
                    act.wait_ge(s["h_new"], base + b + 1)
                    for c in (2 * b, 2 * b + 1):
                        nc.scalar.activation(dst[:, c, :], h[:, c, :], ACT.Copy, scale=g[:, c:c + 1]).then_inc(s["xhi_done"], 1)
                    nc.scalar.activation(sq[:, 2 * b:2 * b + 2, :], h[:, 2 * b:2 * b + 2, :], ACT.Square).then_inc(s["sq_done"], 1)

            def rstd_root(k, lo, hi):
                act.wait_ge(s["rec_ready"], k)
                nc.scalar.activation(rstd[:, 0, lo:hi], rec[:, 0, lo:hi], ACT.Sqrt).then_inc(s["rstd_ready"], 1)

            def ffn(f, lookahead=True):
                n, J0 = N_FFN[f], PAIRS * f

                def gate(J, m, it=None):
                    act.wait_ge(s["gate_scaled"], up(J + 1, it, 2))
                    nc.scalar.activation(ga_a, ga_s, ACT.Silu).then_inc(s["silu_done"], 1)
                    split_hi(m + 3, it)

                def hidden(J, m, it=None, pf=True):
                    act.wait_ge(s["hidden"], up(J + 1, it, 2))
                    if not (f == 0 and J < 2 and it is None):
                        act.wait_ge(s["slab_used"], up(m - 1, it))
                    nc.scalar.activation(hidden_part(f, 0, J), pair(hid), ACT.Copy).then_inc(s["hid_hi_done"], 1)
                    if pf:
                        split_hi(m + 3, it)

                gate(J0, n)
                hidden(J0, n + 1)
                loops = (PAIRS - 1) // 2 if lookahead else (PAIRS - 3) // 2
                with act.Fori(0, loops) as it:
                    for b in range(2):
                        gate(J0 + 1 + b, n + 2 + 3 * b, it)
                        hidden(J0 + 1 + b, n + 3 + 3 * b, it)
                        split_hi(n + 4 + 3 * b + 3, it)
                if not lookahead:
                    last = n + FFN_SLABS - 1
                    for j in (PAIRS - 2, PAIRS - 1):
                        m = n + 3 * j - 1
                        gate(J0 + j, m)
                        hidden(J0 + j, m + 1, pf=m + 4 <= last)
                        if m + 5 <= last:
                            split_hi(m + 5)

            for n in range(RING):
                split_hi(n)
            act.wait_ge(s["vec_ready"], 1)
            act.wait_ge(s["lb_ready"], 1)
            nc.scalar.activation(lb[:, 1:3, :], lb[:, 1:3, :], ACT.Exp).then_inc(s["lb_exp"], 1)
            input_hi(ffn_input(0)[0], vec[:, VEC["ffn1_norm"]:VEC["ffn1_norm"] + 8], 0)
            rstd_root(1, X0, L2)
            ffn(0)
            input_hi(x_hi[:, :, X0:], vec[:, VEC["mix_norm"]:], 4)
            split_hi(N_MIX1 + 2)
            rstd_root(2, X0, L2)
            act.wait_ge(s["rec_ready"], 3)
            nc.scalar.activation(rcol[:, 1, 0:2], rcol[:, 0, 0:2], ACT.Sqrt).then_inc(s["rstd_ready"], 1)
            mixer1_act(act, split_hi, input_hi)
            rstd_root(5, X0, L2)
            ffn(1)
            fg = vec[:, VEC["final_norm"]:]
            for b in range(4):
                input_hi(x_hi[:, :, X0:], gfp, 12, [b])
                for c in (2 * b, 2 * b + 1):
                    nc.scalar.activation(sq2[:, c, :], h[:, c, :], ACT.Square, scale=fg[:, c:c + 1]).then_inc(s["sq2_done"], 1)
            split_hi(N_MIX2 + 2)
            rstd_root(6, X0, L2)
            act.wait_ge(s["rec_ready"], 7)
            nc.scalar.activation(rstd[:, 1, :], rec[:, 1, :], ACT.Sqrt).then_inc(s["rstd_ready"], 1)
            mixer2_act(act, split_hi)
            rstd_root(8, X0, L2)
            input_hi(a_hi, vec[:, VEC["ffn_pre_g_2"]:], 16)
            rstd_root(9, X0, L2)
            ffn(2, lookahead=False)
            pg = vec[:, VEC["ffn_post_g_2"]:]
            for b in range(4):
                if b < 3:
                    act.wait_ge(s["y_bank"], 6 + b + 1)
                else:
                    act.wait_ge(s["slab_used"], N_ALL)
                for c in range(2):
                    nc.scalar.activation(yg[:, 2 * b + c, :], ps[:, 4 + b, SEQ * c:SEQ * c + SEQ], ACT.Copy,
                                         scale=pg[:, 2 * b + c:2 * b + c + 1]).then_inc(s["yg_done"], 1)
                nc.scalar.activation(sq[:, 2 * b:2 * b + 2, :].rearrange("p c t -> p (c t)"), ps[:, 4 + b, :],
                                     ACT.Square).then_inc(s["ysq_done"], 1)
            rstd_root(10, X0, L2)

        @block.vector
        def _(dve):
            chain = [0]

            def seq(ins):
                chain[0] += 1
                ins.then_inc(s["dve_chain"], 1)
                dve.wait_ge(s["dve_chain"], chain[0])

            def split_lo(n, it=None):
                if it is None and n >= N_ALL:
                    return
                dve.wait_ge(s["hi_ready"], up(n + 1, it))
                if it is None and n in (N_MIX2 + 5, N_MIX2 + 6):
                    for los, his, src in zip(q_parts(w_lo, n), q_parts(w_hi, n), q_parts(stage, n)):
                        for o, b, i in zip(los, his, src):
                            last = nc.vector.tensor_tensor(o, i, b.bitcast(F32), ALU.subtract)
                    last.then_inc(s["lo_ready"], 1)
                    return
                if it is None and n == N_MIX2 + 2:
                    o, b = (v[:, n % RING, 0:D].rearrange("p (k two c) -> p k two c", k=DC, two=2) for v in (w_lo, w_hi))
                    i = wview(stage, n, DC, ROPE).unsqueeze(2).to_broadcast([P, DC, 2, ROPE])
                else:
                    o, b, i = (v[:, n % RING, 0:slab_words(n)] for v in (w_lo, w_hi, stage))
                nc.vector.tensor_tensor(o, i, b.bitcast(F32), ALU.subtract).then_inc(s["lo_ready"], 1)

            def input_lo(b, g, base, dst=(x_hi[:, :, X0:], x_lo[:, :, X0:])):
                for c in (2 * b, 2 * b + 1):
                    dve.wait_ge(s["xhi_done"], base + c + 1)
                    nc.vector.scalar_tensor_tensor(out=dst[1][:, c, :], in0=h[:, c, :], scalar=g[:, c:c + 1],
                                                   in1=dst[0][:, c, :].bitcast(F32), op0=ALU.mult,
                                                   op1=ALU.subtract).then_inc(s["xlo_done"], 1)

            def sum_squares(src, dst, sq_count):
                dve.wait_ge(s["sq_done"], sq_count)
                nc.vector.tensor_reduce(dst, src.rearrange("p c t -> p t c"), AX_X, ALU.add).then_inc(s["ss_ready"], 1)

            def zero_y():
                nc.vector.memset(ps[:, 4:8, :], 0.0).then_inc(s["y_zeroed"], 1)

            def mean_to_rec(k, src):
                dve.wait_ge(s["mean_done"], k)
                seq(nc.vector.tensor_scalar(rec[:, 0, X0:], src, EPS, None, ALU.add))
                nc.vector.reciprocal(rec[:, 0, X0:], rec[:, 0, X0:]).then_inc(s["rec_ready"], 1)

            bc2 = rstd[:, 0, X0:].unsqueeze(1).to_broadcast([P, 2, SEQ])

            def ffn(f, norm, rstd_count, lookahead=True):
                n, J0 = N_FFN[f], PAIRS * f

                def gate(J, m, it=None):
                    dve.wait_ge(s["slab_used"], up(m + 1, it))
                    nc.vector.tensor_tensor(ga_s.rearrange("p (c t) -> p c t", c=2), ps[:, J % 2, :].rearrange("p (c t) -> p c t", c=2), bc2,
                                            ALU.mult).then_inc(s["gate_scaled"], 1)
                    split_lo(m + 3, it)

                def hidden(J, m, it=None, pf=True):
                    dve.wait_ge(s["slab_used"], up(m + 1, it))
                    nc.vector.tensor_tensor(up_s.rearrange("p (c t) -> p c t", c=2), ps[:, 2 + J % 2, :].rearrange("p (c t) -> p c t", c=2), bc2,
                                            ALU.mult).then_inc(s["up_scaled"], 1)
                    dve.wait_ge(s["up_scaled"], up(J + 1, it, 2))
                    dve.wait_ge(s["silu_done"], up(J + 1, it, 2))
                    nc.vector.tensor_tensor(hid, ga_a, up_s, ALU.mult).then_inc(s["hidden"], 1)
                    dve.wait_ge(s["hidden"], up(J + 1, it, 2))
                    dve.wait_ge(s["hid_hi_done"], up(J + 1, it, 2))
                    nc.vector.tensor_tensor(hidden_part(f, 1, J), pair(hid), hidden_part(f, 0, J).bitcast(F32),
                                            ALU.subtract).then_inc(s["hid_lo_done"], 1)
                    if pf:
                        split_lo(m + 3, it)

                zero_y()
                mean_to_rec(norm, ps[:, 3 - J0 % 2, 0:SEQ])
                dve.wait_ge(s["rstd_ready"], rstd_count)
                gate(J0, n)
                hidden(J0, n + 1)
                loops = (PAIRS - 1) // 2 if lookahead else (PAIRS - 3) // 2
                with dve.Fori(0, loops) as it:
                    for b in range(2):
                        gate(J0 + 1 + b, n + 2 + 3 * b, it)
                        hidden(J0 + 1 + b, n + 3 + 3 * b, it)
                        split_lo(n + 4 + 3 * b + 3, it)
                if not lookahead:
                    last = n + FFN_SLABS - 1
                    for j in (PAIRS - 2, PAIRS - 1):
                        m = n + 3 * j - 1
                        gate(J0 + j, m)
                        hidden(J0 + j, m + 1, pf=m + 4 <= last)
                        if m + 5 <= last:
                            split_lo(m + 5)

            def residual(b, scale):
                hb = h[:, 2 * b:2 * b + 2, :].rearrange("p c t -> p (c t)")
                nc.vector.scalar_tensor_tensor(out=hb, in0=ps[:, 4 + b, :], scalar=scale, in1=hb,
                                               op0=ALU.mult, op1=ALU.add).then_inc(s["h_new"], 1)

            def ffn_residual(f, g, base, scale=0.5):
                n = N_FFN[f]
                for b in range(4):
                    if b < 3:
                        dve.wait_ge(s["y_bank"], 3 * f + b + 1)
                    else:
                        dve.wait_ge(s["slab_used"], n + FFN_SLABS)
                    residual(b, scale)
                    if g is not None:
                        dve.wait_ge(s["h_new"], base // 2 + b + 1)
                        input_lo(b, g, base)

            for n in range(RING):
                split_lo(n)
            dve.wait_ge(s["vec_T"], 1)
            nc.vector.tensor_copy(vec[:], ps[:, 0, 0:NVEC]).then_inc(s["vec_ready"], 1)
            dve.wait_ge(s["vec_ready"], 1)
            l0 = vec[:, VEC["lb_logits_2"]:VEC["lb_logits_2"] + DC]
            l1 = vec[:, VEC["lb_logits_2"] + DC:VEC["lb_logits_2"] + 2 * DC]
            seq(nc.vector.tensor_tensor(lb[:, 0, :], l0, l1, ALU.max))
            seq(nc.vector.tensor_tensor(lb[:, 1, :], l0, lb[:, 0, :], ALU.subtract))
            nc.vector.tensor_tensor(lb[:, 2, :], l1, lb[:, 0, :], ALU.subtract).then_inc(s["lb_ready"], 1)
            nc.vector.tensor_tensor(gfp[:], vec[:, VEC["final_norm"]:VEC["final_norm"] + DC],
                                    vec[:, VEC["mix_pre_g_2"]:VEC["mix_pre_g_2"] + DC], ALU.mult).then_inc(s["gfp_ready"], 1)
            g = vec[:, VEC["ffn1_norm"]:]
            for b in range(4):
                dve.wait_ge(s["x_T"], b + 1)
                nc.vector.tensor_copy(h[:, 2 * b:2 * b + 2, :].rearrange("p c t -> p (c t)"), ps[:, 4 + b, :]).then_inc(s["h_new"], 1)
                dve.wait_ge(s["h_new"], b + 1)
                input_lo(b, g, 0)
            sum_squares(sq[:], ss[:, 0, X0:], 4)
            dve.wait_ge(s["ws_T"], 1)
            nc.vector.tensor_copy(wsT.rearrange("p g i -> p (g i)"), ps[:, 1:3, :].rearrange("p b i -> p (b i)")).then_inc(s["ws_T_copied"], 1)
            dve.wait_ge(s["lb_exp"], 1)
            seq(nc.vector.tensor_tensor(lb[:, 3, :], lb[:, 1, :], lb[:, 2, :], ALU.add))
            seq(nc.vector.reciprocal(lb[:, 3, :], lb[:, 3, :]))
            seq(nc.vector.tensor_tensor(lb[:, 4, :], lb[:, 1, :], lb[:, 3, :], ALU.mult))
            seq(nc.vector.tensor_scalar(lb[:, 5, :], lb[:, 4, :], -1.0, 1.0, ALU.mult, ALU.add))
            dve.wait_ge(s["meta_T"], 1)
            gp = vec[:, VEC["mix_pre_g_2"]:VEC["mix_pre_g_2"] + DC].unsqueeze(2).to_broadcast([P, DC, META])
            seq(nc.vector.tensor_copy(meta[:, 0], ps[:, 3, 0:P].rearrange("p (c t) -> p c t", c=DC)))
            seq(nc.vector.tensor_tensor(meta[:, 1], meta[:, 0], meta[:, 0], ALU.mult))
            nc.vector.tensor_reduce(ss[:, 1, 0:META], meta[:, 1].rearrange("p c t -> p t c"), AX_X, ALU.add)
            seq(nc.vector.tensor_tensor(meta[:, 0], meta[:, 0], gp, ALU.mult))
            nc.vector.tensor_copy(x_hi[:, :, 0:META], meta[:, 0]).then_inc(s["meta_hi"], 1)
            dve.wait_ge(s["meta_hi"], 1)
            nc.vector.tensor_tensor(x_lo[:, :, 0:META], meta[:, 0], x_hi[:, :, 0:META].bitcast(F32),
                                    ALU.subtract).then_inc(s["meta_lo"], 1)
            ffn(0, 1, 1)
            ffn_residual(0, vec[:, VEC["mix_norm"]:], 8)
            split_lo(N_MIX1 + 2)
            sum_squares(sq[:], ss[:, 0, X0:], 8)
            mixer1_dve(dve, split_lo, seq, input_lo, residual, mean_to_rec)
            sum_squares(sq[:], ss[:, 0, X0:], 12)
            ffn(1, 3, 5)
            ffn_residual(1, gfp, 24)
            split_lo(N_MIX2 + 2)
            sum_squares(sq[:], ss[:, 0, X0:], 16)
            dve.wait_ge(s["sq2_done"], 8)
            nc.vector.tensor_reduce(ss[:, 1, X0:], sq2.rearrange("p c t -> p t c"), AX_X, ALU.add).then_inc(s["ss_ready"], 1)
            mixer2_dve(dve, split_lo, seq, mean_to_rec)
            for b in range(4):
                dve.wait_ge(s["h_new"], 16 + b + 1)
                input_lo(b, vec[:, VEC["ffn_pre_g_2"]:], 32, (a_hi, a_lo))
            sum_squares(sq[:], ss[:, 0, X0:], 20)
            ffn(2, 6, 9, lookahead=False)
            dve.wait_ge(s["ysq_done"], 4)
            nc.vector.tensor_reduce(ss[:, 0, X0:], sq[:].rearrange("p c t -> p t c"), AX_X, ALU.add).then_inc(s["ss_ready"], 1)
            mean_to_rec(7, ps[:, 0, 0:SEQ])
            dve.wait_ge(s["rstd_ready"], 10)
            dve.wait_ge(s["yg_done"], 8)
            for b in range(4):
                v, hb = yg[:, 2 * b:2 * b + 2, :], h[:, 2 * b:2 * b + 2, :]
                seq(nc.vector.tensor_tensor(v, v, bc2, ALU.mult))
                nc.vector.tensor_tensor(hb, hb, v, ALU.add).then_inc(s["h_new"], 1)
            for i in range(NT):
                for b in range(2):
                    dve.wait_ge(s["out_T"], 2 * i + b + 1)
                    nc.vector.tensor_copy(out_tok[:, i, 512 * b:512 * b + 512], ps[:, 2 * i + b, :]).then_inc(s["out_copied"], 1)

        @block.tensor
        def _(pe):
            def products(o, wh, wl, xh, xl, start, stop, skip=False):
                nc.tensor.matmul(o, wl, xh, start=start, stop=False, skip_group_check=skip)
                nc.tensor.matmul(o, wh, xl, start=False, stop=False, skip_group_check=skip)
                return nc.tensor.matmul(o, wh, xh, start=False, stop=stop, skip_group_check=skip)

            def slab_ready(n, it=None):
                pe.wait_ge(s["lo_ready"], up(n + 1, it))

            def feature_slab(n, outs, src=(x_hi[:, :, X0:], x_lo[:, :, X0:]), it=None, parts_base=None):
                slab_ready(n, it)
                wh, wl = wview(w_hi, n, DC), wview(w_lo, n, DC)
                for c in range(2):
                    for k in range(DC):
                        if parts_base is not None and c == 0:
                            pe.wait_ge(s["xlo_done"], parts_base + k + 1)
                        last = products(outs[c], wh[:, k, P * c:P * c + P], wl[:, k, P * c:P * c + P],
                                        src[0][:, k, :], src[1][:, k, :], k == 0, k == DC - 1)
                last.then_inc(s["slab_used"], 1)

            def down_slab(f, n, J, last_one=False, it=None):
                slab_ready(n, it)
                pe.wait_ge(s["hid_lo_done"], up(J + 1, it, 2))
                wh, wl = wview(w_hi, n, 2), wview(w_lo, n, 2)
                hh, hl = hidden_part(f, 0, J), hidden_part(f, 1, J)
                order = [(k, m) for m in range(DC) for k in range(2)] if last_one else [(k, m) for k in range(2) for m in range(DC)]
                for k, m in order:
                    o = ps[:, 4 + m // 2, SEQ * (m % 2):SEQ * (m % 2) + SEQ]
                    last = products(o, wh[:, k, P * m:P * m + P], wl[:, k, P * m:P * m + P], hh[:, k, :], hl[:, k, :],
                                    False, last_one and k == 1, skip=True)
                    if last_one and k == 1 and m in (1, 3, 5):
                        last.then_inc(s["y_bank"], 1)
                last.then_inc(s["slab_used"], 1)

            def halves(bank):
                return [ps[:, bank, 0:SEQ], ps[:, bank, SEQ:2 * SEQ]]

            def mean_mm(k, o, width=SEQ):
                pe.wait_ge(s["ss_ready"], k)
                return nc.tensor.matmul(o, ones[:], ss[:, 0, X0:], start=True, stop=True)

            def ffn(f, base, norm, rec):
                n, J0 = N_FFN[f], PAIRS * f

                def gate(J, m, it=None, first=False):
                    if J >= 1:
                        pe.wait_ge(s["gate_scaled"], up(max(J - 1, 1), it, 2))
                    feature_slab(m, halves(J % 2), ffn_input(f), it=it, parts_base=base if first else None)

                def upward(J, m, it=None):
                    if J >= 1:
                        pe.wait_ge(s["up_scaled"], up(max(J - 1, 1), it, 2))
                    feature_slab(m, halves(2 + J % 2), ffn_input(f), it=it)

                gate(J0, n, first=True)
                mean_mm(norm, ps[:, 3 - J0 % 2, 0:SEQ]).then_inc(s["mean_done"], 1)
                upward(J0, n + 1)
                pe.wait_ge(s["y_zeroed"], f + 1)
                pe.wait_ge(s["rec_ready"], rec)
                with pe.Fori(0, (PAIRS - 1) // 2) as it:
                    for b in range(2):
                        J = J0 + 1 + b
                        gate(J, n + 2 + 3 * b, it)
                        upward(J, n + 3 + 3 * b, it)
                        down_slab(f, n + 4 + 3 * b, J - 1, it=it)
                down_slab(f, n + FFN_SLABS - 1, J0 + PAIRS - 1, last_one=True)

            def token_slab(n, outs):
                slab_ready(n)
                wh, wl = wview(w_hi, n, DC), wview(w_lo, n, DC)
                for t in range(NT):
                    t0 = X0 + P * t
                    for k in range(DC):
                        last = products(outs[t], x_hi[:, k, t0:t0 + P], x_lo[:, k, t0:t0 + P], wh[:, k, :], wl[:, k, :],
                                        k == 0, k == DC - 1)
                last.then_inc(s["slab_used"], 1)

            def branch_slab(n, c0, banks, nk=4, parts=None):
                slab_ready(n)
                wh, wl = wview(w_hi, n, nk), wview(w_lo, n, nk)
                for c in range(4):
                    o = ps[:, banks + c // 2, SEQ * (c % 2):SEQ * (c % 2) + SEQ]
                    for k in range(nk):
                        last = products(o, wh[:, k, P * c:P * c + P], wl[:, k, P * c:P * c + P],
                                        a_hi[:, c0 + k, :], a_lo[:, c0 + k, :], k == 0, k == nk - 1)
                last.then_inc(s["slab_used"], 1)

            def mixer1():
                n = N_MIX1
                order = (0, 2, 1, 3)

                def scores(g):
                    pe.wait_ge(s["evac"], 4)
                    for o, j in enumerate(order):
                        c, r = 2 * g + j // 2, AD * (j % 2)
                        nc.tensor.matmul(ps[:, 6 + o // 2, P * (o % 2):P * (o % 2) + P], qT[r:r + AD, c, 0:P],
                                         kT[r:r + AD, c, 0:P], start=True, stop=True)
                        last = nc.tensor.matmul(ps[:, 4 + o // 2, SEQ * (o % 2):SEQ * (o % 2) + SEQ], qT[r:r + AD, c, P:],
                                                kT[r:r + AD, c, :], start=True, stop=True)
                    last.then_inc(s["s1_mm"], 1)

                def turn_probs(g):
                    pe.wait_ge(s["p1_ready"], 2 * g + 2)
                    for o in range(4):
                        for j in range(3):
                            last = nc.tensor.transpose(ps[:, 4 + o, P * j:P * j + P], S1[:, o, P * j:P * j + P], ident)
                        last.then_inc(s["p1_T"], 1)

                def attend(g):
                    pe.wait_ge(s["p1_copied"], 4 * g + 4)
                    for o, j in enumerate(order):
                        v = AD * (4 * g + j)
                        out_ = ps[AD * (j % 2):AD * (j % 2) + AD, 4, SEQ * (j // 2):SEQ * (j // 2) + SEQ]
                        nc.tensor.matmul(out_, V1[:, 0, v:v + AD], pT1[:, o, 0:SEQ], start=True, stop=False)
                        last = nc.tensor.matmul(out_[:, P:], V1[:, 1, v:v + AD], pT1[:, o, SEQ:], start=False, stop=True)
                    last.then_inc(s["pv1_mm"], 1)

                def spatial():
                    pe.wait_ge(s["vln_ready"], 3)
                    for g in range(GG):
                        for t in range(NT):
                            c = g // 2
                            o = ps[GD * (g % 2):GD * (g % 2) + GD, 5 + c // 2, SEQ * (c % 2) + P * t:SEQ * (c % 2) + P * t + P]
                            last = nc.tensor.matmul(o, vg[:, t, GD * g:GD * g + GD], wsT[:, g, :], start=True, stop=True)
                    last.then_inc(s["mixed_mm"], 1)

                for i in range(26):
                    if 2 <= i < 22:
                        pe.wait_ge(s["evac"], i - 1)
                    k = 2 * (i % 2)
                    outs = [ps[:, k, 0:SEQ], ps[:, k + 1, 0:SEQ]]
                    if i in (4, 5, 8, 9):
                        token_slab(n + i, outs)
                    elif i < 18:
                        feature_slab(n + i, outs, parts_base=8 if i == 0 else None)
                    elif i < 22:
                        if i == 18:
                            pe.wait_ge(s["attn_lo"], 2)
                        if i == 19:
                            pe.wait_ge(s["gm_lo"], 1)
                        branch_slab(n + i, 4 * (i % 2), k)
                    else:
                        pe.wait_ge(s["m_lo"], 2)
                        feature_slab(n + i, halves(4 + i - 22))
                    if i == 0:
                        mean_mm(2, ps[:, 4, 0:SEQ])
                        for t in range(NT):
                            last = nc.tensor.matmul(ps[:, 4, SEQ + 2 * t:SEQ + 2 * t + 2], ss[:, 0, X0 + P * t:X0 + P * t + P],
                                                    ones[:, 0:2], start=True, stop=True)
                        last.then_inc(s["mean_done"], 1)
                    if i == 4:
                        pe.wait_ge(s["rec_ready"], 3)
                        scores(0)
                    if i == 7:
                        turn_probs(0)
                    if i == 8:
                        attend(0)
                    if i == 9:
                        pe.wait_ge(s["attn_lo"], 1)
                        scores(1)
                    if i == 12:
                        turn_probs(1)
                    if i == 13:
                        attend(1)
                    if i == 15:
                        spatial()

            def mixer2():
                n = N_MIX2
                xs, xf = (x_hi[:, :, X0:], x_lo[:, :, X0:]), (x_hi, x_lo)

                def one_chunk_slab(n, o):
                    slab_ready(n)
                    wh, wl = wview(w_hi, n, DC, P), wview(w_lo, n, DC, P)
                    for k in range(DC):
                        last = products(o, wh[:, k, :], wl[:, k, :], x_hi[:, k, :], x_lo[:, k, :], k == 0, k == DC - 1)
                    last.then_inc(s["slab_used"], 1)

                def q_slab(n, banks):
                    slab_ready(n)
                    wh, wl = wview(w_hi, n, 2, 768), wview(w_lo, n, 2, 768)
                    for j in range(4):
                        o = ps[:, banks + j // 2, SEQ * (j % 2):SEQ * (j % 2) + SEQ]
                        for k in range(2):
                            c = NOPE * j
                            products(o, wh[:, k, c:c + NOPE], wl[:, k, c:c + NOPE], a_hi[:, k, :], a_lo[:, k, :], k == 0, k == 1)
                    for j in range(2):
                        for k in range(2):
                            c = 4 * NOPE + 2 * ROPE * j
                            last = products(ps[:, 7, SEQ * j:SEQ * j + SEQ], wh[:, k, c:c + P], wl[:, k, c:c + P], a_hi[:, k, :], a_lo[:, k, :], k == 0, k == 1)
                    last.then_inc(s["slab_used"], 1)

                def kv_slab(n, banks, spare):
                    slab_ready(n)
                    wh, wl = wview(w_hi, n, 2), wview(w_lo, n, 2)
                    ch, cl = kv_part(a_hi), kv_part(a_lo)
                    for j in range(4):
                        o = ps[:, (banks + j) if j < 2 else 2 + j, 0:L2]
                        for k in range(2):
                            c = (NOPE + VH) * j
                            products(o, wh[:, k, c:c + NOPE], wl[:, k, c:c + NOPE], ch[:, k, :], cl[:, k, :], k == 0, k == 1)
                    for t, bank in zip(TILES, (spare, 6, 7)):
                        for k in range(2):
                            vh, vl = (v[:, k, :].rearrange("p (h c) -> p h c", h=4)[:, :, NOPE:] for v in (wh, wl))
                            o = ps[:, bank, :].rearrange("p (h c) -> p h c", h=4)
                            last = products(o, ch[:, k, t:t + P], cl[:, k, t:t + P], vh, vl, k == 0, k == 1)
                    last.then_inc(s["slab_used"], 1)

                def scores(p):
                    for hh in range(2):
                        hd, r = 2 * p + hh, ROPE * hh
                        for o, t, nk in ((ps[:, 5 + hh, 0:K0], 0, K0), (ps[:, 5 + hh, K0:K0 + L2], P, L2)):
                            nc.tensor.matmul(o, qn[:, hd, t:t + P], kn[:, hd, 0:nk], start=True, stop=False)
                            last = nc.tensor.matmul(o, q_pe[r:r + ROPE, p, t:t + P], k_pe[r:r + ROPE, 0:nk], start=False, stop=True)
                    last.then_inc(s["s2_mm"], 1)

                def turn_probs(p):
                    pe.wait_ge(s["p2_ready"], 2 * p + 2)
                    for hh in range(2):
                        for j, c in enumerate((META, K0 + META, K0 + META + P)):
                            nc.tensor.transpose(ps[:, 5 + hh, P * j:P * j + P], S2[:, hh, c:c + P], ident)
                        for t in range(NT):
                            last = nc.tensor.transpose(ps[0:META, 4, SEQ * hh + P * t:SEQ * hh + P * t + P],
                                                       S2[:, hh, K0 * t:K0 * t + META], ident)
                    last.then_inc(s["p2_T"], 1)

                def attend(p):
                    pe.wait_ge(s["p2_copied"], 2 * p + 2)
                    if p:
                        pe.wait_ge(s["mla_lo"], p)
                    for hh in range(2):
                        v = VH * (2 * p + hh)
                        o = ps[:, 7, SEQ * hh:SEQ * hh + SEQ]
                        nc.tensor.matmul(o, V2[:, 0, v:v + VH], pT2[:, hh, 0:SEQ], start=True, stop=False)
                        nc.tensor.matmul(o[:, P:], V2[:, 1, v:v + VH], pT2[:, hh, SEQ:], start=False, stop=False)
                        last = nc.tensor.matmul(o, V2m[0:META, v:v + VH], pT2m[0:META, hh, :], start=False, stop=True)
                    last.then_inc(s["pv2_mm"], 1)

                def level(l):
                    if l == 0:
                        pe.wait_ge(s["f_ready"], 4)
                        pe.wait_ge(s["silu2_done"], 4)
                        pe.wait_ge(s["mla_lo"], 4)
                    else:
                        pe.wait_ge(s["hg_ready"], l)
                        pe.wait_ge(s["lvl_done"], 4 * l)
                    if l == 5:
                        pe.wait_ge(s["v_copied"], 2)
                    for hd in range(HH):
                        for t in range(NT):
                            o = ps[:, 4 + hd // 2, SEQ * (hd % 2) + P * t:SEQ * (hd % 2) + P * t + P]
                            last = nc.tensor.matmul(o, k2[:, hd, X0 + P * t:X0 + P * t + P], q2[:, hd, P * t:P * t + P],
                                                    start=True, stop=True)
                    last.then_inc(s["lvl_mm"], 1)

                def turn_v():
                    pe.wait_ge(s["evac"], E2 + 23)
                    for hd in range(HH):
                        last = nc.tensor.transpose(ps[0:META, hd // 4, P * (hd % 4):P * (hd % 4) + P], hiT[:, hd, 0:META], ident)
                    last.then_inc(s["vm_T"], 1)
                    pe.wait_ge(s["lvl_done"], 20)
                    for t in range(NT):
                        for hd in range(HH):
                            last = nc.tensor.transpose(ps[:, 4 + 2 * t + hd // 4, P * (hd % 4):P * (hd % 4) + P],
                                                       hiT[:, hd, X0 + P * t:X0 + P * t + P], ident)
                    last.then_inc(s["vT"], 1)

                def meta_scores(hd, bank):
                    for t, km in enumerate((k2[:, hd, 0:META], meta[:, 0, hd, :])):
                        c = SEQ * (hd % 2) + P * t
                        last = nc.tensor.matmul(ps[0:META, bank, c:c + P], km, q2[:, hd, P * t:P * t + P], start=True, stop=True)
                    return last

                def cross():
                    pe.wait_ge(s["hg_ready"], 8)
                    pe.wait_ge(s["lvl_done"], 32)
                    for hd in range(HH):
                        nc.tensor.matmul(ps[:, 4 + hd // 4, P * (hd % 4):P * (hd % 4) + P], k2[:, hd, X0:X0 + P],
                                         q2[:, hd, P:], start=True, stop=True)
                    for hd in range(4):
                        last = meta_scores(hd, 6 + hd // 2)
                    last.then_inc(s["cross_mm"], 1)

                def recurrence_out():
                    pe.wait_ge(s["am_copied"], 1)
                    for hd in range(HH):
                        o = ps[:, 4 + hd // 2, SEQ * (hd % 2):SEQ * (hd % 2) + SEQ]
                        v = P * hd
                        nc.tensor.matmul(o, V2[:, 0, v:v + P], AT[:, hd, 0:2, :].rearrange("p j t -> p (j t)"), start=True, stop=False)
                        nc.tensor.matmul(o[:, P:], V2[:, 1, v:v + P], AT[:, hd, 2, :], start=False, stop=False)
                        last = nc.tensor.matmul(o, V2m[0:META, v:v + P], Am[0:META, hd, :], start=False, stop=True)
                        if hd % 2:
                            last.then_inc(s["o_mm"], 1)

                for i in range(43):
                    if 2 <= i < 39:
                        pe.wait_ge(s["evac"], E2 + i - 1)
                    if i == 9:
                        pe.wait_ge(s["evac"], E2 + 9)
                    k = 2 * (i % 2)
                    if i in FULL and i != 2:
                        feature_slab(n + i, [ps[:, k, 0:L2], ps[:, k + 1, 0:L2]], xf)
                    elif i == 2:
                        one_chunk_slab(n + i, ps[:, 0, 0:L2])
                    elif i in (5, 6):
                        if i == 5:
                            pe.wait_ge(s["ac_lo"], 4)
                        else:
                            pe.wait_ge(s["evac"], E2 + i)
                        q_slab(n + i, k)
                    elif i in (7, 8):
                        pe.wait_ge(s["evac"], E2 + i)
                        kv_slab(n + i, k, 2 - k)
                    elif i < 39:
                        if i == 23:
                            pe.wait_ge(s["mla_lo"], 4)
                        if i == 24:
                            pe.wait_ge(s["vm_copied"], 1)
                        if i == 35:
                            pe.wait_ge(s["o_lo"], 2)
                        src = (a_hi, a_lo) if 23 <= i < 27 or i >= 35 else xs
                        feature_slab(n + i, [ps[:, k, 0:SEQ], ps[:, k + 1, 0:SEQ]], src, parts_base=24 if i == 0 else None)
                    else:
                        pe.wait_ge(s["m2_lo"], 4)
                        feature_slab(n + i, halves(4 + i - 39))
                    if i == 0:
                        pe.wait_ge(s["ss_ready"], 5)
                        nc.tensor.matmul(ps[:, 4, 0:SEQ], ones[:], ss[:, 0, X0:], start=True, stop=True)
                        nc.tensor.matmul(ps[:, 5, 0:L2], ones[:], ss[:, 1, :], start=True, stop=True).then_inc(s["mean_done"], 1)
                    if i == 3:
                        pe.wait_ge(s["css_ready"], 2)
                        nc.tensor.matmul(ps[:, 4, 0:SEQ], ones[:], ss[:, 0, X0:], start=True, stop=True)
                        nc.tensor.matmul(ps[:, 5, 0:L2], ones[:], ss[:, 1, :], start=True, stop=True)
                        for j, t in enumerate(TILES):
                            last = nc.tensor.matmul(ps[:, 6, 2 * j:2 * j + 2], ss[:, 1, t:t + P], ones[:, 0:2], start=True, stop=True)
                        last.then_inc(s["cmean_mm"], 1)
                    if i in MLA_T:
                        turn_probs(MLA_T[i])
                    if i in MLA_PV:
                        attend(MLA_PV[i])
                    if i in MLA_S:
                        p = MLA_S[i]
                        if p == 0:
                            pe.wait_ge(s["evac"], E2 + 9)
                            pe.wait_ge(s["rope_done"], 2)
                        scores(p)
                    if i in LSLOT:
                        level(LSLOT[i])
                    if i == 23:
                        turn_v()
                    if i == 27:
                        cross()
                    if i == 28:
                        pe.wait_ge(s["cross_copied"], 2)
                        for hd in range(4, 8):
                            last = meta_scores(hd, 4 + (hd - 4) // 2)
                        last.then_inc(s["am_mm"], 1)
                    if i == 29:
                        recurrence_out()
                    if i == 30:
                        for b in range(4):
                            pe.wait_ge(s["osq_done"], b // 2 + 1)
                            if b == 2:
                                pe.wait_ge(s["o_ready"], 2)
                            nc.tensor.matmul(ps[:, 4 + b, :], ones[:], k2[:, 2 * b:2 * b + 2, 0:SEQ], start=True, stop=True).then_inc(s["osum_mm"], 1)
                mean_mm(6, ps[:, 0, 0:SEQ]).then_inc(s["mean_done"], 1)

            pe.wait_ge(s["tab_loaded"], 16)
            pe.wait_ge(s["vec_loaded"], 16 * len(VEC_ROWS))
            nc.tensor.transpose(ps[:, 0, 0:NVEC], vrows[0:NVEC, :], ident[0:NVEC, 0:NVEC]).then_inc(s["vec_T"], 1)
            pe.wait_ge(s["x_loaded"], 16)
            for c in range(DC):
                for i in range(NT):
                    last = nc.tensor.transpose(ps[:, 4 + c // 2, SEQ * (c % 2) + P * i:SEQ * (c % 2) + P * i + P],
                                               x_tok[:, i, P * c:P * c + P], ident)
                if c % 2:
                    last.then_inc(s["x_T"], 1)
            pe.wait_ge(s["ws_masked"], 1)
            for g in range(GG):
                last = nc.tensor.transpose(ps[:, 1 + g // 4, P * (g % 4):P * (g % 4) + P], ws[:, g, :], ident)
            last.then_inc(s["ws_T"], 1)
            pe.wait_ge(s["meta_loaded"], 16)
            for c in range(DC):
                last = nc.tensor.transpose(ps[:, 3, META * c:META * c + META], meta_tok[0:META, P * c:P * c + P], ident[0:META, 0:META])
            last.then_inc(s["meta_T"], 1)
            pe.wait_ge(s["ones_ready"], 1)
            pe.wait_ge(s["vec_ready"], 1)
            pe.wait_ge(s["ws_T_copied"], 1)
            pe.wait_ge(s["meta_lo"], 1)
            ffn(0, 0, 1, 1)
            mixer1()
            ffn(1, 16, 3, 5)
            mixer2()
            ffn(2, 32, 7, 9)
            mean_mm(8, ps[:, 0, 0:SEQ]).then_inc(s["mean_done"], 1)
            pe.wait_ge(s["h_new"], 24)
            for i in range(NT):
                for b in range(2):
                    for c in range(4 * b, 4 * b + 4):
                        last = nc.tensor.transpose(ps[:, 2 * i + b, P * (c % 4):P * (c % 4) + P], h[:, c, P * i:P * i + P], ident)
                    last.then_inc(s["out_T"], 1)


_INS = [
    "x", "ffn1_norm", "ffn1_w_gate", "ffn1_w_up", "ffn1_w_down", "mix_norm", "w_in", "gmlp_ln_g", "gmlp_ln_b",
    "gmlp_w_s", "gmlp_b_s", "w_branch_attn", "w_branch_gmlp", "w_gate", "b_gate", "w_out", "ffn2_norm",
    "ffn2_w_gate", "ffn2_w_up", "ffn2_w_down", "final_norm", "meta_tokens_2", "w_in_2", "b_gate_2",
    "lb_logits_2", "hg_norm_g_2", "w_hg_o_2", "q_a_norm_g_2", "w_q_b_2", "kv_a_norm_g_2", "w_kv_b_2",
    "w_mla_o_2", "w_out_2", "mix_pre_g_2", "mix_post_g_2", "ffn_pre_g_2", "ffn_post_g_2", "w_ffn_in_2",
    "w_ffn_out_2"]


def kernel(**inputs):
    import concourse.bacc as _bacc
    from concourse.bass_utils import run_bass_kernel_spmd as _run

    nc = _bacc.Bacc("TRN2", target_bir_lowering=False, num_devices=1)
    arrays, args = {}, {}

    def give(name, value):
        v = np.ascontiguousarray(value)
        arrays[f"in_{name}_dram"] = v
        return nc.dram_tensor(f"in_{name}_dram", v.shape, mybir.dt.from_np(v.dtype), kind="ExternalInput").ap()

    for name in _INS:
        args[name] = give(name, inputs[name])
    tab_d = give("tables", constants())
    out = nc.dram_tensor("out_0_dram", (1, SEQ, D), F32, kind="ExternalOutput").ap()
    program(nc, args, tab_d, out)
    r = _run(nc, [arrays], core_ids=[0])
    return r.results[0]["out_0_dram"]
```

```python
from contextlib import ExitStack

import numpy as np

import concourse.bass as bass
from concourse import mybir

F32 = mybir.dt.float32
F32R = mybir.dt.float32r
ALU = mybir.AluOpType
ACT = mybir.ActivationFunctionType
AX_X = mybir.AxisListType.X

P = 128
D = 1024
DC = D // P
SEQ = 256
META = 16
L2 = SEQ + META
X0 = META
FF = 2816
PAIRS = FF // 256
NT = SEQ // P
EPS = 1e-6

AH, AD = 8, 64
AW = AH * AD
GG, GC, GW = 8, 128, 512
GD = GW // GG
HH, HC = 8, 16
NOPE, ROPE, VH = 128, 64, 128
QL = 256
MLA_SCALE = float(NOPE + ROPE) ** -0.5
LEVELS = [0, 1, 2, 4, 8, 16, 32, 64]

RING = 3
SLAB = 2048

FFN_SLABS = 3 * PAIRS
N_FFN = [0, FFN_SLABS + 26, 2 * FFN_SLABS + 26 + 43]
N_MIX1 = FFN_SLABS
N_MIX2 = 2 * FFN_SLABS + 26
N_ALL = 3 * FFN_SLABS + 26 + 43
assert N_FFN[1] == N_MIX1 + 26 and N_FFN[2] == N_MIX2 + 43

VEC_ROWS = [("ffn1_norm", 8), ("mix_norm", 8), ("ffn2_norm", 8), ("final_norm", 8), ("mix_pre_g_2", 8),
            ("mix_post_g_2", 8), ("ffn_pre_g_2", 8), ("ffn_post_g_2", 8), ("b_gate", 16), ("b_gate_2", 16),
            ("lb_logits_2", 16), ("hg_norm_g_2", 1), ("q_a_norm_g_2", 2), ("kv_a_norm_g_2", 2)]
VEC = {}
_at = 0
for _name, _k in VEC_ROWS:
    VEC[_name] = _at
    _at += _k
NVEC = _at

T_MASK, T_COS, T_SIN, T_LVL = 0, L2, 2 * L2, 3 * L2
TAB = T_LVL + P * len(LEVELS)
NEG = -1e30


def constants():
    tab = np.zeros((P, TAB), np.float32)
    q, k = np.arange(P)[:, None], np.arange(P)[None, :]
    tab[:, T_MASK + L2 - P:T_MASK + L2] = np.where(k <= q, 0.0, NEG)
    inv_freq = (1.0 / (np.float32(10000.0) ** (np.arange(0, ROPE, 2, dtype=np.float32) / np.float32(ROPE)))).astype(np.float32)
    ang = (np.arange(L2, dtype=np.float32)[:, None] * inv_freq[None, :]).astype(np.float32)
    row = np.arange(P)
    sign = np.where(row % ROPE < ROPE // 2, -1.0, 1.0).astype(np.float32)
    tab[:, T_COS:T_COS + L2] = np.cos(ang).T[row % (ROPE // 2)]
    tab[:, T_SIN:T_SIN + L2] = np.sin(ang).T[row % (ROPE // 2)] * sign[:, None]
    s, t = np.arange(P)[:, None], np.arange(P)[None, :]
    for i, h in enumerate(LEVELS):
        keep = (s == t) if h == 0 else ((s // (2 * h) == t // (2 * h)) & (s % (2 * h) < h) & (t % (2 * h) >= h))
        tab[:, T_LVL + P * i:T_LVL + P * i + P] = keep
    return tab


SEMS = """slab_used hi_ready lo_ready
x_loaded0 x_loaded1 vec_loaded id_loaded tab_loaded ws_loaded gm_loaded meta_loaded store_done
vec_T x_T meta_T ws_T vec_ready ones_ready gfp_ready ws_masked ws_T_copied lb_exp lb_ready
h_new xhi_done xlo_done sq_done ss_ready mean_done std_ready rstd_ready meta_hi meta_lo
hT_T hT_copied y_bank y_zeroed gate_scaled silu_done up_scaled hidden hid_hi_done hid_lo_done
evac out_T out_copied dve_chain pool_chain ln_stats
""".split()
SEMS1 = """gelu_done gsig_done s1_mm s1_masked s1_biased exp1_done p1_ready p1_T p1_copied pv1_mm  attn_hi attn_lo
vln_ready mixed_mm gm_ready gm_hi gm_lo merged1 m_hi m_lo""".split()
SEMS2 = """sq2_done x2_done m2_summed cstd_ready yg_T ss2_ready kv_left orec_ready obc_mm mg_scaled mg_scaled2 c_ready csq_done ac_hi ac_lo silu2_done rope_done s2_mm s2_masked s2_biased exp2_done
p2_ready p2_T p2_copied pv2_mm mla_hi mla_lo fsig_done f_ready at_zero hg_ready lvl_mm lvl_done gsigb_done vT vm_T v_copied
vm_copied cross_mm cross_copied am_mm am_copied o_mm o_ready osq_done osum_mm ostd_done o_final o_hi o_lo gsiga_done
dve_chain2 css_ready cmean_mm merged2 m2_hi m2_lo mg_done msq_done yg_done ysq_done """.split()


def program(nc, a, vec_d, id_d, tab_d, out):
    ctx = ExitStack()
    with ctx:
        def sb(name, shape, dt):
            return ctx.enter_context(nc.sbuf_tensor(name, shape, dt))

        s = {}
        for name in SEMS + SEMS1 + SEMS2:
            s[name] = ctx.enter_context(nc.semaphore(name))
        slab_in = [ctx.enter_context(nc.semaphore(f"slab_in{i}")) for i in range(RING)]

        ps = ctx.enter_context(nc.psum_tensor("ps", [P, 8, 512], F32))
        stage = sb("stage", [P, RING, SLAB], F32)
        w_hi = sb("w_hi", [P, RING, SLAB], F32R)
        w_lo = sb("w_lo", [P, RING, SLAB], F32R)
        x_hi = sb("x_hi", [P, DC, L2], F32R)
        x_lo = sb("x_lo", [P, DC, L2], F32R)
        a_hi = sb("a_hi", [P, DC, SEQ], F32R)
        a_lo = sb("a_lo", [P, DC, SEQ], F32R)
        h = sb("h", [P, DC, SEQ], F32)
        sq = sb("sq", [P, DC, SEQ], F32)
        ar = sb("ar", [P, 17408], F32)
        tab = sb("tab", [P, TAB], F32)
        ident = sb("ident", [P, P], F32)
        vec = sb("vec", [P, NVEC], F32)
        gfp = sb("gfp", [P, DC], F32)
        lb = sb("lb", [P, 6, DC], F32)
        ones = sb("ones", [P, P], F32)
        eps = sb("eps", [P, 1], F32)
        pick = sb("pick", [P, 2 * HH - 1], F32)
        warm = sb("warm", [P, 16], F32)
        ss = sb("ss", [P, 2, L2], F32)
        std = sb("std", [P, 2, L2], F32)
        rstd = sb("rstd", [P, 2, L2], F32)
        rcol = sb("rcol", [P, 2, 8], F32)

        mask = tab[:, T_MASK:T_MASK + L2]
        lvl = tab[:, T_LVL:].bitcast(mybir.dt.int32).rearrange("p (l t) -> p l t", t=P)

        def view(at, *dims):
            n = int(np.prod(dims))
            v = ar[:, at:at + n]
            if len(dims) == 1:
                return v
            names = "abcd"[:len(dims)]
            return v.rearrange("p (" + " ".join(names) + ") -> p " + " ".join(names),
                               **dict(zip(names, dims)))

        x_tok = view(0, NT, D)
        vrows = view(2048, P)
        ws = view(14336, GG, GC)
        meta_tok = view(2304, D)
        ga_s, ga_a = view(0, 512), view(512, 512)
        up_s, hid = view(1024, 512), view(1536, 512)

        def ffn_input(f):
            return (x_hi[:, :, X0:], x_lo[:, :, X0:]) if f == 0 else (a_hi[:], a_lo[:])

        def hidden_part(f, part, J):
            c = 2 * (J % 2)
            return (a_hi, a_lo)[part][:, c:c + 2, :] if f == 0 else (x_hi, x_lo)[part][:, 4 + c:6 + c, X0:]

        def pair(v):
            return v.rearrange("p (c t) -> p c t", c=2)
        qT, kT = view(2048, 4, SEQ), view(3072, 4, SEQ)
        V1 = view(4096, NT, AW)
        uT = view(5120, 4, SEQ)
        vg = view(6144, NT, GW)
        gates = view(7168, 16, SEQ)
        S1 = view(11264, 4, 384)
        pT1 = view(12800, 4, 384)
        wsT = view(15360, GG, GC)
        gbias = view(16384, 4, GC)
        ln_g, ln_b = view(14336, GW), view(14848, GW)
        tA, tB = view(0, 1024), view(1024, 1024)
        meta = sb("meta", [P, 2, DC, META], F32)
        small = sb("small", [P, 96], F32)
        out_tok = view(2048, NT, D)

        q2, k2, f2 = view(0, HH, SEQ), view(2048, HH, L2), view(4224, HH, L2)
        gA = view(4224, DC, SEQ)
        Am = view(4224, HH, SEQ)
        cq, ckv, q_sw = view(4224, 2, SEQ), view(4736, 2, L2), view(5280, 4, SEQ)
        qn, hiT, hgs = view(6400, HH, SEQ), view(6400, HH, L2), view(6400, HH, SEQ)
        kn, yb, sq2 = view(8576, HH, L2), view(8576, DC, SEQ), view(8576, DC, SEQ)
        V2, V2m = view(10752, NT, D), view(12800, D)
        AT = view(13824, HH, 3, P)
        q_pe, k_pe, k_sw = view(13824, 4, SEQ), view(14848, L2), view(15120, L2)
        S2 = view(15120, 2, P + META + L2)
        pT2, pT2m = view(15952, 2, 384), view(16896, 2, SEQ)
        mT = view(13824, 2, 512)
        mg = view(0, DC, SEQ)
        yg = view(4096, DC, SEQ)
        K0 = P + META
        sq_flat = sq[:].rearrange("p c t -> p (c t)")
        cq_sq, ckv_sq = sq_flat[:, 0:2 * SEQ].rearrange("p (c t) -> p c t", c=2), sq_flat[:, 512:512 + 2 * L2].rearrange("p (c t) -> p c t", c=2)
        r_q, r_kv = sq_flat[:, 1056:1056 + SEQ], sq_flat[:, 1312:1312 + L2]
        def kv_part(v):
            return v[:].rearrange("p c t -> p (c t)")[:, 512:512 + 2 * L2].rearrange("p (c t) -> p c t", c=2)
        R2 = rstd[:, 1, :]
        gB = sq
        TILES = (0, X0, X0 + P)
        FULL = (1, 2, 11, 12, 13, 14, 19, 20, 21, 22)
        LSLOT = {18: 0, 19: 1, 20: 2, 21: 3, 22: 4, 24: 5, 25: 6, 26: 7}
        MLA_S = {9: 0, 11: 1, 13: 2, 15: 3}
        MLA_T = {10: 0, 12: 1, 14: 2, 16: 3}
        MLA_PV = {11: 0, 13: 1, 15: 2, 17: 3}
        E2 = 22

        def token_means():
            return ps[:, 4, SEQ:SEQ + 4].rearrange("p (i two) -> p i two", two=2)[:, :, 0]

        def mixer_out(j):
            return ps[:, 4:6, 0:SEQ] if j == 0 else ps[:, (6, 7, 3)[j - 1], :].rearrange("p (c t) -> p c t", c=2)

        def slab_words(n):
            i = n - N_MIX2
            return 1536 if i in (5, 6) else SLAB

        def q_parts(v, n):
            nope, rope = 4 * NOPE, 4 * ROPE
            w = wview(v, n, 2, 768)
            if v is stage:
                w = w.rearrange("p k (h c) -> p k h c", h=4)
                return [(w[:, k, :, 0:NOPE], w[:, k, :, NOPE:]) for k in range(2)]
            return [(w[:, k, 0:nope].rearrange("p (h c) -> p h c", h=4), w[:, k, nope:].rearrange("p (h c) -> p h c", h=4))
                    for k in range(2)]

        def wait_slab(eng, n, it):
            base = 16 * (n // RING + 1)
            eng.wait_ge(slab_in[n % RING], base if it is None else it * (16 * 2) + base)

        def up(n, it, per=6):
            return n if it is None else it * per + n

        def wview(w, n, k, width=None):
            v = w[:, n % RING, :] if width is None else w[:, n % RING, 0:k * width]
            return v.rearrange("p (k c) -> p k c", k=k)

        def mixer1_act(act, split_hi, input_hi):
            n = N_MIX1

            def exps(g):
                act.wait_ge(s["s1_biased"], g + 1)
                for t in range(NT):
                    for o in range(4):
                        v = S1[:, o, P:] if t else S1[:, o, 0:P]
                        k = 4 * t + o
                        nc.scalar.activation(v, v, ACT.Exp, bias=small[:, 8 + k:9 + k],
                                             accum_out=small[:, 16 + k:17 + k]).then_inc(s["exp1_done"], 1)

            def copy_probs(g):
                for o in range(4):
                    act.wait_ge(s["p1_T"], 4 * g + o + 1)
                    nc.scalar.copy(pT1[:, o, :], ps[:, 4 + o, 0:384]).then_inc(s["p1_copied"], 1)

            def attn_hi(g):
                act.wait_ge(s["pv1_mm"], g + 1)
                nc.scalar.activation(a_hi[:, 2 * g:2 * g + 2, :].rearrange("p c t -> p (c t)"), ps[:, 4, :],
                                     ACT.Copy).then_inc(s["attn_hi"], 1)

            for i in range(26):
                if i in (19, 21):
                    q = (i - 19) // 2
                    act.wait_ge(s["merged1"], q + 1)
                    nc.scalar.activation(x_hi[:, 4 * q:4 * q + 4, X0:], tA.rearrange("p (c t) -> p c t", c=4),
                                         ACT.Copy).then_inc(s["m_hi"], 1)
                if i >= 22:
                    input_hi(a_hi, vec[:, VEC["ffn2_norm"]:], 8, [i - 22])
                split_hi(n + i + 3)
                if i == 5:
                    exps(0)
                if i == 7:
                    copy_probs(0)
                if i == 8:
                    attn_hi(0)
                if i == 9:
                    for j in range(2):
                        act.wait_ge(s["evac"], 9 + j)
                        v = vg[:, :, 256 * j:256 * j + 256]
                        nc.scalar.activation(v, v, ACT.Gelu_apprx_tanh).then_inc(s["gelu_done"], 1)
                    nc.scalar.activation(uT, uT, ACT.Gelu_apprx_tanh).then_inc(s["gelu_done"], 1)
                    act.wait_ge(s["ln_stats"], 2)
                    nc.scalar.activation(small[:, 58:60], small[:, 49:57:4], ACT.Sqrt, bias=eps[:]).then_inc(s["std_ready"], 1)
                if i == 10:
                    exps(1)
                if i == 12:
                    copy_probs(1)
                if i == 13:
                    attn_hi(1)
                if i == 15:
                    act.wait_ge(s["gm_ready"], 1)
                    nc.scalar.activation(a_hi[:, 4:8, :], tA.rearrange("p (c t) -> p c t", c=4), ACT.Copy).then_inc(s["gm_hi"], 1)
                if i == 17:
                    for c in range(16):
                        act.wait_ge(s["evac"], 10 + c // 2 + 1)
                        nc.scalar.activation(gates[:, c, :], gates[:, c, :], ACT.Sigmoid,
                                             bias=vec[:, VEC["b_gate"] + c:VEC["b_gate"] + c + 1]).then_inc(s["gsig_done"], 1)

        def mixer1_dve(dve, split_lo, seq, input_lo, residual, inverse):
            n = N_MIX1
            bc2 = rstd[:, 0, X0:].unsqueeze(1).to_broadcast([P, 2, SEQ])

            def acc(i):
                k = 2 * (i % 2)
                return ps[:, k:k + 2, 0:SEQ]

            def group_scores(g):
                dve.wait_ge(s["s1_mm"], g + 1)
                if g:
                    dve.wait_ge(s["p1_T"], 4)
                m0 = mask[:, L2 - P:].unsqueeze(1).to_broadcast([P, 2, P])
                m1 = mask[:, L2 - SEQ:].unsqueeze(1).to_broadcast([P, 4, SEQ])
                for b in range(2):
                    nc.vector.scalar_tensor_tensor(out=S1[:, 2 * b:2 * b + 2, 0:P],
                                                   in0=ps[:, 6 + b, 0:SEQ].rearrange("p (h k) -> p h k", h=2),
                                                   scalar=AD ** -0.5, in1=m0, op0=ALU.mult, op1=ALU.add).then_inc(s["s1_masked"], 1)
                nc.vector.scalar_tensor_tensor(out=S1[:, :, P:], in0=ps[:, 4:6, :].rearrange("p b (h k) -> p (b h) k", h=2),
                                               scalar=AD ** -0.5, in1=m1, op0=ALU.mult, op1=ALU.add).then_inc(s["s1_masked"], 1)
                dve.wait_ge(s["s1_masked"], 3 * g + 3)
                nc.vector.reduce_max(small[:, 0:4], S1[:, :, 0:P], AX_X)
                seq(nc.vector.reduce_max(small[:, 4:8], S1[:, :, P:], AX_X))
                nc.vector.tensor_scalar(small[:, 8:16], small[:, 0:8], -1.0, None, ALU.mult).then_inc(s["s1_biased"], 1)

            def group_probs(g):
                dve.wait_ge(s["exp1_done"], 8 * (g + 1))
                seq(nc.vector.reciprocal(small[:, 24:32], small[:, 16:24]))
                r0 = small[:, 24:28].unsqueeze(2).to_broadcast([P, 4, P])
                r1 = small[:, 28:32].unsqueeze(2).to_broadcast([P, 4, SEQ])
                nc.vector.tensor_tensor(S1[:, :, 0:P], S1[:, :, 0:P], r0, ALU.mult).then_inc(s["p1_ready"], 1)
                nc.vector.tensor_tensor(S1[:, :, P:], S1[:, :, P:], r1, ALU.mult).then_inc(s["p1_ready"], 1)

            def attn_lo(g):
                dve.wait_ge(s["attn_hi"], g + 1)
                nc.vector.tensor_tensor(a_lo[:, 2 * g:2 * g + 2, :].rearrange("p c t -> p (c t)"), ps[:, 4, :],
                                        a_hi[:, 2 * g:2 * g + 2, :].rearrange("p c t -> p (c t)").bitcast(F32),
                                        ALU.subtract).then_inc(s["attn_lo"], 1)

            def layer_norm():
                dve.wait_ge(s["gelu_done"], 2)
                for t in range(NT):
                    st, mv = small[:, 32 + 8 * t:38 + 8 * t], small[:, 48 + 4 * t:50 + 4 * t]
                    seq(nc.vector.bn_stats(st, vg[:, t, :]))
                    nc.vector.bn_aggr(mv, st).then_inc(s["ln_stats"], 1)

            def layer_norm_apply():
                dve.wait_ge(s["std_ready"], 4)
                nc.vector.reciprocal(small[:, 60:62], small[:, 58:60]).then_inc(s["rstd_ready"], 1)
                dve.wait_ge(s["rstd_ready"], 4)
                dve.wait_ge(s["gm_loaded"], 64)
                for t in range(NT):
                    nc.vector.tensor_scalar(vg[:, t, :], vg[:, t, :], small[:, 48 + 4 * t:49 + 4 * t], small[:, 60 + t:61 + t],
                                            ALU.subtract, ALU.mult).then_inc(s["vln_ready"], 1)
                dve.wait_ge(s["vln_ready"], 2)
                lg = ln_g.unsqueeze(1).to_broadcast([P, NT, GW])
                lb_ = ln_b.unsqueeze(1).to_broadcast([P, NT, GW])
                seq(nc.vector.tensor_tensor(vg, vg, lg, ALU.mult))
                nc.vector.tensor_tensor(vg, vg, lb_, ALU.add).then_inc(s["vln_ready"], 1)

            def spatial_gate():
                dve.wait_ge(s["mixed_mm"], 1)
                dve.wait_ge(s["gelu_done"], 3)
                t4 = tA.rearrange("p (c i t) -> p c i t", c=4, i=NT)
                mixed = ps[:, 5:7, :].rearrange("p b (c i t) -> p (b c) i t", c=2, i=NT)
                gb = gbias.unsqueeze(2).to_broadcast([P, 4, NT, P])
                seq(nc.vector.tensor_tensor(t4, mixed, gb, ALU.add))
                nc.vector.tensor_tensor(tA, tA, uT.rearrange("p c t -> p (c t)"), ALU.mult).then_inc(s["gm_ready"], 1)

            dve.wait_ge(s["tab_loaded"], 16)
            inverse(2)
            inverse(3, rcol[:, 1, 0:2], rcol[:, 0, 0:2])
            dve.wait_ge(s["rstd_ready"], 3)
            for i in range(26):
                dve.wait_ge(s["slab_used"], n + i + 1)
                if i < 4:
                    dst = (qT, kT)[i // 2][:, 2 * (i % 2):2 * (i % 2) + 2, :]
                    nc.vector.tensor_tensor(dst, acc(i), bc2, ALU.mult).then_inc(s["evac"], 1)
                elif i < 6 or i in (8, 9):
                    dst, j = (V1, i - 4) if i < 6 else (vg, i - 8)
                    for t in range(NT):
                        op = nc.vector.tensor_scalar(dst[:, t, 256 * j:256 * j + 256], ps[:, 2 * (i % 2) + t, 0:256],
                                                     rcol[:, 1, t:t + 1], None, ALU.mult)
                    op.then_inc(s["evac"], 1)
                elif i < 8:
                    nc.vector.tensor_tensor(uT[:, 2 * (i - 6):2 * (i - 5), :], acc(i), bc2, ALU.mult).then_inc(s["evac"], 1)
                elif i < 18:
                    nc.vector.tensor_tensor(gates[:, 2 * (i - 10):2 * (i - 9), :], acc(i), bc2, ALU.mult).then_inc(s["evac"], 1)
                elif i < 22:
                    q, b = (i - 18) // 2, i % 2
                    dve.wait_ge(s["gsig_done"], 16)
                    if q and not b:
                        dve.wait_ge(s["m_lo"], q)
                    y = ps[:, 2 * b:2 * b + 2, :].rearrange("p b t -> p (b t)")
                    gt = gates[:, 8 * b + 4 * q:8 * b + 4 * q + 4, :].rearrange("p c t -> p (c t)")
                    nc.vector.tensor_tensor((tA, tB)[b], y, gt, ALU.mult).then_inc(s["evac"], 1)
                    if b:
                        dve.wait_ge(s["evac"], i + 1)
                        nc.vector.tensor_tensor(tA, tA, tB, ALU.add).then_inc(s["merged1"], 1)
                        dve.wait_ge(s["merged1"], q + 1)
                        dve.wait_ge(s["m_hi"], q + 1)
                        nc.vector.tensor_tensor(x_lo[:, 4 * q:4 * q + 4, X0:], tA.rearrange("p (c t) -> p c t", c=4),
                                                x_hi[:, 4 * q:4 * q + 4, X0:].bitcast(F32), ALU.subtract).then_inc(s["m_lo"], 1)
                else:
                    residual(i - 22, 1.0, mixer_out(i - 22))
                    dve.wait_ge(s["h_new"], 8 + i - 22 + 1)
                    input_lo(i - 22, vec[:, VEC["ffn2_norm"]:], 16, (a_hi, a_lo))
                if i == 6:
                    group_probs(0)
                if i == 21:
                    split_lo(n + i + 2)
                if i != 20:
                    split_lo(n + i + 3)
                if i == 5:
                    group_scores(0)
                if i == 8:
                    attn_lo(0)
                if i == 9:
                    layer_norm()
                    group_scores(1)
                if i == 10:
                    group_probs(1)
                    layer_norm_apply()
                if i == 13:
                    attn_lo(1)
                if i == 15:
                    spatial_gate()
                    dve.wait_ge(s["gm_hi"], 1)
                    nc.vector.tensor_tensor(a_lo[:, 4:8, :], tA.rearrange("p (c t) -> p c t", c=4),
                                            a_hi[:, 4:8, :].bitcast(F32), ALU.subtract).then_inc(s["gm_lo"], 1)

        def mixer2_act(act, split_hi):
            n = N_MIX2
            bg = vec[:, VEC["b_gate_2"]:]

            def pair_hi(p):
                act.wait_ge(s["pv2_mm"], p + 1)
                nc.scalar.activation(a_hi[:, 2 * p:2 * p + 2, :].rearrange("p c t -> p (c t)"), ps[:, 7, :],
                                     ACT.Copy).then_inc(s["mla_hi"], 1)

            for i in range(43):
                if i < 2:
                    src, sqs, dst, g = ((cq, cq_sq, a_hi[:, 0:2, :], "q_a_norm_g_2"), (ckv, ckv_sq, kv_part(a_hi), "kv_a_norm_g_2"))[i]
                    act.wait_ge(s["evac"], E2 + i + 1)
                    nc.scalar.activation(sqs, src, ACT.Square).then_inc(s["csq_done"], 1)
                    for c in range(2):
                        k = VEC[g] + c
                        nc.scalar.activation(dst[:, c, :], src[:, c, :], ACT.Copy, scale=vec[:, k:k + 1]).then_inc(s["ac_hi"], 1)
                if 35 <= i < 39:
                    j = i - 35
                    act.wait_ge(s["merged2"], j + 1)
                    nc.scalar.activation(x_hi[:, 2 * j:2 * j + 2, X0:], pair(mT[:, j % 2, :]), ACT.Copy).then_inc(s["m2_hi"], 1)
                if i >= 39:
                    j = i - 39
                    act.wait_ge(s["slab_used"], n + i + 1)
                    for c in range(2):
                        k = VEC["mix_post_g_2"] + 2 * j + c
                        nc.scalar.activation(mg[:, 2 * j + c, :], mixer_out(j)[:, c, :], ACT.Copy,
                                             scale=vec[:, k:k + 1]).then_inc(s["mg_done"], 1)
                    nc.scalar.activation(sq[:, 2 * j:2 * j + 2, :], mixer_out(j), ACT.Square).then_inc(s["msq_done"], 1)
                if i < 42:
                    split_hi(n + i + 3)
                if i == 2:
                    act.wait_ge(s["cmean_mm"], 1)
                    for dst, src in ((r_q, ps[:, 4, 0:SEQ]), (r_kv, ps[:, 5, 0:L2]),
                                     (rcol[:, 0, 2:5], ps[:, 6, 0:6].rearrange("p (t two) -> p t two", two=2)[:, :, 0])):
                        nc.scalar.activation(dst, src, ACT.Sqrt, scale=float(D // QL), bias=eps[:]).then_inc(s["cstd_ready"], 1)
                if i in MLA_PV:
                    pair_hi(MLA_PV[i])
                if i in MLA_S:
                    p = MLA_S[i]
                    for t in range(NT):
                        act.wait_ge(s["s2_biased"], 2 * p + t + 1)
                        for hh in range(2):
                            v = S2[:, hh, K0:] if t else S2[:, hh, 0:K0]
                            k = 2 * t + hh
                            nc.scalar.activation(v, v, ACT.Exp, bias=small[:, 8 + k:9 + k],
                                                 accum_out=small[:, 16 + k:17 + k]).then_inc(s["exp2_done"], 1)
                if i in MLA_T:
                    p = MLA_T[i]
                    act.wait_ge(s["p2_T"], p + 1)
                    nc.scalar.copy(pT2, ps[:, 5:7, 0:384]).then_inc(s["p2_copied"], 1)
                    nc.scalar.copy(pT2m[0:META].rearrange("p c t -> p (c t)"), ps[0:META, 4, :]).then_inc(s["p2_copied"], 1)
                if i in (3, 4, 9, 10):
                    j = i - 3 if i < 5 else i - 7
                    act.wait_ge(s["evac"], E2 + i + 1)
                    nc.scalar.activation(q2[:, 2 * j:2 * j + 2, :], q2[:, 2 * j:2 * j + 2, :], ACT.Silu).then_inc(s["silu2_done"], 1)
                if 11 <= i < 15:
                    j = i - 11
                    act.wait_ge(s["evac"], E2 + i + 1)
                    nc.scalar.activation(f2[:, 2 * j:2 * j + 2, :], f2[:, 2 * j:2 * j + 2, :], ACT.Sigmoid).then_inc(s["fsig_done"], 1)
                if 27 <= i < 31:
                    j = i - 27
                    act.wait_ge(s["evac"], E2 + i + 1)
                    nc.scalar.activation(hgs[:, 2 * j:2 * j + 2, :], hgs[:, 2 * j:2 * j + 2, :], ACT.Silu).then_inc(s["silu2_done"], 1)
                if i == 18:
                    for c in range(DC):
                        act.wait_ge(s["evac"], E2 + 15 + c // 2 + 1)
                        nc.scalar.activation(gB[:, c, :], gB[:, c, :], ACT.Sigmoid, bias=bg[:, DC + c:DC + c + 1]).then_inc(s["gsigb_done"], 1)
                if i == 23:
                    act.wait_ge(s["vm_T"], 1)
                    nc.scalar.copy(V2m[0:META], ps[0:META, 0:2, :].rearrange("p b c -> p (b c)")).then_inc(s["vm_copied"], 1)
                    act.wait_ge(s["vT"], 1)
                    for t in range(NT):
                        nc.scalar.copy(V2[:, t, :], ps[:, 4 + 2 * t:6 + 2 * t, :].rearrange("p b c -> p (b c)")).then_inc(s["v_copied"], 1)
                if i == 27:
                    act.wait_ge(s["cross_mm"], 1)
                    nc.scalar.copy(AT[:, :, 1, :], ps[:, 4:6, :].rearrange("p b (h t) -> p (b h) t", h=4)).then_inc(s["cross_copied"], 1)
                    nc.scalar.copy(Am[0:META, 0:4, :].rearrange("p h t -> p (h t)"),
                                   ps[0:META, 6:8, :].rearrange("p b t -> p (b t)")).then_inc(s["cross_copied"], 1)
                if i == 28:
                    act.wait_ge(s["am_mm"], 1)
                    nc.scalar.copy(Am[0:META, 4:8, :].rearrange("p h t -> p (h t)"),
                                   ps[0:META, 4:6, :].rearrange("p b t -> p (b t)")).then_inc(s["am_copied"], 1)
                if i == 29:
                    for b in range(2):
                        act.wait_ge(s["o_ready"], b + 1)
                        nc.scalar.activation(k2[:, 4 * b:4 * b + 4, 0:SEQ], q2[:, 4 * b:4 * b + 4, :], ACT.Square).then_inc(s["osq_done"], 1)
                if i == 30:
                    act.wait_ge(s["osum_mm"], 1)
                    nc.scalar.activation(std[0:HH, 1, 0:SEQ], ps[0:HH, 4, 0:SEQ], ACT.Sqrt, bias=eps[0:HH]).then_inc(s["ostd_done"], 1)
                if i == 32:
                    for b in range(2):
                        act.wait_ge(s["o_final"], b + 1)
                        nc.scalar.activation(a_hi[:, 4 * b:4 * b + 4, :], q2[:, 4 * b:4 * b + 4, :], ACT.Copy).then_inc(s["o_hi"], 1)
                if i == 34:
                    for c in range(DC):
                        act.wait_ge(s["evac"], E2 + 31 + c // 2 + 1)
                        nc.scalar.activation(gA[:, c, :], gA[:, c, :], ACT.Sigmoid, bias=bg[:, c:c + 1]).then_inc(s["gsiga_done"], 1)

        def mixer2_dve(dve, split_lo, seq, inverse, input_lo):
            n = N_MIX2

            def bc(r, k):
                return r.unsqueeze(1).to_broadcast([P, k, r.shape[1]])

            def acc(i, width):
                k = 2 * (i % 2)
                return ps[:, k:k + 2, 0:width]

            def pair_scores(p):
                dve.wait_ge(s["s2_mm"], p + 1)
                if p:
                    dve.wait_ge(s["p2_T"], p)
                else:
                    dve.wait_ge(s["rope_done"], 2)
                parts = ((S2[:, :, 0:K0], ps[:, 5:7, 0:K0], bc(mask[:, P:], 2), K0), (S2[:, :, K0:], ps[:, 5:7, K0:K0 + L2], bc(mask, 2), L2))
                for t, (v, src, m, _) in enumerate(parts):
                    nc.vector.scalar_tensor_tensor(out=v, in0=src, scalar=MLA_SCALE, in1=m, op0=ALU.mult, op1=ALU.add).then_inc(s["s2_masked"], 1)
                    dve.wait_ge(s["s2_masked"], 2 * p + t + 1)
                    if p:
                        dve.wait_ge(s["exp2_done"], 4 * p)
                    seq(nc.vector.reduce_max(small[:, 2 * t:2 * t + 2], v, AX_X))
                    nc.vector.tensor_scalar(small[:, 8 + 2 * t:10 + 2 * t], small[:, 2 * t:2 * t + 2], -1.0, None, ALU.mult).then_inc(s["s2_biased"], 1)
                for t, (v, _, _, nk) in enumerate(parts):
                    dve.wait_ge(s["exp2_done"], 4 * p + 2 * t + 2)
                    r = small[:, 24 + 2 * t:26 + 2 * t]
                    seq(nc.vector.reciprocal(r, small[:, 16 + 2 * t:18 + 2 * t]))
                    nc.vector.tensor_tensor(v, v, r.unsqueeze(2).to_broadcast([P, 2, nk]), ALU.mult).then_inc(s["p2_ready"], 1)

            def pair_lo(p):
                dve.wait_ge(s["mla_hi"], p + 1)
                nc.vector.tensor_tensor(a_lo[:, 2 * p:2 * p + 2, :].rearrange("p c t -> p (c t)"), ps[:, 7, :],
                                        a_hi[:, 2 * p:2 * p + 2, :].rearrange("p c t -> p (c t)").bitcast(F32),
                                        ALU.subtract).then_inc(s["mla_lo"], 1)

            def forget(j):
                dve.wait_ge(s["fsig_done"], j + 1)
                for c in (2 * j, 2 * j + 1):
                    seq(nc.vector.tensor_scalar(f2[:, c, :], f2[:, c, :], lb[:, 5, c:c + 1], lb[:, 4, c:c + 1], ALU.mult, ALU.add))
                nc.vector.tensor_scalar(k2[:, 2 * j:2 * j + 2, :], f2[:, 2 * j:2 * j + 2, :], -1.0, 1.0, ALU.mult,
                                        ALU.add).then_inc(s["f_ready"], 1)

            def level(l):
                size = LEVELS[l]
                dve.wait_ge(s["lvl_mm"], l + 1)
                if size == 0:
                    nc.vector.tensor_tensor(q2, q2, f2[:, :, X0:], ALU.mult).then_inc(s["hg_ready"], 1)
                else:
                    nb = SEQ // (2 * size)
                    fx = f2[:, :, X0:].rearrange("p h (b two s) -> p h b two s", two=2, s=size)
                    qx = q2.rearrange("p h (b two s) -> p (h b) two s", two=2, s=size)
                    if size < META:
                        kk, ff = k2, f2
                    else:
                        kk, ff = k2[:, :, X0:], f2[:, :, X0:]
                    kx = kk.rearrange("p h (b two s) -> p h b two s", two=2, s=size)
                    fk = ff.rearrange("p h (b two s) -> p h b two s", two=2, s=size)
                    nk = kk.shape[2] // (2 * size)
                    o = kx[:, :, :, 0, :]
                    nc.vector.tensor_tensor(o, o, fk[:, :, :, 1, 0:1].to_broadcast([P, HH, nk, size]), ALU.mult).then_inc(s["dve_chain2"], 1)
                    qv = q2.rearrange("p h (b two s) -> p h b two s", two=2, s=size)[:, :, :, 1, :]
                    nc.vector.tensor_tensor(qv, qv, fx[:, :, :, 0, 0:1].to_broadcast([P, HH, nb, size]), ALU.mult).then_inc(s["dve_chain2"], 1)
                    dve.wait_ge(s["dve_chain2"], 3 * l - 1)
                    t0 = fk[:, :, :, 0, 0]
                    nc.vector.tensor_tensor(t0, t0, fk[:, :, :, 1, 0], ALU.mult).then_inc(s["dve_chain2"], 1)
                    dve.wait_ge(s["dve_chain2"], 3 * l)
                    if l == len(LEVELS) - 1:
                        tot = f2[:, :, X0:X0 + 1].to_broadcast([P, HH, META])
                        nc.vector.tensor_tensor(meta[:, 0], k2[:, :, 0:META], tot, ALU.mult).then_inc(s["hg_ready"], 1)
                    else:
                        nc.vector.tensor_copy(meta[:, 1, 0, 0:1], f2[:, 0, 0:1]).then_inc(s["hg_ready"], 1)
                if l == 0:
                    dve.wait_ge(s["at_zero"], 1)
                else:
                    dve.wait_ge(s["lvl_done"], 4 * l)
                for b in range(4):
                    for hd in range(2):
                        op = nc.vector.copy_predicated(AT[:, 2 * b + hd, 0:3:2, :], lvl[:, l, :].unsqueeze(1).to_broadcast([P, 2, P]),
                                                       ps[:, 4 + b, 256 * hd:256 * hd + 256].rearrange("p (t q) -> p t q", t=2))
                    op.then_inc(s["lvl_done"], 1)

            dve.wait_ge(s["mean_done"], 4)
            seq(nc.vector.tensor_scalar(std[:, 1, X0:], ps[:, 4, 0:SEQ], EPS, EPS * EPS, ALU.mult, ALU.add))
            seq(nc.vector.tensor_tensor(std[:, 1, X0:], std[:, 1, X0:], ps[:, 5, X0:L2], ALU.add))
            nc.vector.tensor_scalar(std[:, 1, 0:META], ps[:, 5, 0:META], EPS, None, ALU.add).then_inc(s["m2_summed"], 1)
            inverse(6, R2, std[:, 1, :])
            inverse(7)
            dve.wait_ge(s["rstd_ready"], 6)
            for i in range(43):
                if i < 39:
                    dve.wait_ge(s["slab_used"], n + i + 1)
                if i < 2:
                    dst, w = ((cq, SEQ), (ckv, L2))[i]
                    nc.vector.tensor_tensor(dst, acc(i, w), bc(R2[:, L2 - w:], 2), ALU.mult).then_inc(s["evac"], 1)
                    src, sqs, hi, lo, g, o = ((cq, cq_sq, a_hi[:, 0:2, :], a_lo[:, 0:2, :], "q_a_norm_g_2", ss[:, 0, X0:]),
                                              (ckv, ckv_sq, kv_part(a_hi), kv_part(a_lo), "kv_a_norm_g_2", ss[:, 1, :]))[i]
                    dve.wait_ge(s["csq_done"], i + 1)
                    nc.vector.tensor_tensor(o, sqs[:, 0, :], sqs[:, 1, :], ALU.add).then_inc(s["css_ready"], 1)
                    dve.wait_ge(s["evac"], E2 + i + 1)
                    for c in range(2):
                        dve.wait_ge(s["ac_hi"], 2 * i + c + 1)
                        k = VEC[g] + c
                        nc.vector.scalar_tensor_tensor(out=lo[:, c, :], in0=src[:, c, :], scalar=vec[:, k:k + 1],
                                                       in1=hi[:, c, :].bitcast(F32), op0=ALU.mult, op1=ALU.subtract).then_inc(s["ac_lo"], 1)
                elif i == 2:
                    nc.vector.tensor_tensor(k_pe, ps[:, 0, 0:L2], R2, ALU.mult).then_inc(s["evac"], 1)
                elif i in (3, 4, 9, 10):
                    j = i - 3 if i < 5 else i - 7
                    nc.vector.tensor_tensor(q2[:, 2 * j:2 * j + 2, :], acc(i, SEQ), bc(R2[:, X0:], 2), ALU.mult).then_inc(s["evac"], 1)
                elif i in (5, 6):
                    k, j = 2 * (i % 2), i - 5
                    dve.wait_ge(s["c_ready"], 3)
                    nc.vector.tensor_tensor(qn[:, 4 * j:4 * j + 4, :], ps[:, k:k + 2, :].rearrange("p b (h t) -> p (b h) t", h=2),
                                            bc(r_q, 4), ALU.mult)
                    nc.vector.tensor_tensor(q_pe[:, 2 * j:2 * j + 2, :], pair(ps[:, 12 - i, :]), bc(r_q, 2), ALU.mult).then_inc(s["evac"], 1)
                elif i in (7, 8):
                    k, j = 2 * (i % 2), i - 7
                    nc.vector.tensor_scalar(V2m[0:META, 512 * j:512 * j + 512], ps[0:META, 2 - k, :], rcol[0:META, 1, 2:3], None,
                                            ALU.mult).then_inc(s["kv_left"], 1)
                    nc.vector.tensor_tensor(kn[:, 4 * j + 2:4 * j + 4, :], ps[:, 4:6, 0:L2], bc(r_kv, 2), ALU.mult).then_inc(s["kv_left"], 1)
                    for t in range(NT):
                        nc.vector.tensor_scalar(V2[:, t, 512 * j:512 * j + 512], ps[:, 6 + t, :], rcol[:, 1, 3 + t:4 + t], None,
                                                ALU.mult).then_inc(s["kv_left"], 1)
                    nc.vector.tensor_tensor(kn[:, 4 * j:4 * j + 2, :], ps[:, k:k + 2, 0:L2], bc(r_kv, 2), ALU.mult).then_inc(s["evac"], 1)
                elif 11 <= i < 15:
                    j = i - 11
                    nc.vector.tensor_tensor(f2[:, 2 * j:2 * j + 2, :], acc(i, L2), bc(R2, 2), ALU.mult).then_inc(s["evac"], 1)
                elif 15 <= i < 19:
                    j = i - 15
                    nc.vector.tensor_tensor(gB[:, 2 * j:2 * j + 2, :], acc(i, SEQ), bc(R2[:, X0:], 2), ALU.mult).then_inc(s["evac"], 1)
                elif 19 <= i < 23:
                    j = i - 19
                    nc.vector.tensor_tensor(hiT[:, 2 * j:2 * j + 2, :], acc(i, L2), bc(R2, 2), ALU.mult).then_inc(s["evac"], 1)
                elif 23 <= i < 27:
                    j = i - 23
                    dve.wait_ge(s["gsigb_done"], 2 * j + 2)
                    nc.vector.tensor_tensor(yb[:, 2 * j:2 * j + 2, :], acc(i, SEQ), gB[:, 2 * j:2 * j + 2, :], ALU.mult).then_inc(s["evac"], 1)
                elif 27 <= i < 31:
                    j = i - 27
                    if j == 0:
                        dve.wait_ge(s["v_copied"], 2)
                    nc.vector.tensor_tensor(hgs[:, 2 * j:2 * j + 2, :], acc(i, SEQ), bc(R2[:, X0:], 2), ALU.mult).then_inc(s["evac"], 1)
                elif 31 <= i < 35:
                    j = i - 31
                    nc.vector.tensor_tensor(gA[:, 2 * j:2 * j + 2, :], acc(i, SEQ), bc(R2[:, X0:], 2), ALU.mult).then_inc(s["evac"], 1)
                elif 35 <= i < 39:
                    j = i - 35
                    dve.wait_ge(s["gsiga_done"], 2 * j + 2)
                    if j >= 2:
                        dve.wait_ge(s["m2_lo"], j - 1)
                    m = pair(mT[:, j % 2, :])
                    nc.vector.tensor_tensor(m, acc(i, SEQ), gA[:, 2 * j:2 * j + 2, :], ALU.mult).then_inc(s["evac"], 1)
                    dve.wait_ge(s["evac"], E2 + i + 1)
                    nc.vector.tensor_tensor(m, m, yb[:, 2 * j:2 * j + 2, :], ALU.add).then_inc(s["merged2"], 1)
                    dve.wait_ge(s["merged2"], j + 1)
                    dve.wait_ge(s["m2_hi"], j + 1)
                    nc.vector.tensor_tensor(x_lo[:, 2 * j:2 * j + 2, X0:], m, x_hi[:, 2 * j:2 * j + 2, X0:].bitcast(F32),
                                            ALU.subtract).then_inc(s["m2_lo"], 1)
                if i == 31:
                    dve.wait_ge(s["ostd_done"], 1)
                    nc.vector.reciprocal(std[0:HH, 0, 0:SEQ], std[0:HH, 1, 0:SEQ]).then_inc(s["orec_ready"], 1)
                if i == 3:
                    for k, (dst, src) in enumerate(((r_q, r_q), (r_kv, r_kv), (rcol[:, 1, 2:5], rcol[:, 0, 2:5]))):
                        dve.wait_ge(s["cstd_ready"], k + 1)
                        nc.vector.reciprocal(dst, src).then_inc(s["c_ready"], 1)
                if i == 38:
                    split_lo(n + i + 2)
                if i not in (37, 42):
                    split_lo(n + i + 3)
                if i in MLA_PV:
                    pair_lo(MLA_PV[i])
                if i in MLA_S:
                    pair_scores(MLA_S[i])
                if 12 <= i < 16:
                    forget(i - 12)
                if i in LSLOT:
                    level(LSLOT[i])
                if i == 29:
                    for b in range(2):
                        dve.wait_ge(s["o_mm"], 2 * b + 2)
                        nc.vector.tensor_copy(q2[:, 4 * b:4 * b + 4, :], ps[:, 4 + 2 * b:6 + 2 * b, :].rearrange("p b (h t) -> p (b h) t", h=2)).then_inc(s["o_ready"], 1)
                if i == 32:
                    dve.wait_ge(s["obc_mm"], 1)
                    dve.wait_ge(s["silu2_done"], 8)
                    k = VEC["hg_norm_g_2"]
                    for b in range(2):
                        o = q2[:, 4 * b:4 * b + 4, :]
                        seq(nc.vector.tensor_tensor(o, o, ps[:, 4 + 2 * b:6 + 2 * b, :].rearrange("p b (h t) -> p (b h) t", h=2), ALU.mult))
                        nc.vector.scalar_tensor_tensor(out=o, in0=o, scalar=vec[:, k:k + 1], in1=hgs[:, 4 * b:4 * b + 4, :],
                                                       op0=ALU.mult, op1=ALU.mult).then_inc(s["o_final"], 1)
                if i == 33:
                    for b in range(2):
                        dve.wait_ge(s["o_hi"], b + 1)
                        nc.vector.tensor_tensor(a_lo[:, 4 * b:4 * b + 4, :], q2[:, 4 * b:4 * b + 4, :],
                                                a_hi[:, 4 * b:4 * b + 4, :].bitcast(F32), ALU.subtract).then_inc(s["o_lo"], 1)
            inverse(8)
            dve.wait_ge(s["rstd_ready"], 8)
            dve.wait_ge(s["mg_done"], 8)
            dve.wait_ge(s["x2_done"], 2 * DC)
            for b in range(4):
                v, hb = mg[:, 2 * b:2 * b + 2, :], h[:, 2 * b:2 * b + 2, :]
                if b < 2:
                    nc.vector.tensor_tensor(v, v, bc(rstd[:, 0, X0:], 2), ALU.mult).then_inc(s["mg_scaled"], 1)
                    dve.wait_ge(s["mg_scaled"], b + 1)
                else:
                    dve.wait_ge(s["mg_scaled2"], b - 1)
                nc.vector.tensor_tensor(hb, hb, v, ALU.add).then_inc(s["h_new"], 1)
                if b:
                    input_lo(b - 1, vec[:, VEC["ffn_pre_g_2"]:], 32, (a_hi, a_lo))
            input_lo(3, vec[:, VEC["ffn_pre_g_2"]:], 32, (a_hi, a_lo))
            split_lo(n + 45)

        block = ctx.enter_context(nc.Block())

        @block.sync
        def _(sp):
            xs = a["x"][0].rearrange("(i p) d -> p i d", p=P)
            for half in range(2):
                sp.dma_start(x_tok[:, :, 512 * half:512 * half + 512], xs[:, :, 512 * half:512 * half + 512]).then_inc(s[f"x_loaded{half}"], 16)

            def load(n, src, dst=None, it=None):
                if n >= RING or it is not None:
                    sp.wait_ge(s["lo_ready"], up(max(n - RING + 1, 1), it))
                if dst is None:
                    dst = wview(stage, n, src.shape[1])
                sp.dma_start(dst, src).then_inc(slab_in[n % RING], 16)

            def cols(w, c0, width=256):
                return w.rearrange("(k p) c -> p k c", p=P)[:, :, bass.ds(c0, width)]

            def rows(w, r0):
                return w[bass.ds(r0, 256), :].rearrange("(k p) c -> p k c", p=P)

            def ffn_loads(f, wg, g0, wu, u0, wd):
                n = N_FFN[f]
                load(n, cols(wg, g0))
                load(n + 1, cols(wu, u0))
                if f == 0:
                    sp.dma_start(ws, a["gmlp_w_s"][0].rearrange("g i j -> i g j")).then_inc(s["ws_loaded"], 16)
                    sp.dma_start(meta_tok[0:META, :], a["meta_tokens_2"]).then_inc(s["meta_loaded"], 16)
                with sp.Fori(0, (PAIRS - 1) // 2) as it:
                    for b in range(2):
                        load(n + 2 + 3 * b, cols(wg, it * 512 + (g0 + 256 * (b + 1))), it=it)
                        load(n + 3 + 3 * b, cols(wu, it * 512 + (u0 + 256 * (b + 1))), it=it)
                        load(n + 4 + 3 * b, rows(wd, it * 512 + 256 * b), it=it)
                load(n + FFN_SLABS - 1, rows(wd, 256 * (PAIRS - 1)))

            ffn_loads(0, a["ffn1_w_gate"][0], 0, a["ffn1_w_up"][0], 0, a["ffn1_w_down"][0])
            n = N_MIX1
            for i in range(10):
                load(n + i, cols(a["w_in"][0], 256 * i))
            for i in range(8):
                load(n + 10 + i, cols(a["w_gate"][0], 256 * i))
            for i in range(2):
                load(n + 18 + 2 * i, cols(a["w_branch_attn"][0], 512 * i, 512))
                load(n + 19 + 2 * i, cols(a["w_branch_gmlp"][0], 512 * i, 512))
            for i in range(4):
                load(n + 22 + i, cols(a["w_out"][0], 256 * i))
            ffn_loads(1, a["ffn2_w_gate"][0], 0, a["ffn2_w_up"][0], 0, a["ffn2_w_down"][0])
            n, w = N_MIX2, a["w_in_2"][0]
            q0, f0, i0, g0, cq0, ckv0, kpe0 = 0, 1024, 2048, 3072, 4096, 4096 + QL, 4096 + 2 * QL
            ga0 = kpe0 + ROPE
            gb0 = ga0 + D
            load(n, cols(w, cq0))
            load(n + 1, cols(w, ckv0))
            load(n + 2, cols(w, kpe0, ROPE), wview(stage, n + 2, DC, ROPE))
            for i in range(2):
                load(n + 3 + i, cols(w, q0 + 256 * i))
            for i in range(2):
                load(n + 5 + i, cols(a["w_q_b_2"][0], 768 * i, 768), wview(stage, n + 5 + i, 2, 768))
            for i in range(2):
                load(n + 7 + i, cols(a["w_kv_b_2"][0], 1024 * i, 1024))
            for i in range(2, 4):
                load(n + 7 + i, cols(w, q0 + 256 * i))
            for j, src, c0 in ((11, w, f0), (15, w, gb0), (19, w, i0), (23, a["w_mla_o_2"][0], 0), (27, w, g0),
                               (31, w, ga0), (35, a["w_hg_o_2"][0], 0), (39, a["w_out_2"][0], 0)):
                for i in range(4):
                    load(n + j + i, cols(src, c0 + 256 * i))
            ffn_loads(2, a["w_ffn_in_2"][0], 0, a["w_ffn_in_2"][0], FF, a["w_ffn_out_2"][0])
            for i in range(NT):
                sp.wait_ge(s["out_copied"], 2 * (i + 1))
                sp.dma_start(out[0, P * i:P * (i + 1), :], out_tok[:, i, :]).then_inc(s["store_done"], 16)
            sp.wait_ge(s["store_done"], 16 * NT)

        @block.gpsimd
        def _(pool):
            chain = [0]

            def seq(ins):
                chain[0] += 1
                ins.then_inc(s["pool_chain"], 1)
                pool.wait_ge(s["pool_chain"], chain[0])

            def sum_squares(dst, src, done, base):
                pool.wait_ge(s[done], base + 1)
                seq(nc.gpsimd.tensor_tensor(dst, src[:, 0, :], src[:, 1, :], ALU.add))
                for c in range(2, DC):
                    if c % 2 == 0:
                        pool.wait_ge(s[done], base + c // 2 + 1)
                    last = nc.gpsimd.tensor_tensor(dst, dst, src[:, c, :], ALU.add)
                    if c < DC - 1:
                        seq(last)
                last.then_inc(s["ss_ready"], 1)

            ssx = ss[:, 0, X0:]
            nc.gpsimd.memset(eps[:], EPS)
            seq(nc.gpsimd.memset(pick[:], 0.0))
            nc.gpsimd.memset(pick[:, HH - 1:HH], 1.0 / P)
            nc.gpsimd.memset(ones[:], 1.0 / D).then_inc(s["ones_ready"], 1)
            pool.wait_ge(s["ws_loaded"], 16)
            nc.gpsimd.affine_select(out=ws, in_=ws, compare_op=ALU.is_ge, fill=0.0, base=0,
                                    pattern=[[0, GG], [-1, GC]], channel_multiplier=1).then_inc(s["ws_masked"], 1)
            sum_squares(ssx, sq, "sq_done", 0)
            nc.gpsimd.dma_start(tab[:], tab_d).then_inc(s["tab_loaded"], 16)
            pool.wait_ge(s["ws_T"], 1)
            nc.gpsimd.dma_start(ln_g, a["gmlp_ln_g"].partition_broadcast(P)).then_inc(s["gm_loaded"], 16)
            nc.gpsimd.dma_start(ln_b, a["gmlp_ln_b"].partition_broadcast(P)).then_inc(s["gm_loaded"], 16)
            for half in range(2):
                src = a["gmlp_b_s"].rearrange("l (c two) i -> l two c i", two=2)[:, half]
                nc.gpsimd.dma_start(gbias[64 * half:64 * half + 64], src.partition_broadcast(64)).then_inc(s["gm_loaded"], 16)
            pool.wait_ge(s["mean_done"], 1)
            sum_squares(ssx, sq, "sq_done", 4)
            pool.wait_ge(s["mean_done"], 2)
            sum_squares(ssx, sq, "sq_done", 8)
            pool.wait_ge(s["mean_done"], 3)
            sum_squares(ssx, sq, "sq_done", 12)
            pool.wait_ge(s["rstd_ready"], 7)
            pool.wait_ge(s["xlo_done"], 32)
            fg = vec[:, VEC["final_norm"]:]
            for c in range(DC):
                nc.gpsimd.tensor_scalar(h[:, c, :], h[:, c, :], fg[:, c:c + 1], None, ALU.mult).then_inc(s["x2_done"], 1)
            pool.wait_ge(s["x2_done"], DC)
            for c in range(DC):
                nc.gpsimd.tensor_tensor(h[:, c, :], h[:, c, :], rstd[:, 0, X0:], ALU.mult).then_inc(s["x2_done"], 1)
            pool.wait_ge(s["tab_loaded"], 16)
            pool.wait_ge(s["x2_done"], 2 * DC)
            cos_x = tab[:, T_COS + X0:T_COS + L2].unsqueeze(1).to_broadcast([P, 4, SEQ])
            sin_x = tab[:, T_SIN + X0:T_SIN + L2].unsqueeze(1).to_broadcast([P, 4, SEQ])
            for v, sw, cos, sin, count in ((k_pe, k_sw, tab[:, T_COS:T_COS + L2], tab[:, T_SIN:T_SIN + L2], 3),
                                           (q_pe, q_sw, cos_x, sin_x, 7)):
                pool.wait_ge(s["evac"], E2 + count)
                for d, r in ((0, 32), (32, 0), (64, 96), (96, 64)):
                    seq(nc.gpsimd.tensor_copy(sw[d:d + 32], v[r:r + 32]))
                seq(nc.gpsimd.tensor_tensor(v, v, cos, ALU.mult))
                seq(nc.gpsimd.tensor_tensor(sw, sw, sin, ALU.mult))
                nc.gpsimd.tensor_tensor(v, v, sw, ALU.add).then_inc(s["rope_done"], 1)
                pool.wait_ge(s["rope_done"], 1 if v is k_pe else 2)
            pool.wait_ge(s["mla_lo"], 4)
            nc.gpsimd.memset(AT, 0.0).then_inc(s["at_zero"], 1)
            sum_squares(ssx, sq, "msq_done", 0)
            pool.wait_ge(s["rstd_ready"], 8)
            pool.wait_ge(s["mg_done"], 8)
            for b in (2, 3):
                v = mg[:, 2 * b:2 * b + 2, :]
                nc.gpsimd.tensor_tensor(v, v, rstd[:, 0, X0:].unsqueeze(1).to_broadcast([P, 2, SEQ]), ALU.mult).then_inc(s["mg_scaled2"], 1)
            sum_squares(ssx, sq, "sq_done", 16)
            pool.wait_ge(s["mean_done"], 6)
            sum_squares(ssx, sq, "ysq_done", 0)

        @block.scalar
        def _(act):
            warmed = [0]

            def load_table(func):
                nc.scalar.activation(warm[:, warmed[0]:warmed[0] + 1], ones[:, 0:1], func)
                warmed[0] += 1

            act.dma_start(ident[:], id_d).then_inc(s["id_loaded"], 16)
            act.dma_start(vrows[0:NVEC, :], vec_d).then_inc(s["vec_loaded"], 16)

            def split_hi(n, it=None):
                if it is None and n >= N_ALL:
                    return
                wait_slab(act, n, it)
                if n >= RING:
                    act.wait_ge(s["slab_used"], up(n - RING + 1, it))
                if it is None and n in (N_MIX2 + 5, N_MIX2 + 6):
                    for dst, src in zip(q_parts(w_hi, n), q_parts(stage, n)):
                        for o, i in zip(dst, src):
                            last = nc.scalar.activation(o, i, ACT.Copy)
                    last.then_inc(s["hi_ready"], 1)
                    return
                if it is None and n == N_MIX2 + 2:
                    o = w_hi[:, n % RING, 0:D].rearrange("p (k two c) -> p k two c", k=DC, two=2)
                    i = wview(stage, n, DC, ROPE).unsqueeze(2).to_broadcast([P, DC, 2, ROPE])
                else:
                    o, i = w_hi[:, n % RING, 0:slab_words(n)], stage[:, n % RING, 0:slab_words(n)]
                nc.scalar.activation(o, i, ACT.Copy).then_inc(s["hi_ready"], 1)

            def input_hi(dst, g, base, bs=range(4)):
                for b in bs:
                    act.wait_ge(s["h_new"], base + b + 1)
                    for c in (2 * b, 2 * b + 1):
                        nc.scalar.activation(dst[:, c, :], h[:, c, :], ACT.Copy, scale=g[:, c:c + 1]).then_inc(s["xhi_done"], 1)
                    nc.scalar.activation(sq[:, 2 * b:2 * b + 2, :], h[:, 2 * b:2 * b + 2, :], ACT.Square).then_inc(s["sq_done"], 1)

            def root(mean, src, dst=std[:, 0, X0:]):
                load_table(ACT.Sqrt)
                act.wait_ge(s["mean_done"], mean)
                nc.scalar.activation(dst, src, ACT.Sqrt, bias=eps[:]).then_inc(s["std_ready"], 1)

            def ffn(f, lookahead=True):
                n, J0 = N_FFN[f], PAIRS * f

                def gate(J, m, it=None):
                    act.wait_ge(s["gate_scaled"], up(J + 1, it, 2))
                    nc.scalar.activation(ga_a, ga_s, ACT.Silu).then_inc(s["silu_done"], 1)
                    split_hi(m + 3, it)

                def hidden(J, m, it=None, pf=True):
                    act.wait_ge(s["hidden"], up(J + 1, it, 2))
                    if not (f == 0 and J < 2 and it is None):
                        act.wait_ge(s["slab_used"], up(m - 1, it))
                    nc.scalar.activation(hidden_part(f, 0, J), pair(hid), ACT.Copy).then_inc(s["hid_hi_done"], 1)
                    if pf:
                        split_hi(m + 3, it)

                gate(J0, n)
                hidden(J0, n + 1)
                loops = (PAIRS - 1) // 2 if lookahead else (PAIRS - 3) // 2
                with act.Fori(0, loops) as it:
                    for b in range(2):
                        gate(J0 + 1 + b, n + 2 + 3 * b, it)
                        hidden(J0 + 1 + b, n + 3 + 3 * b, it)
                        split_hi(n + 4 + 3 * b + 3, it)
                if not lookahead:
                    last = n + FFN_SLABS - 1
                    for j in (PAIRS - 2, PAIRS - 1):
                        m = n + 3 * j - 1
                        gate(J0 + j, m)
                        hidden(J0 + j, m + 1, pf=m + 4 <= last)
                        if m + 5 <= last:
                            split_hi(m + 5)

            act.wait_ge(s["ones_ready"], 1)
            load_table(ACT.Square)
            act.wait_ge(s["vec_ready"], 1)
            for b in range(4):
                input_hi(ffn_input(0)[0], vec[:, VEC["ffn1_norm"]:], 0, [b])
                if b % 2:
                    split_hi(b // 2)
            root(1, ps[:, 3, 0:SEQ])
            split_hi(2)
            act.wait_ge(s["lb_ready"], 1)
            nc.scalar.activation(lb[:, 1:3, :], lb[:, 1:3, :], ACT.Exp).then_inc(s["lb_exp"], 1)
            load_table(ACT.Silu)
            ffn(0)
            input_hi(x_hi[:, :, X0:], vec[:, VEC["mix_norm"]:], 4)
            split_hi(N_MIX1 + 2)
            root(2, ps[:, 4, 0:SEQ])
            root(2, token_means(), rcol[:, 0, 0:2])
            mixer1_act(act, split_hi, input_hi)
            root(3, ps[:, 3 - PAIRS % 2, 0:SEQ])
            load_table(ACT.Silu)
            ffn(1)
            fg = vec[:, VEC["final_norm"]:]
            for b in range(4):
                input_hi(x_hi[:, :, X0:], gfp, 12, [b])
                for c in (2 * b, 2 * b + 1):
                    op = nc.scalar.activation(sq2[:, c, :], h[:, c, :], ACT.Square, scale=fg[:, c:c + 1])
                op.then_inc(s["sq2_done"], 1)
            split_hi(N_MIX2 + 2)
            load_table(ACT.Sqrt)
            act.wait_ge(s["m2_summed"], 1)
            nc.scalar.activation(std[:, 1, :], std[:, 1, :], ACT.Sqrt).then_inc(s["std_ready"], 1)
            root(4, ps[:, 4, 0:SEQ])
            mixer2_act(act, split_hi)
            root(5, ps[:, 0, 0:SEQ])
            input_hi(a_hi, vec[:, VEC["ffn_pre_g_2"]:], 16)
            split_hi(N_FFN[2] + 2)
            root(6, ps[:, 3, 0:SEQ])
            load_table(ACT.Silu)
            ffn(2, lookahead=False)
            for i in range(NT):
                act.wait_ge(s["hT_T"], i + 1)
                nc.scalar.copy(out_tok[:, i, :], ps[:, 2 * i:2 * i + 2, :].rearrange("p b c -> p (b c)")).then_inc(s["hT_copied"], 1)
            pg = vec[:, VEC["ffn_post_g_2"]:]
            for b in range(4):
                if b < 3:
                    act.wait_ge(s["y_bank"], 6 + b + 1)
                else:
                    act.wait_ge(s["slab_used"], N_ALL)
                for c in range(2):
                    nc.scalar.activation(yg[:, 2 * b + c, :], ps[:, 4 + b, SEQ * c:SEQ * c + SEQ], ACT.Copy,
                                         scale=pg[:, 2 * b + c:2 * b + c + 1]).then_inc(s["yg_done"], 1)
                nc.scalar.activation(sq[:, 2 * b:2 * b + 2, :].rearrange("p c t -> p (c t)"), ps[:, 4 + b, :],
                                     ACT.Square).then_inc(s["ysq_done"], 1)
            root(7, token_means(), rcol[:, 0, 0:2])

        @block.vector
        def _(dve):
            chain = [0]

            def seq(ins):
                chain[0] += 1
                ins.then_inc(s["dve_chain"], 1)
                dve.wait_ge(s["dve_chain"], chain[0])

            def split_lo(n, it=None):
                if it is None and n >= N_ALL:
                    return
                dve.wait_ge(s["hi_ready"], up(n + 1, it))
                if it is None and n in (N_MIX2 + 5, N_MIX2 + 6):
                    for los, his, src in zip(q_parts(w_lo, n), q_parts(w_hi, n), q_parts(stage, n)):
                        for o, b, i in zip(los, his, src):
                            last = nc.vector.tensor_tensor(o, i, b.bitcast(F32), ALU.subtract)
                    last.then_inc(s["lo_ready"], 1)
                    return
                if it is None and n == N_MIX2 + 2:
                    o, b = (v[:, n % RING, 0:D].rearrange("p (k two c) -> p k two c", k=DC, two=2) for v in (w_lo, w_hi))
                    i = wview(stage, n, DC, ROPE).unsqueeze(2).to_broadcast([P, DC, 2, ROPE])
                else:
                    o, b, i = (v[:, n % RING, 0:slab_words(n)] for v in (w_lo, w_hi, stage))
                nc.vector.tensor_tensor(o, i, b.bitcast(F32), ALU.subtract).then_inc(s["lo_ready"], 1)

            def input_lo(b, g, base, dst=(x_hi[:, :, X0:], x_lo[:, :, X0:])):
                for c in (2 * b, 2 * b + 1):
                    dve.wait_ge(s["xhi_done"], base + c + 1)
                    nc.vector.scalar_tensor_tensor(out=dst[1][:, c, :], in0=h[:, c, :], scalar=g[:, c:c + 1],
                                                   in1=dst[0][:, c, :].bitcast(F32), op0=ALU.mult,
                                                   op1=ALU.subtract).then_inc(s["xlo_done"], 1)

            def zero_y():
                nc.vector.memset(ps[:, 4:8, :], 0.0).then_inc(s["y_zeroed"], 1)

            def inverse(k, dst=rstd[:, 0, X0:], src=std[:, 0, X0:]):
                dve.wait_ge(s["std_ready"], k)
                nc.vector.reciprocal(dst, src).then_inc(s["rstd_ready"], 1)

            bc2 = rstd[:, 0, X0:].unsqueeze(1).to_broadcast([P, 2, SEQ])

            def ffn(f, rstd_count, lookahead=True):
                n, J0 = N_FFN[f], PAIRS * f

                def gate(J, m, it=None, first=False):
                    dve.wait_ge(s["slab_used"], up(m + 1, it))
                    nc.vector.tensor_tensor(pair(ga_s), ps[:, 0:2, 0:SEQ] if first else pair(ps[:, J % 2, :]), bc2,
                                            ALU.mult).then_inc(s["gate_scaled"], 1)
                    split_lo(m + 3, it)

                def hidden(J, m, it=None, pf=True):
                    dve.wait_ge(s["slab_used"], up(m + 1, it))
                    nc.vector.tensor_tensor(up_s.rearrange("p (c t) -> p c t", c=2), ps[:, 2 + J % 2, :].rearrange("p (c t) -> p c t", c=2), bc2,
                                            ALU.mult).then_inc(s["up_scaled"], 1)
                    dve.wait_ge(s["up_scaled"], up(J + 1, it, 2))
                    dve.wait_ge(s["silu_done"], up(J + 1, it, 2))
                    nc.vector.tensor_tensor(hid, ga_a, up_s, ALU.mult).then_inc(s["hidden"], 1)
                    dve.wait_ge(s["hidden"], up(J + 1, it, 2))
                    dve.wait_ge(s["hid_hi_done"], up(J + 1, it, 2))
                    nc.vector.tensor_tensor(hidden_part(f, 1, J), pair(hid), hidden_part(f, 0, J).bitcast(F32),
                                            ALU.subtract).then_inc(s["hid_lo_done"], 1)
                    if pf:
                        split_lo(m + 3, it)

                inverse(rstd_count)
                dve.wait_ge(s["rstd_ready"], rstd_count)
                gate(J0, n, first=True)
                if f == 0:
                    spatial_weights_and_meta()
                zero_y()
                hidden(J0, n + 1)
                loops = (PAIRS - 1) // 2 if lookahead else (PAIRS - 3) // 2
                with dve.Fori(0, loops) as it:
                    for b in range(2):
                        gate(J0 + 1 + b, n + 2 + 3 * b, it)
                        hidden(J0 + 1 + b, n + 3 + 3 * b, it)
                        split_lo(n + 4 + 3 * b + 3, it)
                if not lookahead:
                    last = n + FFN_SLABS - 1
                    for j in (PAIRS - 2, PAIRS - 1):
                        m = n + 3 * j - 1
                        gate(J0 + j, m)
                        hidden(J0 + j, m + 1, pf=m + 4 <= last)
                        if m + 5 <= last:
                            split_lo(m + 5)

            def residual(b, scale, y=None):
                hb = h[:, 2 * b:2 * b + 2, :]
                nc.vector.scalar_tensor_tensor(out=hb, in0=pair(ps[:, 4 + b, :]) if y is None else y, scalar=scale, in1=hb,
                                               op0=ALU.mult, op1=ALU.add).then_inc(s["h_new"], 1)

            def ffn_residual(f, g, base, scale=0.5):
                n = N_FFN[f]
                for b in range(4):
                    if b < 3:
                        dve.wait_ge(s["y_bank"], 3 * f + b + 1)
                    else:
                        dve.wait_ge(s["slab_used"], n + FFN_SLABS)
                    residual(b, scale)
                    if g is not None:
                        dve.wait_ge(s["h_new"], base // 2 + b + 1)
                        input_lo(b, g, base)

            def spatial_weights_and_meta():
                dve.wait_ge(s["lb_exp"], 1)
                seq(nc.vector.tensor_tensor(lb[:, 3, :], lb[:, 1, :], lb[:, 2, :], ALU.add))
                seq(nc.vector.reciprocal(lb[:, 3, :], lb[:, 3, :]))
                seq(nc.vector.tensor_tensor(lb[:, 4, :], lb[:, 1, :], lb[:, 3, :], ALU.mult))
                seq(nc.vector.tensor_scalar(lb[:, 5, :], lb[:, 4, :], -1.0, 1.0, ALU.mult, ALU.add))
                dve.wait_ge(s["ws_T"], 1)
                nc.vector.tensor_copy(wsT.rearrange("p g i -> p (g i)"), ps[:, 4:6, :].rearrange("p b i -> p (b i)")).then_inc(s["ws_T_copied"], 1)
                dve.wait_ge(s["meta_T"], 1)
                gp = vec[:, VEC["mix_pre_g_2"]:VEC["mix_pre_g_2"] + DC].unsqueeze(2).to_broadcast([P, DC, META])
                seq(nc.vector.tensor_copy(meta[:, 0], ps[:, 6, 0:P].rearrange("p (c t) -> p c t", c=DC)))
                seq(nc.vector.tensor_tensor(meta[:, 1], meta[:, 0], meta[:, 0], ALU.mult))
                nc.vector.tensor_reduce(ss[:, 1, 0:META], meta[:, 1].rearrange("p c t -> p t c"), AX_X, ALU.add)
                seq(nc.vector.tensor_tensor(meta[:, 0], meta[:, 0], gp, ALU.mult))
                nc.vector.tensor_copy(x_hi[:, :, 0:META], meta[:, 0]).then_inc(s["meta_hi"], 1)
                dve.wait_ge(s["meta_hi"], 1)
                nc.vector.tensor_tensor(x_lo[:, :, 0:META], meta[:, 0], x_hi[:, :, 0:META].bitcast(F32),
                                        ALU.subtract).then_inc(s["meta_lo"], 1)

            dve.wait_ge(s["vec_T"], 1)
            nc.vector.tensor_copy(vec[:], ps[:, 0, 0:NVEC]).then_inc(s["vec_ready"], 1)
            dve.wait_ge(s["vec_ready"], 1)
            for b in range(4):
                dve.wait_ge(s["x_T"], b + 1)
                nc.vector.tensor_copy(h[:, 2 * b:2 * b + 2, :].rearrange("p c t -> p (c t)"), ps[:, 4 + b, :]).then_inc(s["h_new"], 1)
                dve.wait_ge(s["h_new"], b + 1)
                input_lo(b, vec[:, VEC["ffn1_norm"]:], 0)
                if b % 2:
                    split_lo(b // 2)
            l0 = vec[:, VEC["lb_logits_2"]:VEC["lb_logits_2"] + DC]
            l1 = vec[:, VEC["lb_logits_2"] + DC:VEC["lb_logits_2"] + 2 * DC]
            seq(nc.vector.tensor_tensor(lb[:, 0, :], l0, l1, ALU.max))
            seq(nc.vector.tensor_tensor(lb[:, 1, :], l0, lb[:, 0, :], ALU.subtract))
            nc.vector.tensor_tensor(lb[:, 2, :], l1, lb[:, 0, :], ALU.subtract).then_inc(s["lb_ready"], 1)
            nc.vector.tensor_tensor(gfp[:], vec[:, VEC["final_norm"]:VEC["final_norm"] + DC],
                                    vec[:, VEC["mix_pre_g_2"]:VEC["mix_pre_g_2"] + DC], ALU.mult).then_inc(s["gfp_ready"], 1)
            split_lo(2)
            ffn(0, 1)
            ffn_residual(0, vec[:, VEC["mix_norm"]:], 8)
            split_lo(N_MIX1 + 2)
            mixer1_dve(dve, split_lo, seq, input_lo, residual, inverse)
            ffn(1, 5)
            ffn_residual(1, gfp, 24)
            dve.wait_ge(s["sq2_done"], 4)
            nc.vector.tensor_reduce(ss[:, 1, X0:], sq2.rearrange("p c t -> p t c"), AX_X, ALU.add).then_inc(s["ss2_ready"], 1)
            split_lo(N_MIX2 + 2)
            mixer2_dve(dve, split_lo, seq, inverse, input_lo)
            ffn(2, 9, lookahead=False)
            inverse(10, rcol[:, 1, 0:2], rcol[:, 0, 0:2])
            dve.wait_ge(s["rstd_ready"], 10)
            for i in range(NT):
                for b in range(2):
                    dve.wait_ge(s["yg_T"], 1)
                    o = out_tok[:, i, 512 * b:512 * b + 512]
                    nc.vector.scalar_tensor_tensor(out=o, in0=ps[:, 2 * i + b, :], scalar=rcol[:, 1, i:i + 1], in1=o,
                                                   op0=ALU.mult, op1=ALU.add).then_inc(s["out_copied"], 1)

        @block.tensor
        def _(pe):
            def products(o, wh, wl, xh, xl, start, stop, skip=False):
                nc.tensor.matmul(o, wl, xh, start=start, stop=False, skip_group_check=skip)
                nc.tensor.matmul(o, wh, xl, start=False, stop=False, skip_group_check=skip)
                return nc.tensor.matmul(o, wh, xh, start=False, stop=stop, skip_group_check=skip)

            def slab_ready(n, it=None):
                pe.wait_ge(s["lo_ready"], up(n + 1, it))

            def feature_slab(n, outs, src=(x_hi[:, :, X0:], x_lo[:, :, X0:]), it=None, parts_base=None, parts="xlo_done", parts_step=1):
                slab_ready(n, it)
                wh, wl = wview(w_hi, n, DC), wview(w_lo, n, DC)
                if parts_base is not None:
                    for k in range(DC):
                        pe.wait_ge(s[parts], parts_base + k // parts_step + 1)
                        for c in range(2):
                            last = products(outs[c], wh[:, k, P * c:P * c + P], wl[:, k, P * c:P * c + P],
                                            src[0][:, k, :], src[1][:, k, :], k == 0, k == DC - 1, skip=True)
                    last.then_inc(s["slab_used"], 1)
                    return
                for c in range(2):
                    for k in range(DC):
                        last = products(outs[c], wh[:, k, P * c:P * c + P], wl[:, k, P * c:P * c + P],
                                        src[0][:, k, :], src[1][:, k, :], k == 0, k == DC - 1)
                last.then_inc(s["slab_used"], 1)

            def down_slab(f, n, J, last_one=False, it=None):
                slab_ready(n, it)
                pe.wait_ge(s["hid_lo_done"], up(J + 1, it, 2))
                wh, wl = wview(w_hi, n, 2), wview(w_lo, n, 2)
                hh, hl = hidden_part(f, 0, J), hidden_part(f, 1, J)
                order = [(k, m) for m in range(DC) for k in range(2)] if last_one else [(k, m) for k in range(2) for m in range(DC)]
                for k, m in order:
                    o = ps[:, 4 + m // 2, SEQ * (m % 2):SEQ * (m % 2) + SEQ]
                    last = products(o, wh[:, k, P * m:P * m + P], wl[:, k, P * m:P * m + P], hh[:, k, :], hl[:, k, :],
                                    False, last_one and k == 1, skip=True)
                    if last_one and k == 1 and m in (1, 3, 5):
                        last.then_inc(s["y_bank"], 1)
                last.then_inc(s["slab_used"], 1)

            def halves(bank):
                return [ps[:, bank, 0:SEQ], ps[:, bank, SEQ:2 * SEQ]]

            def mean_mm(k, o, width=SEQ):
                pe.wait_ge(s["ss_ready"], k)
                return nc.tensor.matmul(o, ones[:], ss[:, 0, X0:], start=True, stop=True)

            def turn(src, done):
                for i in range(NT):
                    for c in range(DC):
                        last = nc.tensor.transpose(ps[:, 2 * i + c // 4, P * (c % 4):P * (c % 4) + P], src[:, c, P * i:P * i + P], ident[:])
                    last.then_inc(s[done], 1)

            def spatial_weights_and_meta():
                pe.wait_ge(s["ws_masked"], 1)
                for g in range(GG):
                    last = nc.tensor.transpose(ps[:, 4 + g // 4, P * (g % 4):P * (g % 4) + P], ws[:, g, :], ident[:])
                last.then_inc(s["ws_T"], 1)
                pe.wait_ge(s["meta_loaded"], 16)
                for c in range(DC):
                    last = nc.tensor.transpose(ps[:, 6, META * c:META * c + META], meta_tok[0:META, P * c:P * c + P], ident[0:META, 0:META])
                last.then_inc(s["meta_T"], 1)

            def ffn(f, base, norm, rec):
                n, J0 = N_FFN[f], PAIRS * f

                def gate(J, m, it=None, first=False):
                    if J >= 1:
                        pe.wait_ge(s["gate_scaled"], up(max(J - 1, 1), it, 2))
                    outs = [ps[:, 0, 0:SEQ], ps[:, 1, 0:SEQ]] if first else halves(J % 2)
                    feature_slab(m, outs, ffn_input(f), it=it, parts_base=base if first else None)

                def upward(J, m, it=None):
                    if J >= 1:
                        pe.wait_ge(s["up_scaled"], up(max(J - 1, 1), it, 2))
                    feature_slab(m, halves(2 + J % 2), ffn_input(f), it=it)

                gate(J0, n, first=True)
                mean_mm(norm, ps[:, 3 - J0 % 2, 0:SEQ]).then_inc(s["mean_done"], 1)
                if f == 0:
                    spatial_weights_and_meta()
                upward(J0, n + 1)
                pe.wait_ge(s["std_ready"], rec)
                pe.wait_ge(s["gate_scaled"], J0 + 1)
                with pe.Fori(0, (PAIRS - 1) // 2) as it:
                    for b in range(2):
                        J = J0 + 1 + b
                        gate(J, n + 2 + 3 * b, it)
                        upward(J, n + 3 + 3 * b, it)
                        pe.wait_ge(s["y_zeroed"], f + 1)
                        down_slab(f, n + 4 + 3 * b, J - 1, it=it)
                if f == 2:
                    pe.wait_ge(s["hid_lo_done"], 3 * PAIRS)
                    turn(h, "hT_T")
                down_slab(f, n + FFN_SLABS - 1, J0 + PAIRS - 1, last_one=True)

            def token_slab(n, outs):
                slab_ready(n)
                wh, wl = wview(w_hi, n, DC), wview(w_lo, n, DC)
                for t in range(NT):
                    t0 = X0 + P * t
                    for k in range(DC):
                        last = products(outs[t], x_hi[:, k, t0:t0 + P], x_lo[:, k, t0:t0 + P], wh[:, k, :], wl[:, k, :],
                                        k == 0, k == DC - 1)
                last.then_inc(s["slab_used"], 1)

            def branch_slab(n, c0, banks, nk=4, parts=None):
                slab_ready(n)
                wh, wl = wview(w_hi, n, nk), wview(w_lo, n, nk)
                for c in range(4):
                    o = ps[:, banks + c // 2, SEQ * (c % 2):SEQ * (c % 2) + SEQ]
                    for k in range(nk):
                        last = products(o, wh[:, k, P * c:P * c + P], wl[:, k, P * c:P * c + P],
                                        a_hi[:, c0 + k, :], a_lo[:, c0 + k, :], k == 0, k == nk - 1)
                last.then_inc(s["slab_used"], 1)

            def mixer1():
                n = N_MIX1
                order = (0, 2, 1, 3)

                def scores(g):
                    pe.wait_ge(s["evac"], 4)
                    for o, j in enumerate(order):
                        c, r = 2 * g + j // 2, AD * (j % 2)
                        nc.tensor.matmul(ps[:, 6 + o // 2, P * (o % 2):P * (o % 2) + P], qT[r:r + AD, c, 0:P],
                                         kT[r:r + AD, c, 0:P], start=True, stop=True)
                        last = nc.tensor.matmul(ps[:, 4 + o // 2, SEQ * (o % 2):SEQ * (o % 2) + SEQ], qT[r:r + AD, c, P:],
                                                kT[r:r + AD, c, :], start=True, stop=True)
                    last.then_inc(s["s1_mm"], 1)

                def turn_probs(g):
                    pe.wait_ge(s["p1_ready"], 2 * g + 2)
                    for o in range(4):
                        for j in range(3):
                            last = nc.tensor.transpose(ps[:, 4 + o, P * j:P * j + P], S1[:, o, P * j:P * j + P], ident[:])
                        last.then_inc(s["p1_T"], 1)

                def attend(g):
                    pe.wait_ge(s["p1_copied"], 4 * g + 4)
                    for o, j in enumerate(order):
                        v = AD * (4 * g + j)
                        out_ = ps[AD * (j % 2):AD * (j % 2) + AD, 4, SEQ * (j // 2):SEQ * (j // 2) + SEQ]
                        nc.tensor.matmul(out_, V1[:, 0, v:v + AD], pT1[:, o, 0:SEQ], start=True, stop=False)
                        last = nc.tensor.matmul(out_[:, P:], V1[:, 1, v:v + AD], pT1[:, o, SEQ:], start=False, stop=True)
                    last.then_inc(s["pv1_mm"], 1)

                def spatial():
                    pe.wait_ge(s["vln_ready"], 3)
                    for g in range(GG):
                        for t in range(NT):
                            c = g // 2
                            o = ps[GD * (g % 2):GD * (g % 2) + GD, 5 + c // 2, SEQ * (c % 2) + P * t:SEQ * (c % 2) + P * t + P]
                            last = nc.tensor.matmul(o, vg[:, t, GD * g:GD * g + GD], wsT[:, g, :], start=True, stop=True)
                    last.then_inc(s["mixed_mm"], 1)

                for i in range(26):
                    if 2 <= i < 22:
                        pe.wait_ge(s["evac"], i - 1)
                    k = 2 * (i % 2)
                    outs = [ps[:, k, 0:SEQ], ps[:, k + 1, 0:SEQ]]
                    if i in (4, 5, 8, 9):
                        token_slab(n + i, outs)
                    elif i < 18:
                        feature_slab(n + i, outs, parts_base=8 if i == 0 else None)
                    elif i < 22:
                        if i == 18:
                            pe.wait_ge(s["attn_lo"], 2)
                        if i == 19:
                            pe.wait_ge(s["gm_lo"], 1)
                        branch_slab(n + i, 4 * (i % 2), k)
                    else:
                        o = mixer_out(i - 22)
                        feature_slab(n + i, [o[:, 0, :], o[:, 1, :]], parts_base=0 if i == 22 else None, parts="m_lo", parts_step=4)
                    if i == 0:
                        mean_mm(2, ps[:, 4, 0:SEQ])
                        for t in range(NT):
                            last = nc.tensor.matmul(ps[:, 4, SEQ + 2 * t:SEQ + 2 * t + 2], ss[:, 0, X0 + P * t:X0 + P * t + P],
                                                    ones[:, 0:2], start=True, stop=True)
                        last.then_inc(s["mean_done"], 1)
                    if i == 4:
                        pe.wait_ge(s["std_ready"], 3)
                        scores(0)
                    if i == 7:
                        turn_probs(0)
                    if i == 8:
                        attend(0)
                    if i == 9:
                        pe.wait_ge(s["attn_lo"], 1)
                        scores(1)
                    if i == 12:
                        turn_probs(1)
                    if i == 13:
                        attend(1)
                    if i == 15:
                        spatial()

            def mixer2():
                n = N_MIX2
                xs, xf = (x_hi[:, :, X0:], x_lo[:, :, X0:]), (x_hi, x_lo)

                def one_chunk_slab(n, o):
                    slab_ready(n)
                    wh, wl = wview(w_hi, n, DC, P), wview(w_lo, n, DC, P)
                    for k in range(DC):
                        last = products(o, wh[:, k, :], wl[:, k, :], x_hi[:, k, :], x_lo[:, k, :], k == 0, k == DC - 1)
                    last.then_inc(s["slab_used"], 1)

                def q_slab(n, banks, rope_bank):
                    slab_ready(n)
                    wh, wl = wview(w_hi, n, 2, 768), wview(w_lo, n, 2, 768)
                    for j in range(4):
                        o = ps[:, banks + j // 2, SEQ * (j % 2):SEQ * (j % 2) + SEQ]
                        for k in range(2):
                            c = NOPE * j
                            products(o, wh[:, k, c:c + NOPE], wl[:, k, c:c + NOPE], a_hi[:, k, :], a_lo[:, k, :], k == 0, k == 1)
                    for j in range(2):
                        for k in range(2):
                            c = 4 * NOPE + 2 * ROPE * j
                            last = products(ps[:, rope_bank, SEQ * j:SEQ * j + SEQ], wh[:, k, c:c + P], wl[:, k, c:c + P], a_hi[:, k, :], a_lo[:, k, :], k == 0, k == 1)
                    last.then_inc(s["slab_used"], 1)

                def kv_slab(n, banks, spare, i):
                    slab_ready(n)
                    wh, wl = wview(w_hi, n, 2), wview(w_lo, n, 2)
                    ch, cl = kv_part(a_hi), kv_part(a_lo)
                    for j in range(4):
                        if i == 8 and j in (0, 2):
                            pe.wait_ge(s["kv_left"], j // 2 + 1)
                        o = ps[:, (banks + j) if j < 2 else 2 + j, 0:L2]
                        for k in range(2):
                            c = (NOPE + VH) * j
                            products(o, wh[:, k, c:c + NOPE], wl[:, k, c:c + NOPE], ch[:, k, :], cl[:, k, :], k == 0, k == 1)
                    if i == 7:
                        pe.wait_ge(s["evac"], E2 + 7)
                    else:
                        pe.wait_ge(s["evac"], E2 + 8)
                    for t, bank in zip(TILES, (spare, 6, 7)):
                        for k in range(2):
                            vh, vl = (v[:, k, :].rearrange("p (h c) -> p h c", h=4)[:, :, NOPE:] for v in (wh, wl))
                            o = ps[:, bank, :].rearrange("p (h c) -> p h c", h=4)
                            last = products(o, ch[:, k, t:t + P], cl[:, k, t:t + P], vh, vl, k == 0, k == 1)
                    last.then_inc(s["slab_used"], 1)

                def scores(p):
                    for hh in range(2):
                        hd, r = 2 * p + hh, ROPE * hh
                        for o, t, nk in ((ps[:, 5 + hh, 0:K0], 0, K0), (ps[:, 5 + hh, K0:K0 + L2], P, L2)):
                            nc.tensor.matmul(o, qn[:, hd, t:t + P], kn[:, hd, 0:nk], start=True, stop=False)
                            last = nc.tensor.matmul(o, q_pe[r:r + ROPE, p, t:t + P], k_pe[r:r + ROPE, 0:nk], start=False, stop=True)
                    last.then_inc(s["s2_mm"], 1)

                def turn_probs(p):
                    pe.wait_ge(s["p2_ready"], 2 * p + 2)
                    for hh in range(2):
                        for j, c in enumerate((META, K0 + META, K0 + META + P)):
                            nc.tensor.transpose(ps[:, 5 + hh, P * j:P * j + P], S2[:, hh, c:c + P], ident[:])
                        for t in range(NT):
                            last = nc.tensor.transpose(ps[0:META, 4, SEQ * hh + P * t:SEQ * hh + P * t + P],
                                                       S2[:, hh, K0 * t:K0 * t + META], ident[:])
                    last.then_inc(s["p2_T"], 1)

                def attend(p):
                    pe.wait_ge(s["p2_copied"], 2 * p + 2)
                    if p:
                        pe.wait_ge(s["mla_lo"], p)
                    for hh in range(2):
                        v = VH * (2 * p + hh)
                        o = ps[:, 7, SEQ * hh:SEQ * hh + SEQ]
                        nc.tensor.matmul(o, V2[:, 0, v:v + VH], pT2[:, hh, 0:SEQ], start=True, stop=False)
                        nc.tensor.matmul(o[:, P:], V2[:, 1, v:v + VH], pT2[:, hh, SEQ:], start=False, stop=False)
                        last = nc.tensor.matmul(o, V2m[0:META, v:v + VH], pT2m[0:META, hh, :], start=False, stop=True)
                    last.then_inc(s["pv2_mm"], 1)

                def level(l):
                    if l == 0:
                        pe.wait_ge(s["f_ready"], 4)
                        pe.wait_ge(s["silu2_done"], 4)
                        pe.wait_ge(s["mla_lo"], 4)
                    else:
                        pe.wait_ge(s["hg_ready"], l)
                        pe.wait_ge(s["lvl_done"], 4 * l)
                    if l == 5:
                        pe.wait_ge(s["v_copied"], 2)
                    for hd in range(HH):
                        for t in range(NT):
                            o = ps[:, 4 + hd // 2, SEQ * (hd % 2) + P * t:SEQ * (hd % 2) + P * t + P]
                            last = nc.tensor.matmul(o, k2[:, hd, X0 + P * t:X0 + P * t + P], q2[:, hd, P * t:P * t + P],
                                                    start=True, stop=True)
                    last.then_inc(s["lvl_mm"], 1)

                def turn_v():
                    pe.wait_ge(s["evac"], E2 + 23)
                    for hd in range(HH):
                        last = nc.tensor.transpose(ps[0:META, hd // 4, P * (hd % 4):P * (hd % 4) + P], hiT[:, hd, 0:META], ident[:])
                    last.then_inc(s["vm_T"], 1)
                    pe.wait_ge(s["lvl_done"], 20)
                    for t in range(NT):
                        for hd in range(HH):
                            last = nc.tensor.transpose(ps[:, 4 + 2 * t + hd // 4, P * (hd % 4):P * (hd % 4) + P],
                                                       hiT[:, hd, X0 + P * t:X0 + P * t + P], ident[:])
                    last.then_inc(s["vT"], 1)

                def meta_scores(hd, bank):
                    for t, km in enumerate((k2[:, hd, 0:META], meta[:, 0, hd, :])):
                        c = SEQ * (hd % 2) + P * t
                        last = nc.tensor.matmul(ps[0:META, bank, c:c + P], km, q2[:, hd, P * t:P * t + P], start=True, stop=True)
                    return last

                def cross():
                    pe.wait_ge(s["hg_ready"], 8)
                    pe.wait_ge(s["lvl_done"], 32)
                    for hd in range(HH):
                        nc.tensor.matmul(ps[:, 4 + hd // 4, P * (hd % 4):P * (hd % 4) + P], k2[:, hd, X0:X0 + P],
                                         q2[:, hd, P:], start=True, stop=True)
                    for hd in range(4):
                        last = meta_scores(hd, 6 + hd // 2)
                    last.then_inc(s["cross_mm"], 1)

                def recurrence_out():
                    pe.wait_ge(s["am_copied"], 1)
                    for hd in range(HH):
                        o = ps[:, 4 + hd // 2, SEQ * (hd % 2):SEQ * (hd % 2) + SEQ]
                        v = P * hd
                        nc.tensor.matmul(o, V2[:, 0, v:v + P], AT[:, hd, 0:2, :].rearrange("p j t -> p (j t)"), start=True, stop=False)
                        nc.tensor.matmul(o[:, P:], V2[:, 1, v:v + P], AT[:, hd, 2, :], start=False, stop=False)
                        last = nc.tensor.matmul(o, V2m[0:META, v:v + P], Am[0:META, hd, :], start=False, stop=True)
                        if hd % 2:
                            last.then_inc(s["o_mm"], 1)

                for i in range(43):
                    if 2 <= i < 39:
                        pe.wait_ge(s["evac"], E2 + i - 1)
                    if i == 9:
                        pe.wait_ge(s["kv_left"], 5)
                    k = 2 * (i % 2)
                    if i in FULL and i != 2:
                        feature_slab(n + i, [ps[:, k, 0:L2], ps[:, k + 1, 0:L2]], xf)
                    elif i == 2:
                        one_chunk_slab(n + i, ps[:, 0, 0:L2])
                    elif i in (5, 6):
                        if i == 5:
                            pe.wait_ge(s["ac_lo"], 4)
                        else:
                            pe.wait_ge(s["cstd_ready"], 3)
                        q_slab(n + i, k, 12 - i)
                    elif i in (7, 8):
                        kv_slab(n + i, k, 2 - k, i)
                    elif i < 39:
                        if i == 23:
                            pe.wait_ge(s["mla_lo"], 4)
                        if i == 24:
                            pe.wait_ge(s["vm_copied"], 1)
                        if i == 35:
                            pe.wait_ge(s["o_lo"], 2)
                        src = (a_hi, a_lo) if 23 <= i < 27 or i >= 35 else xs
                        feature_slab(n + i, [ps[:, k, 0:SEQ], ps[:, k + 1, 0:SEQ]], src, parts_base=24 if i == 0 else None)
                    else:
                        o = mixer_out(i - 39)
                        feature_slab(n + i, [o[:, 0, :], o[:, 1, :]], parts_base=0 if i == 39 else None, parts="m2_lo", parts_step=2)
                    if i == 0:
                        pe.wait_ge(s["ss_ready"], 4)
                        pe.wait_ge(s["ss2_ready"], 1)
                        nc.tensor.matmul(ps[:, 4, 0:SEQ], ones[:], ss[:, 0, X0:], start=True, stop=True)
                        nc.tensor.matmul(ps[:, 5, 0:L2], ones[:], ss[:, 1, :], start=True, stop=True).then_inc(s["mean_done"], 1)
                    if i == 2:
                        pe.wait_ge(s["css_ready"], 2)
                        pe.wait_ge(s["std_ready"], 7)
                        nc.tensor.matmul(ps[:, 4, 0:SEQ], ones[:], ss[:, 0, X0:], start=True, stop=True)
                        nc.tensor.matmul(ps[:, 5, 0:L2], ones[:], ss[:, 1, :], start=True, stop=True)
                        for j, t in enumerate(TILES):
                            last = nc.tensor.matmul(ps[:, 6, 2 * j:2 * j + 2], ss[:, 1, t:t + P], ones[:, 0:2], start=True, stop=True)
                        last.then_inc(s["cmean_mm"], 1)
                    if i in MLA_T:
                        turn_probs(MLA_T[i])
                    if i in MLA_PV:
                        attend(MLA_PV[i])
                    if i in MLA_S:
                        p = MLA_S[i]
                        if p == 0:
                            pe.wait_ge(s["evac"], E2 + 9)
                            pe.wait_ge(s["rope_done"], 2)
                        scores(p)
                    if i in LSLOT:
                        level(LSLOT[i])
                    if i == 23:
                        turn_v()
                    if i == 27:
                        cross()
                    if i == 28:
                        pe.wait_ge(s["cross_copied"], 2)
                        for hd in range(4, 8):
                            last = meta_scores(hd, 4 + (hd - 4) // 2)
                        last.then_inc(s["am_mm"], 1)
                    if i == 29:
                        recurrence_out()
                    if i == 30:
                        for hd in range(HH):
                            if hd % 4 == 0:
                                pe.wait_ge(s["osq_done"], hd // 4 + 1)
                            last = nc.tensor.matmul(ps[0:HH, 4, 0:SEQ], pick[:, HH - 1 - hd:2 * HH - 1 - hd], k2[:, hd, 0:SEQ],
                                                    start=hd == 0, stop=hd == HH - 1)
                        last.then_inc(s["osum_mm"], 1)
                    if i == 31:
                        pe.wait_ge(s["orec_ready"], 1)
                        pe.wait_ge(s["o_ready"], 2)
                        for hd in range(HH):
                            last = nc.tensor.matmul(ps[:, 4 + hd // 2, SEQ * (hd % 2):SEQ * (hd % 2) + SEQ],
                                                    ident[0:HH, hd:hd + 1].to_broadcast([HH, P]), std[0:HH, 0, 0:SEQ], start=True, stop=True)
                        last.then_inc(s["obc_mm"], 1)
                mean_mm(5, ps[:, 0, 0:SEQ]).then_inc(s["mean_done"], 1)

            pe.wait_ge(s["id_loaded"], 16)
            pe.wait_ge(s["vec_loaded"], 16)
            nc.tensor.transpose(ps[:, 0, 0:NVEC], vrows[0:NVEC, :], ident[0:NVEC, 0:NVEC]).then_inc(s["vec_T"], 1)
            for c in range(DC):
                pe.wait_ge(s[f"x_loaded{c // 4}"], 16)
                for i in range(NT):
                    last = nc.tensor.transpose(ps[:, 4 + c // 2, SEQ * (c % 2) + P * i:SEQ * (c % 2) + P * i + P],
                                               x_tok[:, i, P * c:P * c + P], ident[:])
                if c % 2:
                    last.then_inc(s["x_T"], 1)
            pe.wait_ge(s["ones_ready"], 1)
            pe.wait_ge(s["vec_ready"], 1)
            ffn(0, 0, 1, 1)
            mixer1()
            ffn(1, 16, 3, 5)
            mixer2()
            ffn(2, 32, 6, 9)
            for k in range(4):
                pe.wait_ge(s["yg_done"], 2 * k + 2)
                if k == 0:
                    pe.wait_ge(s["hT_copied"], 2)
                for c in (2 * k, 2 * k + 1):
                    for i in range(NT):
                        last = nc.tensor.transpose(ps[:, 2 * i + c // 4, P * (c % 4):P * (c % 4) + P], yg[:, c, P * i:P * i + P], ident[:])
            last.then_inc(s["yg_T"], 1)
            pe.wait_ge(s["ss_ready"], 7)
            for i in range(NT):
                last = nc.tensor.matmul(ps[:, 4, SEQ + 2 * i:SEQ + 2 * i + 2], ss[:, 0, X0 + P * i:X0 + P * i + P], ones[:, 0:2],
                                        start=True, stop=True)
            last.then_inc(s["mean_done"], 1)


_INS = [
    "x", "ffn1_norm", "ffn1_w_gate", "ffn1_w_up", "ffn1_w_down", "mix_norm", "w_in", "gmlp_ln_g", "gmlp_ln_b",
    "gmlp_w_s", "gmlp_b_s", "w_branch_attn", "w_branch_gmlp", "w_gate", "b_gate", "w_out", "ffn2_norm",
    "ffn2_w_gate", "ffn2_w_up", "ffn2_w_down", "final_norm", "meta_tokens_2", "w_in_2", "b_gate_2",
    "lb_logits_2", "hg_norm_g_2", "w_hg_o_2", "q_a_norm_g_2", "w_q_b_2", "kv_a_norm_g_2", "w_kv_b_2",
    "w_mla_o_2", "w_out_2", "mix_pre_g_2", "mix_post_g_2", "ffn_pre_g_2", "ffn_post_g_2", "w_ffn_in_2",
    "w_ffn_out_2"]


def kernel(**inputs):
    import concourse.bacc as _bacc
    from concourse.bass_utils import run_bass_kernel_spmd as _run

    nc = _bacc.Bacc("TRN2", target_bir_lowering=False, num_devices=1)
    arrays, args = {}, {}

    def give(name, value):
        v = np.ascontiguousarray(value)
        arrays[f"in_{name}_dram"] = v
        return nc.dram_tensor(f"in_{name}_dram", v.shape, mybir.dt.from_np(v.dtype), kind="ExternalInput").ap()

    packed = [name for name, _ in VEC_ROWS]
    for name in _INS:
        if name in packed:
            continue
        args[name] = give(name, inputs[name])
    vec_d = give("vectors", np.concatenate([np.asarray(inputs[name]).reshape(-1, P) for name, _ in VEC_ROWS]))
    id_d = give("identity", np.eye(P, dtype=np.float32))
    tab_d = give("tables", constants())
    out = nc.dram_tensor("out_0_dram", (1, SEQ, D), F32, kind="ExternalOutput").ap()
    program(nc, args, vec_d, id_d, tab_d, out)
    r = _run(nc, [arrays], core_ids=[0])
    return r.results[0]["out_0_dram"]
```

```python
from contextlib import ExitStack

import numpy as np

import concourse.bass as bass
from concourse import mybir

F32 = mybir.dt.float32
F32R = mybir.dt.float32r
ALU = mybir.AluOpType
ACT = mybir.ActivationFunctionType
AX_X = mybir.AxisListType.X

P = 128
D = 1024
DC = D // P
SEQ = 256
META = 16
L2 = SEQ + META
X0 = META
FF = 2816
PAIRS = FF // 256
NT = SEQ // P
EPS = 1e-6

AH, AD = 8, 64
AW = AH * AD
GG, GC, GW = 8, 128, 512
GD = GW // GG
HH, HC = 8, 16
NOPE, ROPE, VH = 128, 64, 128
QL = 256
MLA_SCALE = float(NOPE + ROPE) ** -0.5
LEVELS = [0, 1, 2, 4, 8, 16, 32, 64]

RING = 3
SLAB = 2048

FFN_SLABS = 3 * PAIRS
N_FFN = [0, FFN_SLABS + 26, 2 * FFN_SLABS + 26 + 43]
N_MIX1 = FFN_SLABS
N_MIX2 = 2 * FFN_SLABS + 26
N_ALL = 3 * FFN_SLABS + 26 + 43
assert N_FFN[1] == N_MIX1 + 26 and N_FFN[2] == N_MIX2 + 43

VEC_ROWS = [("ffn1_norm", 8), ("mix_norm", 8), ("ffn2_norm", 8), ("final_norm", 8), ("mix_pre_g_2", 8),
            ("mix_post_g_2", 8), ("ffn_pre_g_2", 8), ("ffn_post_g_2", 8), ("b_gate", 16), ("b_gate_2", 16),
            ("lb_logits_2", 16), ("hg_norm_g_2", 1), ("q_a_norm_g_2", 2), ("kv_a_norm_g_2", 2)]
VEC = {}
_at = 0
for _name, _k in VEC_ROWS:
    VEC[_name] = _at
    _at += _k
NVEC = _at

T_MASK, T_COS, T_SIN, T_LVL = 0, L2, 2 * L2, 3 * L2
TAB = T_LVL + P * len(LEVELS)
NEG = -1e30


def constants():
    tab = np.zeros((P, TAB), np.float32)
    q, k = np.arange(P)[:, None], np.arange(P)[None, :]
    tab[:, T_MASK + L2 - P:T_MASK + L2] = np.where(k <= q, 0.0, NEG)
    inv_freq = (1.0 / (np.float32(10000.0) ** (np.arange(0, ROPE, 2, dtype=np.float32) / np.float32(ROPE)))).astype(np.float32)
    ang = (np.arange(L2, dtype=np.float32)[:, None] * inv_freq[None, :]).astype(np.float32)
    row = np.arange(P)
    sign = np.where(row % ROPE < ROPE // 2, -1.0, 1.0).astype(np.float32)
    tab[:, T_COS:T_COS + L2] = np.cos(ang).T[row % (ROPE // 2)]
    tab[:, T_SIN:T_SIN + L2] = np.sin(ang).T[row % (ROPE // 2)] * sign[:, None]
    s, t = np.arange(P)[:, None], np.arange(P)[None, :]
    for i, h in enumerate(LEVELS):
        keep = (s == t) if h == 0 else ((s // (2 * h) == t // (2 * h)) & (s % (2 * h) < h) & (t % (2 * h) >= h))
        tab[:, T_LVL + P * i:T_LVL + P * i + P] = keep
    return tab


SEMS = """
slab_used hi_ready lo_ready slab0_in hi0_ready lo0_ready
x_loaded0 x_loaded1 vec_loaded id_loaded tab_loaded ws_loaded gm_loaded meta_loaded store_done
vec_T x_T meta_T ws_T vec_ready ones_ready gfp_ready ws_masked ws_T_copied lb_exp lb_ready meta_T_copied meta_hi meta_lo
h_new xhi_done xlo_done sq_done ss_ready mean_done std_ready rstd_ready
y_bank y_zeroed gate_scaled silu_done up_scaled hidden hid_hi_done hid_lo_done evac
hT_T hT_copied yg_done ysq_done yg_T out_copied
dve_chain dve_chain2 pool_chain
""".split()
SEMS1 = """
gelu_done gsig_done s1_mm s1_masked s1_biased exp1_done p1_ready p1_T p1_copied pv1_mm attn_hi attn_lo
ln_stats vln_ready mixed_mm gm_ready gm_hi gm_lo merged1 merged1b half_done m_hi m_lo
""".split()
SEMS2 = """
sq2_done ss2_ready m2_summed x2_done csq_done css_ready cmean_mm cstd_ready c_ready ac_hi ac_lo kv_left swapped rope_done
s2_mm s2_masked s2_biased exp2_done p2_ready p2_T p2_copied pv2_mm mla_hi mla_lo
silu2_done fsig_done f_ready at_zero hg_ready lvl_mm lvl_done vT vm_T v_copied vm_copied cross_mm cross_copied
am_mm am_copied o_mm o_ready osq_done osum_mm ostd_done orec_ready obc_mm o_final o_hi o_lo
gsigb_done gsiga_done merged2 m2_hi m2_lo mg_done msq_done mg_scaled spread h_first
""".split()


def program(nc, a, vec_d, id_d, tab_d, out):
    ctx = ExitStack()
    with ctx:
        def sb(name, shape, dt):
            return ctx.enter_context(nc.sbuf_tensor(name, shape, dt))

        s = {}
        for name in SEMS + SEMS1 + SEMS2:
            s[name] = ctx.enter_context(nc.semaphore(name))
        slab_in = [ctx.enter_context(nc.semaphore(f"slab_in{i}")) for i in range(RING)]

        ps = ctx.enter_context(nc.psum_tensor("ps", [P, 8, 512], F32))
        stage = sb("stage", [P, RING, SLAB], F32)
        w_hi = sb("w_hi", [P, RING, SLAB], F32R)
        w_lo = sb("w_lo", [P, RING, SLAB], F32R)
        x_hi = sb("x_hi", [P, DC, L2], F32R)
        x_lo = sb("x_lo", [P, DC, L2], F32R)
        a_hi = sb("a_hi", [P, DC, SEQ], F32R)
        a_lo = sb("a_lo", [P, DC, SEQ], F32R)
        h = sb("h", [P, DC, SEQ], F32)
        sq = sb("sq", [P, DC, SEQ], F32)
        ar = sb("ar", [P, 17408], F32)
        tab = sb("tab", [P, TAB], F32)
        ident = sb("ident", [P, P], F32)
        vec = sb("vec", [P, NVEC], F32)
        gfp = sb("gfp", [P, DC], F32)
        lb = sb("lb", [P, 6, DC], F32)
        ones = sb("ones", [P, P], F32)
        eps = sb("eps", [P, 1], F32)
        pick = sb("pick", [P, 2 * HH - 1], F32)
        warm = sb("warm", [P, 16], F32)
        ss = sb("ss", [P, 2, L2], F32)
        std = sb("std", [P, 2, L2], F32)
        rstd = sb("rstd", [P, 2, L2], F32)
        rcol = sb("rcol", [P, 2, 8], F32)

        mask = tab[:, T_MASK:T_MASK + L2]
        lvl = tab[:, T_LVL:].bitcast(mybir.dt.int32).rearrange("p (l t) -> p l t", t=P)

        def view(at, *dims):
            n = int(np.prod(dims))
            v = ar[:, at:at + n]
            if len(dims) == 1:
                return v
            names = "abcd"[:len(dims)]
            return v.rearrange("p (" + " ".join(names) + ") -> p " + " ".join(names),
                               **dict(zip(names, dims)))

        x_tok = view(0, NT, D)
        vrows = view(2048, P)
        ws = view(14336, GG, GC)
        meta_tok = view(2304, D)
        ga_s, ga_a = view(0, 512), view(512, 512)
        up_s, hid = view(1024, 512), view(1536, 512)

        def ffn_input(f):
            return (x_hi[:, :, X0:], x_lo[:, :, X0:]) if f == 0 else (a_hi[:], a_lo[:])

        def hidden_part(f, part, J):
            c = 2 * (J % 2)
            return (a_hi, a_lo)[part][:, c:c + 2, :] if f == 0 else (x_hi, x_lo)[part][:, 4 + c:6 + c, X0:]

        def pair(v):
            return v.rearrange("p (c t) -> p c t", c=2)
        qT, kT = view(2048, 4, SEQ), view(3072, 4, SEQ)
        V1 = view(4096, NT, AW)
        uT = view(5120, 4, SEQ)
        vg = view(6144, NT, GW)
        gates = view(7168, 16, SEQ)
        S1 = view(11264, 4, 384)
        pT1 = view(12800, 4, 384)
        wsT = view(15360, GG, GC)
        gbias = view(16384, 4, GC)
        ln_g, ln_b = view(14336, GW), view(14848, GW)
        tA, tB = view(0, 1024), view(1024, 1024)
        tC, tD = view(11264, 1024), view(12288, 1024)
        meta = sb("meta", [P, 2, DC, META], F32)
        small = sb("small", [P, 96], F32)
        out_tok = view(2048, NT, D)

        q2, k2, f2 = view(0, HH, SEQ), view(2048, HH, L2), view(4224, HH, L2)
        gA = view(4224, DC, SEQ)
        Am = view(4224, HH, SEQ)
        cq, ckv, q_sw = view(4224, 2, SEQ), view(4736, 2, L2), view(5280, 4, SEQ)
        qn, hiT, hgs = view(6400, HH, SEQ), view(6400, HH, L2), view(6400, HH, SEQ)
        kn, yb, sq2 = view(8576, HH, L2), view(8576, DC, SEQ), view(8576, DC, SEQ)
        V2, V2m = view(10752, NT, D), view(12800, D)
        AT = view(13824, HH, 3, P)
        q_pe, k_pe, k_sw = view(13824, 4, SEQ), view(14848, L2), view(15120, L2)
        S2 = view(15120, 2, P + META + L2)
        pT2, pT2m = view(15952, 2, 384), view(16896, 2, SEQ)
        mT = view(13824, 2, 512)
        mg = view(0, DC, SEQ)
        yg = view(4096, DC, SEQ)
        K0 = P + META
        sq_flat = sq[:].rearrange("p c t -> p (c t)")
        cq_sq, ckv_sq = sq_flat[:, 0:2 * SEQ].rearrange("p (c t) -> p c t", c=2), sq_flat[:, 512:512 + 2 * L2].rearrange("p (c t) -> p c t", c=2)
        r_q, r_kv = sq_flat[:, 1056:1056 + SEQ], sq_flat[:, 1312:1312 + L2]
        def kv_part(v):
            return v[:].rearrange("p c t -> p (c t)")[:, 512:512 + 2 * L2].rearrange("p (c t) -> p c t", c=2)
        R2 = rstd[:, 1, :]
        gB = sq
        TILES = (0, X0, X0 + P)
        FULL = (1, 11, 12, 13, 14, 19, 20, 21, 22)
        LSLOT = {18: 0, 19: 1, 20: 2, 21: 3, 22: 4, 24: 5, 25: 6, 26: 7}
        MLA_S = {9: 0, 11: 1, 13: 2, 15: 3}
        MLA_T = {10: 0, 12: 1, 14: 2, 16: 3}
        MLA_PV = {11: 0, 13: 1, 15: 2, 17: 3}
        E2 = 22

        def token_means():
            return ps[:, 4, SEQ:SEQ + 4].rearrange("p (i two) -> p i two", two=2)[:, :, 0]

        def mixer_out(j):
            return ps[:, 4:6, 0:SEQ] if j == 0 else ps[:, (6, 7, 3)[j - 1], :].rearrange("p (c t) -> p c t", c=2)

        def slab_words(n):
            i = n - N_MIX2
            return 1536 if i in (5, 6) else SLAB

        def q_parts(v, n):
            nope, rope = 4 * NOPE, 4 * ROPE
            w = wview(v, n, 2, 768)
            if v is stage:
                w = w.rearrange("p k (h c) -> p k h c", h=4)
                return [(w[:, k, :, 0:NOPE], w[:, k, :, NOPE:]) for k in range(2)]
            return [(w[:, k, 0:nope].rearrange("p (h c) -> p h c", h=4), w[:, k, nope:].rearrange("p (h c) -> p h c", h=4))
                    for k in range(2)]

        def wait_slab(eng, n, it):
            base = 16 * (n // RING + 1)
            eng.wait_ge(slab_in[n % RING], base if it is None else it * (16 * 2) + base)

        def up(n, it, per=6):
            return n if it is None else it * per + n

        def wview(w, n, k, width=None):
            v = w[:, n % RING, :] if width is None else w[:, n % RING, 0:k * width]
            return v.rearrange("p (k c) -> p k c", k=k)

        def mixer1_act(act, split_hi, input_hi):
            n = N_MIX1

            def exps(g):
                act.wait_ge(s["s1_biased"], g + 1)
                for t in range(NT):
                    for o in range(4):
                        v = S1[:, o, P:] if t else S1[:, o, 0:P]
                        k = 4 * t + o
                        nc.scalar.activation(v, v, ACT.Exp, bias=small[:, 8 + k:9 + k],
                                             accum_out=small[:, 16 + k:17 + k]).then_inc(s["exp1_done"], 1)

            def copy_probs(g):
                for o in range(4):
                    act.wait_ge(s["p1_T"], 4 * g + o + 1)
                    nc.scalar.copy(pT1[:, o, :], ps[:, 4 + o, 0:384]).then_inc(s["p1_copied"], 1)

            def attn_hi(g):
                act.wait_ge(s["pv1_mm"], g + 1)
                nc.scalar.activation(a_hi[:, 2 * g:2 * g + 2, :].rearrange("p c t -> p (c t)"), ps[:, 4, :],
                                     ACT.Copy).then_inc(s["attn_hi"], 1)

            for i in range(26):
                if i == 21:
                    for half in range(2):
                        act.wait_ge(s["merged1b"], half + 1)
                        nc.scalar.activation(x_hi[:, 4 + 2 * half:6 + 2 * half, X0:], pair(tC[:, 512 * half:512 * half + 512]),
                                             ACT.Copy).then_inc(s["m_hi"], 1)
                if i == 25:
                    input_hi(a_hi, vec[:, VEC["ffn2_norm"]:], 8, [3])
                split_hi(n + i + 3)
                if i == 19:
                    act.wait_ge(s["merged1"], 1)
                    nc.scalar.activation(x_hi[:, 0:4, X0:], tA.rearrange("p (c t) -> p c t", c=4), ACT.Copy).then_inc(s["m_hi"], 1)
                if 22 <= i < 25:
                    input_hi(a_hi, vec[:, VEC["ffn2_norm"]:], 8, [i - 22])
                if i == 5:
                    exps(0)
                if i == 8:
                    copy_probs(0)
                if i == 9:
                    attn_hi(0)
                if i == 10:
                    for j in range(2):
                        act.wait_ge(s["evac"], 9 + j)
                        v = vg[:, :, 256 * j:256 * j + 256]
                        nc.scalar.activation(v, v, ACT.Gelu_apprx_tanh).then_inc(s["gelu_done"], 1)
                    nc.scalar.activation(uT, uT, ACT.Gelu_apprx_tanh).then_inc(s["gelu_done"], 1)
                    act.wait_ge(s["ln_stats"], 2)
                    nc.scalar.activation(small[:, 58:60], small[:, 49:57:4], ACT.Sqrt, bias=eps[:]).then_inc(s["std_ready"], 1)
                if i == 11:
                    exps(1)
                if i == 13:
                    copy_probs(1)
                if i == 14:
                    attn_hi(1)
                if i == 15:
                    act.wait_ge(s["gm_ready"], 1)
                    nc.scalar.activation(a_hi[:, 4:8, :], tA.rearrange("p (c t) -> p c t", c=4), ACT.Copy).then_inc(s["gm_hi"], 1)
                if i == 17:
                    for c in range(16):
                        act.wait_ge(s["evac"], 10 + c // 2 + 1)
                        nc.scalar.activation(gates[:, c, :], gates[:, c, :], ACT.Sigmoid,
                                             bias=vec[:, VEC["b_gate"] + c:VEC["b_gate"] + c + 1]).then_inc(s["gsig_done"], 1)

        def mixer1_dve(dve, split_lo, seq, input_lo, residual, inverse):
            n = N_MIX1
            bc2 = rstd[:, 0, X0:].unsqueeze(1).to_broadcast([P, 2, SEQ])

            def acc(i):
                k = 6 if i == 2 else 2 * (i % 2)
                return ps[:, k:k + 2, 0:SEQ]

            def group_scores(g):
                dve.wait_ge(s["s1_mm"], g + 1)
                if g:
                    dve.wait_ge(s["p1_T"], 4)
                m0 = mask[:, L2 - P:].unsqueeze(1).to_broadcast([P, 2, P])
                m1 = mask[:, L2 - SEQ:].unsqueeze(1).to_broadcast([P, 4, SEQ])
                for b in range(2):
                    nc.vector.scalar_tensor_tensor(out=S1[:, 2 * b:2 * b + 2, 0:P],
                                                   in0=ps[:, 6 + b, 0:SEQ].rearrange("p (h k) -> p h k", h=2),
                                                   scalar=AD ** -0.5, in1=m0, op0=ALU.mult, op1=ALU.add).then_inc(s["s1_masked"], 1)
                nc.vector.scalar_tensor_tensor(out=S1[:, :, P:], in0=ps[:, 4:6, :].rearrange("p b (h k) -> p (b h) k", h=2),
                                               scalar=AD ** -0.5, in1=m1, op0=ALU.mult, op1=ALU.add).then_inc(s["s1_masked"], 1)
                dve.wait_ge(s["s1_masked"], 3 * g + 3)
                nc.vector.reduce_max(small[:, 0:4], S1[:, :, 0:P], AX_X)
                seq(nc.vector.reduce_max(small[:, 4:8], S1[:, :, P:], AX_X))
                nc.vector.tensor_scalar(small[:, 8:16], small[:, 0:8], -1.0, None, ALU.mult).then_inc(s["s1_biased"], 1)

            def group_probs(g):
                dve.wait_ge(s["exp1_done"], 8 * (g + 1))
                seq(nc.vector.reciprocal(small[:, 24:32], small[:, 16:24]))
                r0 = small[:, 24:28].unsqueeze(2).to_broadcast([P, 4, P])
                r1 = small[:, 28:32].unsqueeze(2).to_broadcast([P, 4, SEQ])
                nc.vector.tensor_tensor(S1[:, :, 0:P], S1[:, :, 0:P], r0, ALU.mult).then_inc(s["p1_ready"], 1)
                nc.vector.tensor_tensor(S1[:, :, P:], S1[:, :, P:], r1, ALU.mult).then_inc(s["p1_ready"], 1)

            def attn_lo(g):
                dve.wait_ge(s["attn_hi"], g + 1)
                nc.vector.tensor_tensor(a_lo[:, 2 * g:2 * g + 2, :].rearrange("p c t -> p (c t)"), ps[:, 4, :],
                                        a_hi[:, 2 * g:2 * g + 2, :].rearrange("p c t -> p (c t)").bitcast(F32),
                                        ALU.subtract).then_inc(s["attn_lo"], 1)

            def layer_norm():
                dve.wait_ge(s["gelu_done"], 2)
                for t in range(NT):
                    st, mv = small[:, 32 + 8 * t:38 + 8 * t], small[:, 48 + 4 * t:50 + 4 * t]
                    seq(nc.vector.bn_stats(st, vg[:, t, :]))
                    nc.vector.bn_aggr(mv, st).then_inc(s["ln_stats"], 1)

            def layer_norm_apply():
                dve.wait_ge(s["std_ready"], 4)
                nc.vector.reciprocal(small[:, 60:62], small[:, 58:60]).then_inc(s["rstd_ready"], 1)
                dve.wait_ge(s["rstd_ready"], 4)
                for t in range(NT):
                    nc.vector.tensor_scalar(vg[:, t, :], vg[:, t, :], small[:, 48 + 4 * t:49 + 4 * t], small[:, 60 + t:61 + t],
                                            ALU.subtract, ALU.mult).then_inc(s["vln_ready"], 1)

            def merged_lo(k, c0, c1):
                src = tA if c0 == 0 else tC[:, SEQ * (c0 - 4):SEQ * (c1 - 4)]
                dve.wait_ge(s["m_hi"], k + 1)
                nc.vector.tensor_tensor(x_lo[:, c0:c1, X0:], src.rearrange("p (c t) -> p c t", t=SEQ), x_hi[:, c0:c1, X0:].bitcast(F32),
                                        ALU.subtract).then_inc(s["m_lo"], 1)

            def spatial_gate():
                dve.wait_ge(s["mixed_mm"], 1)
                dve.wait_ge(s["gelu_done"], 3)
                t4 = tA.rearrange("p (c i t) -> p c i t", c=4, i=NT)
                mixed = ps[:, 5:7, :].rearrange("p b (c i t) -> p (b c) i t", c=2, i=NT)
                gb = gbias.unsqueeze(2).to_broadcast([P, 4, NT, P])
                seq(nc.vector.tensor_tensor(t4, mixed, gb, ALU.add))
                nc.vector.tensor_tensor(tA, tA, uT.rearrange("p c t -> p (c t)"), ALU.mult).then_inc(s["gm_ready"], 1)

            dve.wait_ge(s["tab_loaded"], 16)
            inverse(2)
            inverse(3, rcol[:, 1, 0:2], rcol[:, 0, 0:2])
            dve.wait_ge(s["rstd_ready"], 3)
            for i in range(26):
                dve.wait_ge(s["slab_used"], n + i + 1)
                if i < 4:
                    dst = (qT, kT)[i // 2][:, 2 * (i % 2):2 * (i % 2) + 2, :]
                    nc.vector.tensor_tensor(dst, acc(i), bc2, ALU.mult).then_inc(s["evac"], 1)
                elif i < 6 or i in (8, 9):
                    dst, j = (V1, i - 4) if i < 6 else (vg, i - 8)
                    for t in range(NT):
                        op = nc.vector.tensor_scalar(dst[:, t, 256 * j:256 * j + 256], ps[:, 2 * (i % 2) + t, 0:256],
                                                     rcol[:, 1, t:t + 1], None, ALU.mult)
                    op.then_inc(s["evac"], 1)
                elif i < 8:
                    nc.vector.tensor_tensor(uT[:, 2 * (i - 6):2 * (i - 5), :], acc(i), bc2, ALU.mult).then_inc(s["evac"], 1)
                elif i < 18:
                    nc.vector.tensor_tensor(gates[:, 2 * (i - 10):2 * (i - 9), :], acc(i), bc2, ALU.mult).then_inc(s["evac"], 1)
                elif i < 22:
                    q, b = (i - 18) // 2, i % 2
                    dve.wait_ge(s["gsig_done"], 16)
                    y = ps[:, 2 * b:2 * b + 2, :].rearrange("p b t -> p (b t)")
                    gt = gates[:, 8 * b + 4 * q:8 * b + 4 * q + 4, :].rearrange("p c t -> p (c t)")
                    if i < 21:
                        nc.vector.tensor_tensor((tA, tB, tC)[i - 18], y, gt, ALU.mult).then_inc(s["evac"], 1)
                    if i == 20:
                        merged_lo(0, 0, 4)
                    if i == 21:
                        dve.wait_ge(s["evac"], 21)
                        for half in range(2):
                            v = slice(512 * half, 512 * half + 512)
                            op = nc.vector.tensor_tensor(tD[:, v], y[:, v], gt[:, v], ALU.mult)
                            op.then_inc(s["half_done"] if half == 0 else s["evac"], 1)
                            if half == 0:
                                dve.wait_ge(s["half_done"], 1)
                            else:
                                dve.wait_ge(s["evac"], 22)
                            nc.vector.tensor_tensor(tC[:, v], tC[:, v], tD[:, v], ALU.add).then_inc(s["merged1b"], 1)
                        dve.wait_ge(s["merged1b"], 2)
                        merged_lo(1, 4, 6)
                        merged_lo(2, 6, 8)
                else:
                    residual(i - 22, 1.0, mixer_out(i - 22))
                    if i < 25:
                        split_lo(n + i + 3)
                    dve.wait_ge(s["h_new"], 8 + i - 22 + 1)
                    input_lo(i - 22, vec[:, VEC["ffn2_norm"]:], 16, (a_hi, a_lo))
                if i == 6:
                    group_probs(0)
                if i == 21:
                    split_lo(n + i + 2)
                if i < 22 and i != 20 or i == 25:
                    split_lo(n + i + 3)
                if i == 5:
                    group_scores(0)
                if i == 9:
                    attn_lo(0)
                if i == 10:
                    layer_norm()
                    group_scores(1)
                if i == 11:
                    group_probs(1)
                    layer_norm_apply()
                if i == 14:
                    attn_lo(1)
                if i == 15:
                    spatial_gate()
                    dve.wait_ge(s["gm_hi"], 1)
                    nc.vector.tensor_tensor(a_lo[:, 4:8, :], tA.rearrange("p (c t) -> p c t", c=4),
                                            a_hi[:, 4:8, :].bitcast(F32), ALU.subtract).then_inc(s["gm_lo"], 1)

        def mixer2_act(act, split_hi, load_table):
            n = N_MIX2
            bg = vec[:, VEC["b_gate_2"]:]

            def pair_hi(p):
                act.wait_ge(s["pv2_mm"], p + 1)
                nc.scalar.activation(a_hi[:, 2 * p:2 * p + 2, :].rearrange("p c t -> p (c t)"), ps[:, 7, :],
                                     ACT.Copy).then_inc(s["mla_hi"], 1)

            for i in range(43):
                if i < 2:
                    src, sqs, dst, g = ((cq, cq_sq, a_hi[:, 0:2, :], "q_a_norm_g_2"), (ckv, ckv_sq, kv_part(a_hi), "kv_a_norm_g_2"))[i]
                    act.wait_ge(s["evac"], E2 + i + 1)
                    nc.scalar.activation(sqs, src, ACT.Square).then_inc(s["csq_done"], 1)
                    for c in range(2):
                        k = VEC[g] + c
                        nc.scalar.activation(dst[:, c, :], src[:, c, :], ACT.Copy, scale=vec[:, k:k + 1]).then_inc(s["ac_hi"], 1)
                if 35 <= i < 39:
                    j = i - 35
                    act.wait_ge(s["merged2"], j + 1)
                    nc.scalar.activation(x_hi[:, 2 * j:2 * j + 2, X0:], pair(mT[:, j % 2, :]), ACT.Copy).then_inc(s["m2_hi"], 1)
                if i >= 39:
                    j = i - 39
                    if j == 3:
                        load_table(ACT.Sqrt)
                    act.wait_ge(s["slab_used"], n + i + 1)
                    nc.scalar.activation(sq[:, 2 * j:2 * j + 2, :], mixer_out(j), ACT.Square).then_inc(s["msq_done"], 1)
                    for c in range(2):
                        k = VEC["mix_post_g_2"] + 2 * j + c
                        nc.scalar.activation(mg[:, 2 * j + c, :], mixer_out(j)[:, c, :], ACT.Copy,
                                             scale=vec[:, k:k + 1]).then_inc(s["mg_done"], 1)
                if 0 < i < 42:
                    split_hi(n + i + 3)
                if i in (5, 6):
                    j = i - 5
                    act.wait_ge(s["evac"], E2 + i + 1)
                    for d, r in ((0, 32), (32, 0), (64, 96), (96, 64)):
                        nc.scalar.copy(q_sw[d:d + 32, 2 * j:2 * j + 2, :], q_pe[r:r + 32, 2 * j:2 * j + 2, :]).then_inc(s["swapped"], 1)
                if i == 3:
                    act.wait_ge(s["cmean_mm"], 1)
                    for dst, src in ((r_q, ps[:, 4, 0:SEQ]), (r_kv, ps[:, 5, 0:L2]),
                                     (rcol[:, 0, 2:5], ps[:, 6, 0:6].rearrange("p (t two) -> p t two", two=2)[:, :, 0])):
                        nc.scalar.activation(dst, src, ACT.Sqrt, scale=float(D // QL), bias=eps[:]).then_inc(s["cstd_ready"], 1)
                if i in MLA_PV:
                    pair_hi(MLA_PV[i])
                if i in MLA_S:
                    p = MLA_S[i]
                    for t in range(NT):
                        act.wait_ge(s["s2_biased"], 2 * p + t + 1)
                        for hh in range(2):
                            v = S2[:, hh, K0:] if t else S2[:, hh, 0:K0]
                            k = 2 * t + hh
                            nc.scalar.activation(v, v, ACT.Exp, bias=small[:, 8 + k:9 + k],
                                                 accum_out=small[:, 16 + k:17 + k]).then_inc(s["exp2_done"], 1)
                if i in MLA_T:
                    p = MLA_T[i]
                    act.wait_ge(s["p2_T"], p + 1)
                    nc.scalar.copy(pT2, ps[:, 5:7, 0:384]).then_inc(s["p2_copied"], 1)
                    nc.scalar.copy(pT2m[0:META].rearrange("p c t -> p (c t)"), ps[0:META, 4, :]).then_inc(s["p2_copied"], 1)
                if i in (3, 4, 9, 10):
                    j = i - 3 if i < 5 else i - 7
                    act.wait_ge(s["evac"], E2 + i + 1)
                    nc.scalar.activation(q2[:, 2 * j:2 * j + 2, :], q2[:, 2 * j:2 * j + 2, :], ACT.Silu).then_inc(s["silu2_done"], 1)
                if 11 <= i < 15:
                    j = i - 11
                    act.wait_ge(s["evac"], E2 + i + 1)
                    nc.scalar.activation(f2[:, 2 * j:2 * j + 2, :], f2[:, 2 * j:2 * j + 2, :], ACT.Sigmoid).then_inc(s["fsig_done"], 1)
                if 27 <= i < 31:
                    j = i - 27
                    act.wait_ge(s["evac"], E2 + i + 1)
                    nc.scalar.activation(hgs[:, 2 * j:2 * j + 2, :], hgs[:, 2 * j:2 * j + 2, :], ACT.Silu).then_inc(s["silu2_done"], 1)
                if i == 18:
                    for c in range(DC):
                        act.wait_ge(s["evac"], E2 + 15 + c // 2 + 1)
                        nc.scalar.activation(gB[:, c, :], gB[:, c, :], ACT.Sigmoid, bias=bg[:, DC + c:DC + c + 1]).then_inc(s["gsigb_done"], 1)
                if i == 23:
                    act.wait_ge(s["vm_T"], 1)
                    nc.scalar.copy(V2m[0:META], ps[0:META, 0:2, :].rearrange("p b c -> p (b c)")).then_inc(s["vm_copied"], 1)
                    act.wait_ge(s["vT"], 1)
                    for t in range(NT):
                        nc.scalar.copy(V2[:, t, :], ps[:, 4 + 2 * t:6 + 2 * t, :].rearrange("p b c -> p (b c)")).then_inc(s["v_copied"], 1)
                if i == 27:
                    act.wait_ge(s["cross_mm"], 1)
                    nc.scalar.copy(AT[:, :, 1, :], ps[:, 4:6, :].rearrange("p b (h t) -> p (b h) t", h=4)).then_inc(s["cross_copied"], 1)
                    nc.scalar.copy(Am[0:META, 0:4, :].rearrange("p h t -> p (h t)"),
                                   ps[0:META, 6:8, :].rearrange("p b t -> p (b t)")).then_inc(s["cross_copied"], 1)
                if i == 28:
                    act.wait_ge(s["am_mm"], 1)
                    nc.scalar.copy(Am[0:META, 4:8, :].rearrange("p h t -> p (h t)"),
                                   ps[0:META, 4:6, :].rearrange("p b t -> p (b t)")).then_inc(s["am_copied"], 1)
                if i == 29:
                    for b in range(2):
                        act.wait_ge(s["o_ready"], b + 1)
                        nc.scalar.activation(k2[:, 4 * b:4 * b + 4, 0:SEQ], q2[:, 4 * b:4 * b + 4, :], ACT.Square).then_inc(s["osq_done"], 1)
                if i == 30:
                    act.wait_ge(s["osum_mm"], 1)
                    nc.scalar.activation(std[0:HH, 1, 0:SEQ], ps[0:HH, 4, 0:SEQ], ACT.Sqrt, bias=eps[0:HH]).then_inc(s["ostd_done"], 1)
                if i == 31:
                    for b in range(2):
                        act.wait_ge(s["o_final"], b + 1)
                        nc.scalar.activation(a_hi[:, 4 * b:4 * b + 4, :], q2[:, 4 * b:4 * b + 4, :], ACT.Copy).then_inc(s["o_hi"], 1)
                if i == 34:
                    for c in range(DC):
                        act.wait_ge(s["evac"], E2 + 31 + c // 2 + 1)
                        nc.scalar.activation(gA[:, c, :], gA[:, c, :], ACT.Sigmoid, bias=bg[:, c:c + 1]).then_inc(s["gsiga_done"], 1)

        def mixer2_dve(dve, split_lo, seq, inverse, input_lo):
            n = N_MIX2

            def bc(r, k):
                return r.unsqueeze(1).to_broadcast([P, k, r.shape[1]])

            def acc(i, width):
                k = 2 * (i % 2)
                return ps[:, k:k + 2, 0:width]

            def pair_scores(p):
                dve.wait_ge(s["s2_mm"], p + 1)
                if p:
                    dve.wait_ge(s["p2_T"], p)
                else:
                    dve.wait_ge(s["rope_done"], 3)
                parts = ((S2[:, :, 0:K0], ps[:, 5:7, 0:K0], bc(mask[:, P:], 2), K0), (S2[:, :, K0:], ps[:, 5:7, K0:K0 + L2], bc(mask, 2), L2))
                for t, (v, src, m, _) in enumerate(parts):
                    nc.vector.scalar_tensor_tensor(out=v, in0=src, scalar=MLA_SCALE, in1=m, op0=ALU.mult, op1=ALU.add).then_inc(s["s2_masked"], 1)
                    dve.wait_ge(s["s2_masked"], 2 * p + t + 1)
                    if p:
                        dve.wait_ge(s["exp2_done"], 4 * p)
                    seq(nc.vector.reduce_max(small[:, 2 * t:2 * t + 2], v, AX_X))
                    nc.vector.tensor_scalar(small[:, 8 + 2 * t:10 + 2 * t], small[:, 2 * t:2 * t + 2], -1.0, None, ALU.mult).then_inc(s["s2_biased"], 1)
                for t, (v, _, _, nk) in enumerate(parts):
                    dve.wait_ge(s["exp2_done"], 4 * p + 2 * t + 2)
                    r = small[:, 24 + 2 * t:26 + 2 * t]
                    seq(nc.vector.reciprocal(r, small[:, 16 + 2 * t:18 + 2 * t]))
                    nc.vector.tensor_tensor(v, v, r.unsqueeze(2).to_broadcast([P, 2, nk]), ALU.mult).then_inc(s["p2_ready"], 1)

            def pair_lo(p):
                dve.wait_ge(s["mla_hi"], p + 1)
                nc.vector.tensor_tensor(a_lo[:, 2 * p:2 * p + 2, :].rearrange("p c t -> p (c t)"), ps[:, 7, :],
                                        a_hi[:, 2 * p:2 * p + 2, :].rearrange("p c t -> p (c t)").bitcast(F32),
                                        ALU.subtract).then_inc(s["mla_lo"], 1)

            def forget(j):
                dve.wait_ge(s["fsig_done"], j + 1)
                for c in (2 * j, 2 * j + 1):
                    seq(nc.vector.tensor_scalar(f2[:, c, :], f2[:, c, :], lb[:, 5, c:c + 1], lb[:, 4, c:c + 1], ALU.mult, ALU.add))
                nc.vector.tensor_scalar(k2[:, 2 * j:2 * j + 2, :], f2[:, 2 * j:2 * j + 2, :], -1.0, 1.0, ALU.mult,
                                        ALU.add).then_inc(s["f_ready"], 1)

            def level(l):
                size = LEVELS[l]
                dve.wait_ge(s["lvl_mm"], l + 1)
                if size == 0:
                    nc.vector.tensor_tensor(q2, q2, f2[:, :, X0:], ALU.mult).then_inc(s["hg_ready"], 1)
                else:
                    nb = SEQ // (2 * size)
                    fx = f2[:, :, X0:].rearrange("p h (b two s) -> p h b two s", two=2, s=size)
                    qx = q2.rearrange("p h (b two s) -> p (h b) two s", two=2, s=size)
                    if size < META:
                        kk, ff = k2, f2
                    else:
                        kk, ff = k2[:, :, X0:], f2[:, :, X0:]
                    kx = kk.rearrange("p h (b two s) -> p h b two s", two=2, s=size)
                    fk = ff.rearrange("p h (b two s) -> p h b two s", two=2, s=size)
                    nk = kk.shape[2] // (2 * size)
                    o = kx[:, :, :, 0, :]
                    nc.vector.tensor_tensor(o, o, fk[:, :, :, 1, 0:1].to_broadcast([P, HH, nk, size]), ALU.mult).then_inc(s["dve_chain2"], 1)
                    qv = q2.rearrange("p h (b two s) -> p h b two s", two=2, s=size)[:, :, :, 1, :]
                    nc.vector.tensor_tensor(qv, qv, fx[:, :, :, 0, 0:1].to_broadcast([P, HH, nb, size]), ALU.mult).then_inc(s["dve_chain2"], 1)
                    dve.wait_ge(s["dve_chain2"], 3 * l - 1)
                    t0 = fk[:, :, :, 0, 0]
                    nc.vector.tensor_tensor(t0, t0, fk[:, :, :, 1, 0], ALU.mult).then_inc(s["dve_chain2"], 1)
                    dve.wait_ge(s["dve_chain2"], 3 * l)
                    if l == len(LEVELS) - 1:
                        tot = f2[:, :, X0:X0 + 1].to_broadcast([P, HH, META])
                        nc.vector.tensor_tensor(meta[:, 0], k2[:, :, 0:META], tot, ALU.mult).then_inc(s["hg_ready"], 1)
                    else:
                        nc.vector.tensor_copy(meta[:, 1, 0, 0:1], f2[:, 0, 0:1]).then_inc(s["hg_ready"], 1)
                if l == 0:
                    dve.wait_ge(s["at_zero"], 1)
                else:
                    dve.wait_ge(s["lvl_done"], 4 * l)
                for b in range(4):
                    for hd in range(2):
                        o, m = AT[:, 2 * b + hd, 0:3:2, :], lvl[:, l, :]
                        d = ps[:, 4 + b, SEQ * hd:SEQ * hd + SEQ].rearrange("p (t q) -> p t q", t=2)
                        if size:
                            o, d = (v.rearrange("p t (b two s) -> p t b two s", two=2, s=size)[:, :, :, 1, :] for v in (o, d))
                            m = m.rearrange("p (b two s) -> p b two s", two=2, s=size)[:, :, 1, :].unsqueeze(1).to_broadcast([P, 2, P // (2 * size), size])
                        else:
                            m = m.unsqueeze(1).to_broadcast([P, 2, P])
                        op = nc.vector.copy_predicated(o, m, d)
                    op.then_inc(s["lvl_done"], 1)

            dve.wait_ge(s["mean_done"], 4)
            seq(nc.vector.tensor_scalar(std[:, 1, X0:], ps[:, 4, 0:SEQ], EPS, EPS * EPS, ALU.mult, ALU.add))
            seq(nc.vector.tensor_tensor(std[:, 1, X0:], std[:, 1, X0:], ps[:, 5, X0:L2], ALU.add))
            nc.vector.tensor_scalar(std[:, 1, 0:META], ps[:, 5, 0:META], EPS, None, ALU.add).then_inc(s["m2_summed"], 1)
            split_lo(n + 3)
            inverse(6, R2, std[:, 1, :])
            dve.wait_ge(s["rstd_ready"], 6)
            for i in range(43):
                if i < 39:
                    dve.wait_ge(s["slab_used"], n + i + 1)
                if i < 2:
                    if i == 0:
                        for j, (dst, w) in enumerate(((cq, SEQ), (ckv, L2))):
                            dve.wait_ge(s["slab_used"], n + j + 1)
                            nc.vector.tensor_tensor(dst, acc(j, w), bc(R2[:, L2 - w:], 2), ALU.mult).then_inc(s["evac"], 1)
                    src, sqs, hi, lo, g, o = ((cq, cq_sq, a_hi[:, 0:2, :], a_lo[:, 0:2, :], "q_a_norm_g_2", ss[:, 0, X0:]),
                                              (ckv, ckv_sq, kv_part(a_hi), kv_part(a_lo), "kv_a_norm_g_2", ss[:, 1, :]))[i]
                    dve.wait_ge(s["csq_done"], i + 1)
                    nc.vector.tensor_tensor(o, sqs[:, 0, :], sqs[:, 1, :], ALU.add).then_inc(s["css_ready"], 1)
                    dve.wait_ge(s["evac"], E2 + i + 1)
                    for c in range(2):
                        dve.wait_ge(s["ac_hi"], 2 * i + c + 1)
                        k = VEC[g] + c
                        nc.vector.scalar_tensor_tensor(out=lo[:, c, :], in0=src[:, c, :], scalar=vec[:, k:k + 1],
                                                       in1=hi[:, c, :].bitcast(F32), op0=ALU.mult, op1=ALU.subtract).then_inc(s["ac_lo"], 1)
                elif i == 2:
                    nc.vector.tensor_tensor(k_pe, ps[:, 7, 0:L2], R2, ALU.mult).then_inc(s["evac"], 1)
                elif i in (3, 4, 9, 10):
                    j = i - 3 if i < 5 else i - 7
                    nc.vector.tensor_tensor(q2[:, 2 * j:2 * j + 2, :], acc(i, SEQ), bc(R2[:, X0:], 2), ALU.mult).then_inc(s["evac"], 1)
                elif i in (5, 6):
                    k, j = 2 * (i % 2), i - 5
                    dve.wait_ge(s["c_ready"], 3)
                    nc.vector.tensor_tensor(qn[:, 4 * j:4 * j + 4, :], ps[:, k:k + 2, :].rearrange("p b (h t) -> p (b h) t", h=2),
                                            bc(r_q, 4), ALU.mult)
                    nc.vector.tensor_tensor(q_pe[:, 2 * j:2 * j + 2, :], pair(ps[:, 12 - i, :]), bc(r_q, 2), ALU.mult).then_inc(s["evac"], 1)
                elif i in (7, 8):
                    k, j = 2 * (i % 2), i - 7
                    nc.vector.tensor_scalar(V2m[0:META, 512 * j:512 * j + 512], ps[0:META, 2 - k, :], rcol[0:META, 1, 2:3], None,
                                            ALU.mult).then_inc(s["kv_left"], 1)
                    nc.vector.tensor_tensor(kn[:, 4 * j + 2:4 * j + 4, :], ps[:, 4:6, 0:L2], bc(r_kv, 2), ALU.mult).then_inc(s["kv_left"], 1)
                    for t in range(NT):
                        nc.vector.tensor_scalar(V2[:, t, 512 * j:512 * j + 512], ps[:, 6 + t, :], rcol[:, 1, 3 + t:4 + t], None,
                                                ALU.mult).then_inc(s["kv_left"], 1)
                    nc.vector.tensor_tensor(kn[:, 4 * j:4 * j + 2, :], ps[:, k:k + 2, 0:L2], bc(r_kv, 2), ALU.mult).then_inc(s["evac"], 1)
                elif 11 <= i < 15:
                    j = i - 11
                    nc.vector.tensor_tensor(f2[:, 2 * j:2 * j + 2, :], acc(i, L2), bc(R2, 2), ALU.mult).then_inc(s["evac"], 1)
                elif 15 <= i < 19:
                    j = i - 15
                    nc.vector.tensor_tensor(gB[:, 2 * j:2 * j + 2, :], acc(i, SEQ), bc(R2[:, X0:], 2), ALU.mult).then_inc(s["evac"], 1)
                elif 19 <= i < 23:
                    j = i - 19
                    nc.vector.tensor_tensor(hiT[:, 2 * j:2 * j + 2, :], acc(i, L2), bc(R2, 2), ALU.mult).then_inc(s["evac"], 1)
                elif 23 <= i < 27:
                    j = i - 23
                    dve.wait_ge(s["gsigb_done"], 2 * j + 2)
                    nc.vector.tensor_tensor(yb[:, 2 * j:2 * j + 2, :], acc(i, SEQ), gB[:, 2 * j:2 * j + 2, :], ALU.mult).then_inc(s["evac"], 1)
                elif 27 <= i < 31:
                    j = i - 27
                    if j == 0:
                        dve.wait_ge(s["v_copied"], 2)
                    nc.vector.tensor_tensor(hgs[:, 2 * j:2 * j + 2, :], acc(i, SEQ), bc(R2[:, X0:], 2), ALU.mult).then_inc(s["evac"], 1)
                elif 31 <= i < 35:
                    j = i - 31
                    nc.vector.tensor_tensor(gA[:, 2 * j:2 * j + 2, :], acc(i, SEQ), bc(R2[:, X0:], 2), ALU.mult).then_inc(s["evac"], 1)
                elif 35 <= i < 39:
                    j = i - 35
                    dve.wait_ge(s["gsiga_done"], 2 * j + 2)
                    if j >= 2:
                        dve.wait_ge(s["m2_lo"], j - 1)
                    m = pair(mT[:, j % 2, :])
                    nc.vector.tensor_tensor(m, acc(i, SEQ), gA[:, 2 * j:2 * j + 2, :], ALU.mult).then_inc(s["evac"], 1)
                    dve.wait_ge(s["evac"], E2 + i + 1)
                    nc.vector.tensor_tensor(m, m, yb[:, 2 * j:2 * j + 2, :], ALU.add).then_inc(s["merged2"], 1)
                    dve.wait_ge(s["merged2"], j + 1)
                    dve.wait_ge(s["m2_hi"], j + 1)
                    nc.vector.tensor_tensor(x_lo[:, 2 * j:2 * j + 2, X0:], m, x_hi[:, 2 * j:2 * j + 2, X0:].bitcast(F32),
                                            ALU.subtract).then_inc(s["m2_lo"], 1)
                if i == 4:
                    for k, (dst, src) in enumerate(((r_q, r_q), (r_kv, r_kv), (rcol[:, 1, 2:5], rcol[:, 0, 2:5]))):
                        dve.wait_ge(s["cstd_ready"], k + 1)
                        nc.vector.reciprocal(dst, src).then_inc(s["c_ready"], 1)
                if i == 38:
                    split_lo(n + i + 2)
                if i == 6:
                    split_lo(n + i + 2)
                if i == 7:
                    inverse(7)
                if i not in (0, 5, 37, 42):
                    split_lo(n + i + 3)
                if i in MLA_PV:
                    pair_lo(MLA_PV[i])
                if i in MLA_S:
                    pair_scores(MLA_S[i])
                if 12 <= i < 16:
                    forget(i - 12)
                if i in LSLOT:
                    level(LSLOT[i])
                if i == 29:
                    for b in range(2):
                        dve.wait_ge(s["o_mm"], 2 * b + 2)
                        nc.vector.tensor_copy(q2[:, 4 * b:4 * b + 4, :], ps[:, 4 + 2 * b:6 + 2 * b, :].rearrange("p b (h t) -> p (b h) t", h=2)).then_inc(s["o_ready"], 1)
                if i == 30:
                    dve.wait_ge(s["ostd_done"], 1)
                    nc.vector.reciprocal(std[0:HH, 0, 0:SEQ], std[0:HH, 1, 0:SEQ]).then_inc(s["orec_ready"], 1)
                if i == 31:
                    dve.wait_ge(s["obc_mm"], 1)
                    dve.wait_ge(s["silu2_done"], 8)
                    k = VEC["hg_norm_g_2"]
                    for b in range(2):
                        o = q2[:, 4 * b:4 * b + 4, :]
                        seq(nc.vector.tensor_tensor(o, o, ps[:, 4 + 2 * b:6 + 2 * b, :].rearrange("p b (h t) -> p (b h) t", h=2), ALU.mult))
                        nc.vector.scalar_tensor_tensor(out=o, in0=o, scalar=vec[:, k:k + 1], in1=hgs[:, 4 * b:4 * b + 4, :],
                                                       op0=ALU.mult, op1=ALU.mult).then_inc(s["o_final"], 1)
                if i == 31:
                    for b in range(2):
                        dve.wait_ge(s["o_hi"], b + 1)
                        nc.vector.tensor_tensor(a_lo[:, 4 * b:4 * b + 4, :], q2[:, 4 * b:4 * b + 4, :],
                                                a_hi[:, 4 * b:4 * b + 4, :].bitcast(F32), ALU.subtract).then_inc(s["o_lo"], 1)
            inverse(8, rcol[:, 1, 0:2], rcol[:, 0, 0:2])
            dve.wait_ge(s["spread"], 1)
            r, g = ps[:, 0, 0:SEQ], vec[:, VEC["ffn_pre_g_2"]:]
            dve.wait_ge(s["mg_done"], 8)
            dve.wait_ge(s["x2_done"], 2 * DC)
            for b in range(4):
                v, hb = mg[:, 2 * b:2 * b + 2, :], h[:, 2 * b:2 * b + 2, :]
                if b == 0:
                    for c in range(2):
                        nc.vector.tensor_tensor(mg[:, c, :], mg[:, c, :], r, ALU.mult).then_inc(s["mg_scaled"], 1)
                        dve.wait_ge(s["mg_scaled"], c + 1)
                        nc.vector.tensor_tensor(h[:, c, :], h[:, c, :], mg[:, c, :], ALU.add).then_inc(s[("h_first", "h_new")[c]], 1)
                    input_lo(0, g, 32, (a_hi, a_lo), chunks=(0,))
                    continue
                nc.vector.tensor_tensor(v, v, bc(r, 2), ALU.mult).then_inc(s["mg_scaled"], 1)
                if b == 1:
                    input_lo(0, g, 32, (a_hi, a_lo), chunks=(1,))
                dve.wait_ge(s["mg_scaled"], b + 2)
                nc.vector.tensor_tensor(hb, hb, v, ALU.add).then_inc(s["h_new"], 1)
                if b > 1:
                    input_lo(b - 1, g, 32, (a_hi, a_lo))
            input_lo(3, g, 32, (a_hi, a_lo))
            split_lo(n + 45)

        block = ctx.enter_context(nc.Block())

        @block.sync
        def _(sp):
            xs = a["x"][0].rearrange("(i p) d -> p i d", p=P)
            w0 = a["ffn1_w_gate"][0].rearrange("(k p) c -> p k c", p=P)[:, :, 0:256]
            for half in range(2):
                c, k = slice(512 * half, 512 * half + 512), slice(4 * half, 4 * half + 4)
                sp.dma_start(x_tok[:, :, c], xs[:, :, c]).then_inc(s[f"x_loaded{half}"], 16)
                done = slab_in[0] if half else s["slab0_in"]
                sp.dma_start(wview(stage, 0, DC)[:, k, :], w0[:, k, :]).then_inc(done, 16)

            def load(n, src, dst=None, it=None):
                if n >= RING or it is not None:
                    sp.wait_ge(s["lo_ready"], up(max(n - RING + 1, 1), it))
                if dst is None:
                    dst = wview(stage, n, src.shape[1])
                sp.dma_start(dst, src).then_inc(slab_in[n % RING], 16)

            def cols(w, c0, width=256):
                return w.rearrange("(k p) c -> p k c", p=P)[:, :, bass.ds(c0, width)]

            def rows(w, r0):
                return w[bass.ds(r0, 256), :].rearrange("(k p) c -> p k c", p=P)

            def ffn_loads(f, wg, g0, wu, u0, wd):
                n = N_FFN[f]
                if f:
                    load(n, cols(wg, g0))
                load(n + 1, cols(wu, u0))
                if f == 0:
                    sp.dma_start(ws, a["gmlp_w_s"][0].rearrange("g i j -> i g j")).then_inc(s["ws_loaded"], 16)
                    sp.dma_start(meta_tok[0:META, :], a["meta_tokens_2"]).then_inc(s["meta_loaded"], 16)
                with sp.Fori(0, (PAIRS - 1) // 2) as it:
                    for b in range(2):
                        load(n + 2 + 3 * b, cols(wg, it * 512 + (g0 + 256 * (b + 1))), it=it)
                        load(n + 3 + 3 * b, cols(wu, it * 512 + (u0 + 256 * (b + 1))), it=it)
                        load(n + 4 + 3 * b, rows(wd, it * 512 + 256 * b), it=it)
                load(n + FFN_SLABS - 1, rows(wd, 256 * (PAIRS - 1)))

            ffn_loads(0, a["ffn1_w_gate"][0], 0, a["ffn1_w_up"][0], 0, a["ffn1_w_down"][0])
            n = N_MIX1
            for i in range(10):
                load(n + i, cols(a["w_in"][0], 256 * i))
            for i in range(8):
                load(n + 10 + i, cols(a["w_gate"][0], 256 * i))
            for i in range(2):
                load(n + 18 + 2 * i, cols(a["w_branch_attn"][0], 512 * i, 512))
                load(n + 19 + 2 * i, cols(a["w_branch_gmlp"][0], 512 * i, 512))
            for i in range(4):
                load(n + 22 + i, cols(a["w_out"][0], 256 * i))
            ffn_loads(1, a["ffn2_w_gate"][0], 0, a["ffn2_w_up"][0], 0, a["ffn2_w_down"][0])
            n, w = N_MIX2, a["w_in_2"][0]
            q0, f0, i0, g0, cq0, ckv0, kpe0 = 0, 1024, 2048, 3072, 4096, 4096 + QL, 4096 + 2 * QL
            ga0 = kpe0 + ROPE
            gb0 = ga0 + D
            load(n, cols(w, cq0))
            load(n + 1, cols(w, ckv0))
            load(n + 2, cols(w, kpe0, ROPE), wview(stage, n + 2, DC, ROPE))
            for i in range(2):
                load(n + 3 + i, cols(w, q0 + 256 * i))
            for i in range(2):
                load(n + 5 + i, cols(a["w_q_b_2"][0], 768 * i, 768), wview(stage, n + 5 + i, 2, 768))
            for i in range(2):
                load(n + 7 + i, cols(a["w_kv_b_2"][0], 1024 * i, 1024))
            for i in range(2, 4):
                load(n + 7 + i, cols(w, q0 + 256 * i))
            for j, src, c0 in ((11, w, f0), (15, w, gb0), (19, w, i0), (23, a["w_mla_o_2"][0], 0), (27, w, g0),
                               (31, w, ga0), (35, a["w_hg_o_2"][0], 0), (39, a["w_out_2"][0], 0)):
                for i in range(4):
                    load(n + j + i, cols(src, c0 + 256 * i))
            ffn_loads(2, a["w_ffn_in_2"][0], 0, a["w_ffn_in_2"][0], FF, a["w_ffn_out_2"][0])
            for i in range(NT):
                for b in range(2):
                    c = slice(512 * b, 512 * b + 512)
                    sp.wait_ge(s["out_copied"], 2 * i + b + 1)
                    sp.dma_start(out[0, P * i:P * (i + 1), c], out_tok[:, i, c]).then_inc(s["store_done"], 16)
            sp.wait_ge(s["store_done"], 2 * 16 * NT)

        @block.gpsimd
        def _(pool):
            chain = [0]

            def seq(ins):
                chain[0] += 1
                ins.then_inc(s["pool_chain"], 1)
                pool.wait_ge(s["pool_chain"], chain[0])

            def sum_squares(dst, src, done, base, chunks=DC):
                pool.wait_ge(s[done], base + 1)
                seq(nc.gpsimd.tensor_tensor(dst, src[:, 0, :], src[:, 1, :], ALU.add))
                for c in range(2, chunks):
                    if c % 2 == 0:
                        pool.wait_ge(s[done], base + c // 2 + 1)
                    last = nc.gpsimd.tensor_tensor(dst, dst, src[:, c, :], ALU.add)
                    if c < chunks - 1:
                        seq(last)
                last.then_inc(s["ss_ready"], 1)

            ssx = ss[:, 0, X0:]
            nc.gpsimd.memset(eps[:], EPS)
            seq(nc.gpsimd.memset(pick[:], 0.0))
            nc.gpsimd.memset(pick[:, HH - 1:HH], 1.0 / P)
            nc.gpsimd.memset(ones[:], 1.0 / D).then_inc(s["ones_ready"], 1)
            pool.wait_ge(s["ws_loaded"], 16)
            nc.gpsimd.affine_select(out=ws, in_=ws, compare_op=ALU.is_ge, fill=0.0, base=0,
                                    pattern=[[0, GG], [-1, GC]], channel_multiplier=1).then_inc(s["ws_masked"], 1)
            sum_squares(ssx, sq, "sq_done", 0, DC - 2)
            nc.gpsimd.dma_start(tab[:], tab_d).then_inc(s["tab_loaded"], 16)
            pool.wait_ge(s["ws_T"], 1)
            nc.gpsimd.dma_start(ln_g, a["gmlp_ln_g"].partition_broadcast(P)).then_inc(s["gm_loaded"], 16)
            nc.gpsimd.dma_start(ln_b, a["gmlp_ln_b"].partition_broadcast(P)).then_inc(s["gm_loaded"], 16)
            for half in range(2):
                src = a["gmlp_b_s"].rearrange("l (c two) i -> l two c i", two=2)[:, half]
                nc.gpsimd.dma_start(gbias[64 * half:64 * half + 64], src.partition_broadcast(64)).then_inc(s["gm_loaded"], 16)
            pool.wait_ge(s["mean_done"], 1)
            sum_squares(ssx, sq, "sq_done", 4)
            pool.wait_ge(s["vln_ready"], 2)
            pool.wait_ge(s["gm_loaded"], 64)
            seq(nc.gpsimd.tensor_tensor(vg, vg, ln_g.unsqueeze(1).to_broadcast([P, NT, GW]), ALU.mult))
            nc.gpsimd.tensor_tensor(vg, vg, ln_b.unsqueeze(1).to_broadcast([P, NT, GW]), ALU.add).then_inc(s["vln_ready"], 1)
            pool.wait_ge(s["evac"], 20)
            nc.gpsimd.tensor_tensor(tA, tA, tB, ALU.add).then_inc(s["merged1"], 1)
            pool.wait_ge(s["mean_done"], 2)
            sum_squares(ssx, sq, "sq_done", 8)
            pool.wait_ge(s["mean_done"], 3)
            sum_squares(ssx, sq, "sq_done", 12)
            pool.wait_ge(s["tab_loaded"], 16)
            pool.wait_ge(s["ss_ready"], 4)
            cos_x = tab[:, T_COS + X0:T_COS + L2].unsqueeze(1).to_broadcast([P, 2, SEQ])
            sin_x = tab[:, T_SIN + X0:T_SIN + L2].unsqueeze(1).to_broadcast([P, 2, SEQ])
            for part, (v, sw, cos, sin) in enumerate(((k_pe, k_sw, tab[:, T_COS:T_COS + L2], tab[:, T_SIN:T_SIN + L2]),
                                                      (q_pe[:, 0:2, :], q_sw[:, 0:2, :], cos_x, sin_x),
                                                      (q_pe[:, 2:4, :], q_sw[:, 2:4, :], cos_x, sin_x))):
                if part == 0:
                    pool.wait_ge(s["evac"], E2 + 3)
                    for d, r in ((0, 32), (32, 0), (64, 96), (96, 64)):
                        seq(nc.gpsimd.tensor_copy(sw[d:d + 32], v[r:r + 32]))
                else:
                    pool.wait_ge(s["swapped"], 4 * part)
                seq(nc.gpsimd.tensor_tensor(v, v, cos, ALU.mult))
                seq(nc.gpsimd.tensor_tensor(sw, sw, sin, ALU.mult))
                nc.gpsimd.tensor_tensor(v, v, sw, ALU.add).then_inc(s["rope_done"], 1)
                pool.wait_ge(s["rope_done"], part + 1)
            pool.wait_ge(s["rstd_ready"], 7)
            pool.wait_ge(s["xlo_done"], 32)
            fg = vec[:, VEC["final_norm"]:]
            for c in range(DC):
                nc.gpsimd.tensor_scalar(h[:, c, :], h[:, c, :], fg[:, c:c + 1], None, ALU.mult).then_inc(s["x2_done"], 1)
            pool.wait_ge(s["x2_done"], DC)
            for c in range(DC):
                nc.gpsimd.tensor_tensor(h[:, c, :], h[:, c, :], rstd[:, 0, X0:], ALU.mult).then_inc(s["x2_done"], 1)
            pool.wait_ge(s["mla_lo"], 4)
            nc.gpsimd.memset(AT, 0.0).then_inc(s["at_zero"], 1)
            sum_squares(ssx, sq, "msq_done", 0, DC - 2)
            pool.wait_ge(s["rstd_ready"], 8)
            sum_squares(ssx, sq, "sq_done", 16)
            pool.wait_ge(s["mean_done"], 6)
            sum_squares(ssx, sq, "ysq_done", 0, DC - 2)

        @block.scalar
        def _(act):
            warmed = [0]

            def load_table(func):
                nc.scalar.activation(warm[:, warmed[0]:warmed[0] + 1], ones[:, 0:1], func)
                warmed[0] += 1

            act.dma_start(ident[:], id_d).then_inc(s["id_loaded"], 16)
            act.dma_start(vrows[0:NVEC, :], vec_d).then_inc(s["vec_loaded"], 16)

            def split_hi(n, it=None):
                if it is None and n >= N_ALL:
                    return
                wait_slab(act, n, it)
                if n >= RING:
                    act.wait_ge(s["slab_used"], up(n - RING + 1, it))
                if it is None and n in (N_MIX2 + 5, N_MIX2 + 6):
                    for dst, src in zip(q_parts(w_hi, n), q_parts(stage, n)):
                        for o, i in zip(dst, src):
                            last = nc.scalar.activation(o, i, ACT.Copy)
                    last.then_inc(s["hi_ready"], 1)
                    return
                if it is None and n == N_MIX2 + 2:
                    o = w_hi[:, n % RING, 0:D].rearrange("p (k two c) -> p k two c", k=DC, two=2)
                    i = wview(stage, n, DC, ROPE).unsqueeze(2).to_broadcast([P, DC, 2, ROPE])
                else:
                    o, i = w_hi[:, n % RING, 0:slab_words(n)], stage[:, n % RING, 0:slab_words(n)]
                nc.scalar.activation(o, i, ACT.Copy).then_inc(s["hi_ready"], 1)

            def squares(b):
                nc.scalar.activation(sq[:, 2 * b:2 * b + 2, :], h[:, 2 * b:2 * b + 2, :], ACT.Square).then_inc(s["sq_done"], 1)

            def input_hi(dst, g, base, bs=range(4)):
                for b in bs:
                    act.wait_ge(s["h_new"], base + b + 1)
                    for c in (2 * b, 2 * b + 1):
                        nc.scalar.activation(dst[:, c, :], h[:, c, :], ACT.Copy, scale=g[:, c:c + 1]).then_inc(s["xhi_done"], 1)
                    squares(b)

            def root(mean, src, dst=std[:, 0, X0:], loaded=False):
                if not loaded:
                    load_table(ACT.Sqrt)
                act.wait_ge(s["mean_done"], mean)
                nc.scalar.activation(dst, src, ACT.Sqrt, bias=eps[:]).then_inc(s["std_ready"], 1)

            def ffn(f, lookahead=True):
                n, J0 = N_FFN[f], PAIRS * f

                def gate(J, m, it=None):
                    if J == J0:
                        split_hi(m + 3, it)
                    act.wait_ge(s["gate_scaled"], up(J + 1, it, 2))
                    nc.scalar.activation(ga_a, ga_s, ACT.Silu).then_inc(s["silu_done"], 1)
                    if J > J0:
                        split_hi(m + 3, it)

                def hidden(J, m, it=None, pf=True):
                    act.wait_ge(s["hidden"], up(J + 1, it, 2))
                    if not (f == 0 and J < 2 and it is None):
                        act.wait_ge(s["slab_used"], up(m - 1, it))
                    nc.scalar.activation(hidden_part(f, 0, J), pair(hid), ACT.Copy).then_inc(s["hid_hi_done"], 1)
                    if pf:
                        split_hi(m + 3, it)

                gate(J0, n)
                hidden(J0, n + 1)
                act.wait_ge(s["meta_T_copied"], 1)
                act.wait_ge(s["up_scaled"], J0 + 1)
                nc.scalar.activation(ps[:, 4:8, :].rearrange("p b c -> p (b c)"), ones[:, 0:1].to_broadcast([P, 4 * 512]),
                                     ACT.Copy, scale=0.0).then_inc(s["y_zeroed"], 1)
                loops = (PAIRS - 1) // 2 if lookahead else (PAIRS - 3) // 2
                with act.Fori(0, loops) as it:
                    for b in range(2):
                        gate(J0 + 1 + b, n + 2 + 3 * b, it)
                        hidden(J0 + 1 + b, n + 3 + 3 * b, it)
                        split_hi(n + 4 + 3 * b + 3, it)
                if not lookahead:
                    last = n + FFN_SLABS - 1
                    for j in (PAIRS - 2, PAIRS - 1):
                        m = n + 3 * j - 1
                        gate(J0 + j, m)
                        hidden(J0 + j, m + 1, pf=m + 4 <= last)
                        if m + 5 <= last:
                            split_hi(m + 5)

            act.wait_ge(s["ones_ready"], 1)
            load_table(ACT.Square)
            act.wait_ge(s["vec_ready"], 1)
            for b in range(4):
                if b in (0, 2):
                    act.wait_ge(s["slab0_in"] if b == 0 else slab_in[0], 16)
                    w = slice(SLAB // 4 * b, SLAB // 4 * b + SLAB // 2)
                    nc.scalar.activation(w_hi[:, 0, w], stage[:, 0, w], ACT.Copy).then_inc(s["hi0_ready" if b == 0 else "hi_ready"], 1)
                input_hi(ffn_input(0)[0], vec[:, VEC["ffn1_norm"]:], 0, [b])
            split_hi(1)
            root(1, ps[:, 3, 0:SEQ])
            split_hi(2)
            act.wait_ge(s["lb_ready"], 1)
            nc.scalar.activation(lb[:, 1:3, :], lb[:, 1:3, :], ACT.Exp).then_inc(s["lb_exp"], 1)
            load_table(ACT.Silu)
            ffn(0)
            input_hi(x_hi[:, :, X0:], vec[:, VEC["mix_norm"]:], 4)
            split_hi(N_MIX1 + 2)
            root(2, ps[:, 4, 0:SEQ])
            root(2, token_means(), rcol[:, 0, 0:2], loaded=True)
            mixer1_act(act, split_hi, input_hi)
            root(3, ps[:, 2 + PAIRS % 2, 0:SEQ])
            load_table(ACT.Silu)
            ffn(1)
            fg = vec[:, VEC["final_norm"]:]
            for b in range(4):
                input_hi(x_hi[:, :, X0:], gfp, 12, [b])
                for c in (2 * b, 2 * b + 1):
                    op = nc.scalar.activation(sq2[:, c, :], h[:, c, :], ACT.Square, scale=fg[:, c:c + 1])
                op.then_inc(s["sq2_done"], 1)
            split_hi(N_MIX2 + 2)
            split_hi(N_MIX2 + 3)
            load_table(ACT.Sqrt)
            act.wait_ge(s["m2_summed"], 1)
            nc.scalar.activation(std[:, 1, :], std[:, 1, :], ACT.Sqrt).then_inc(s["std_ready"], 1)
            root(4, ps[:, 4, 0:SEQ])
            mixer2_act(act, split_hi, load_table)
            root(5, token_means(), rcol[:, 0, 0:2], loaded=True)
            g = vec[:, VEC["ffn_pre_g_2"]:]
            for c in range(2):
                act.wait_ge(s[("h_first", "h_new")[c]], (1, 17)[c])
                nc.scalar.activation(a_hi[:, c, :], h[:, c, :], ACT.Copy, scale=g[:, c:c + 1]).then_inc(s["xhi_done"], 1)
            squares(0)
            input_hi(a_hi, g, 16, (1, 2, 3))
            split_hi(N_FFN[2] + 2)
            root(6, ps[:, 2, 0:SEQ])
            load_table(ACT.Silu)
            ffn(2, lookahead=False)
            for i in range(NT):
                act.wait_ge(s["hT_T"], i + 1)
                nc.scalar.copy(out_tok[:, i, :], ps[:, 2 * i:2 * i + 2, :].rearrange("p b c -> p (b c)")).then_inc(s["hT_copied"], 1)
            pg = vec[:, VEC["ffn_post_g_2"]:]
            for b in range(4):
                if b < 3:
                    act.wait_ge(s["y_bank"], 6 + b + 1)
                else:
                    load_table(ACT.Sqrt)
                    act.wait_ge(s["slab_used"], N_ALL)
                nc.scalar.activation(sq[:, 2 * b:2 * b + 2, :].rearrange("p c t -> p (c t)"), ps[:, 4 + b, :],
                                     ACT.Square).then_inc(s["ysq_done"], 1)
                for c in range(2):
                    nc.scalar.activation(yg[:, 2 * b + c, :], ps[:, 4 + b, SEQ * c:SEQ * c + SEQ], ACT.Copy,
                                         scale=pg[:, 2 * b + c:2 * b + c + 1]).then_inc(s["yg_done"], 1)
            root(7, token_means(), rcol[:, 0, 0:2], loaded=True)

        @block.vector
        def _(dve):
            chain = [0]

            def seq(ins):
                chain[0] += 1
                ins.then_inc(s["dve_chain"], 1)
                dve.wait_ge(s["dve_chain"], chain[0])

            def split_lo(n, it=None):
                if it is None and n >= N_ALL:
                    return
                dve.wait_ge(s["hi_ready"], up(n + 1, it))
                if it is None and n in (N_MIX2 + 5, N_MIX2 + 6):
                    for los, his, src in zip(q_parts(w_lo, n), q_parts(w_hi, n), q_parts(stage, n)):
                        for o, b, i in zip(los, his, src):
                            last = nc.vector.tensor_tensor(o, i, b.bitcast(F32), ALU.subtract)
                    last.then_inc(s["lo_ready"], 1)
                    return
                if it is None and n == N_MIX2 + 2:
                    o, b = (v[:, n % RING, 0:D].rearrange("p (k two c) -> p k two c", k=DC, two=2) for v in (w_lo, w_hi))
                    i = wview(stage, n, DC, ROPE).unsqueeze(2).to_broadcast([P, DC, 2, ROPE])
                else:
                    o, b, i = (v[:, n % RING, 0:slab_words(n)] for v in (w_lo, w_hi, stage))
                nc.vector.tensor_tensor(o, i, b.bitcast(F32), ALU.subtract).then_inc(s["lo_ready"], 1)

            def input_lo(b, g, base, dst=(x_hi[:, :, X0:], x_lo[:, :, X0:]), chunks=(0, 1)):
                for c in (2 * b + j for j in chunks):
                    dve.wait_ge(s["xhi_done"], base + c + 1)
                    nc.vector.scalar_tensor_tensor(out=dst[1][:, c, :], in0=h[:, c, :], scalar=g[:, c:c + 1],
                                                   in1=dst[0][:, c, :].bitcast(F32), op0=ALU.mult,
                                                   op1=ALU.subtract).then_inc(s["xlo_done"], 1)

            def inverse(k, dst=rstd[:, 0, X0:], src=std[:, 0, X0:]):
                dve.wait_ge(s["std_ready"], k)
                nc.vector.reciprocal(dst, src).then_inc(s["rstd_ready"], 1)

            bc2 = rstd[:, 0, X0:].unsqueeze(1).to_broadcast([P, 2, SEQ])

            def ffn(f, rstd_count, lookahead=True):
                n, J0 = N_FFN[f], PAIRS * f
                g0 = 0 if f == 0 else 4

                def gate(J, m, it=None, first=False):
                    dve.wait_ge(s["slab_used"], up(m + 1, it))
                    nc.vector.tensor_tensor(pair(ga_s), ps[:, g0:g0 + 2, 0:SEQ] if first else pair(ps[:, J % 2, :]), bc2,
                                            ALU.mult).then_inc(s["gate_scaled"], 1)
                    if f == 0 and first:
                        spatial_weights_and_meta()
                    split_lo(m + 3, it)

                def hidden(J, m, it=None, pf=True, first=False):
                    dve.wait_ge(s["slab_used"], up(m + 1, it))
                    nc.vector.tensor_tensor(pair(up_s), ps[:, 6:8, 0:SEQ] if first else pair(ps[:, 2 + J % 2, :]), bc2,
                                            ALU.mult).then_inc(s["up_scaled"], 1)
                    dve.wait_ge(s["up_scaled"], up(J + 1, it, 2))
                    dve.wait_ge(s["silu_done"], up(J + 1, it, 2))
                    nc.vector.tensor_tensor(hid, ga_a, up_s, ALU.mult).then_inc(s["hidden"], 1)
                    dve.wait_ge(s["hidden"], up(J + 1, it, 2))
                    dve.wait_ge(s["hid_hi_done"], up(J + 1, it, 2))
                    nc.vector.tensor_tensor(hidden_part(f, 1, J), pair(hid), hidden_part(f, 0, J).bitcast(F32),
                                            ALU.subtract).then_inc(s["hid_lo_done"], 1)
                    if pf:
                        split_lo(m + 3, it)

                inverse(rstd_count)
                dve.wait_ge(s["rstd_ready"], rstd_count)
                gate(J0, n, first=True)
                hidden(J0, n + 1, first=f > 0)
                loops = (PAIRS - 1) // 2 if lookahead else (PAIRS - 3) // 2
                with dve.Fori(0, loops) as it:
                    for b in range(2):
                        gate(J0 + 1 + b, n + 2 + 3 * b, it)
                        hidden(J0 + 1 + b, n + 3 + 3 * b, it)
                        split_lo(n + 4 + 3 * b + 3, it)
                if not lookahead:
                    last = n + FFN_SLABS - 1
                    for j in (PAIRS - 2, PAIRS - 1):
                        m = n + 3 * j - 1
                        gate(J0 + j, m)
                        hidden(J0 + j, m + 1, pf=m + 4 <= last)
                        if m + 5 <= last:
                            split_lo(m + 5)

            def residual(b, scale, y=None):
                hb = h[:, 2 * b:2 * b + 2, :]
                nc.vector.scalar_tensor_tensor(out=hb, in0=pair(ps[:, 4 + b, :]) if y is None else y, scalar=scale, in1=hb,
                                               op0=ALU.mult, op1=ALU.add).then_inc(s["h_new"], 1)

            def add_squares2(b):
                dve.wait_ge(s["sq2_done"], b + 1)
                ss2 = ss[:, 1, X0:]
                if b == 0:
                    seq(nc.vector.tensor_tensor(ss2, sq2[:, 0, :], sq2[:, 1, :], ALU.add))
                    return
                seq(nc.vector.tensor_tensor(ss2, ss2, sq2[:, 2 * b, :], ALU.add))
                last = nc.vector.tensor_tensor(ss2, ss2, sq2[:, 2 * b + 1, :], ALU.add)
                if b == 3:
                    last.then_inc(s["ss2_ready"], 1)
                else:
                    seq(last)

            def ffn_residual(f, g, base, after=None):
                n = N_FFN[f]
                for b in range(4):
                    if b < 3:
                        dve.wait_ge(s["y_bank"], 3 * f + b + 1)
                    else:
                        dve.wait_ge(s["slab_used"], n + FFN_SLABS)
                    residual(b, 0.5)
                    if after is not None and b:
                        after(b - 1)
                    dve.wait_ge(s["h_new"], base // 2 + b + 1)
                    input_lo(b, g, base)

            def spatial_weights_and_meta():
                dve.wait_ge(s["lb_exp"], 1)
                seq(nc.vector.tensor_tensor(lb[:, 3, :], lb[:, 1, :], lb[:, 2, :], ALU.add))
                seq(nc.vector.reciprocal(lb[:, 3, :], lb[:, 3, :]))
                seq(nc.vector.tensor_tensor(lb[:, 4, :], lb[:, 1, :], lb[:, 3, :], ALU.mult))
                seq(nc.vector.tensor_scalar(lb[:, 5, :], lb[:, 4, :], -1.0, 1.0, ALU.mult, ALU.add))
                dve.wait_ge(s["ws_T"], 1)
                nc.vector.tensor_copy(wsT.rearrange("p g i -> p (g i)"), ps[:, 4:6, :].rearrange("p b i -> p (b i)")).then_inc(s["ws_T_copied"], 1)
                dve.wait_ge(s["meta_T"], 1)
                gp = vec[:, VEC["mix_pre_g_2"]:VEC["mix_pre_g_2"] + DC].unsqueeze(2).to_broadcast([P, DC, META])
                nc.vector.tensor_copy(meta[:, 0], ps[:, 6, 0:P].rearrange("p (c t) -> p c t", c=DC)).then_inc(s["meta_T_copied"], 1)
                dve.wait_ge(s["meta_T_copied"], 1)
                seq(nc.vector.tensor_tensor(meta[:, 1], meta[:, 0], meta[:, 0], ALU.mult))
                nc.vector.tensor_reduce(ss[:, 1, 0:META], meta[:, 1].rearrange("p c t -> p t c"), AX_X, ALU.add)
                seq(nc.vector.tensor_tensor(meta[:, 0], meta[:, 0], gp, ALU.mult))
                nc.vector.tensor_copy(x_hi[:, :, 0:META], meta[:, 0]).then_inc(s["meta_hi"], 1)
                dve.wait_ge(s["meta_hi"], 1)
                nc.vector.tensor_tensor(x_lo[:, :, 0:META], meta[:, 0], x_hi[:, :, 0:META].bitcast(F32),
                                        ALU.subtract).then_inc(s["meta_lo"], 1)

            dve.wait_ge(s["vec_T"], 1)
            nc.vector.tensor_copy(vec[:], ps[:, 0, 0:NVEC]).then_inc(s["vec_ready"], 1)
            dve.wait_ge(s["vec_ready"], 1)
            def tokens_in(b):
                dve.wait_ge(s["x_T"], b + 1)
                nc.vector.tensor_copy(h[:, 2 * b:2 * b + 2, :].rearrange("p c t -> p (c t)"), ps[:, 4 + b, :]).then_inc(s["h_new"], 1)

            def first_split_lo(b):
                dve.wait_ge(s["hi0_ready" if b == 0 else "hi_ready"], 1)
                w = slice(SLAB // 2 * b, SLAB // 2 * b + SLAB // 2)
                nc.vector.tensor_tensor(w_lo[:, 0, w], stage[:, 0, w], w_hi[:, 0, w].bitcast(F32),
                                        ALU.subtract).then_inc(s["lo0_ready" if b == 0 else "lo_ready"], 1)

            g = vec[:, VEC["ffn1_norm"]:]
            tokens_in(0)
            first_split_lo(0)
            tokens_in(1)
            dve.wait_ge(s["h_new"], 2)
            input_lo(0, g, 0)
            tokens_in(2)
            input_lo(1, g, 0)
            tokens_in(3)
            first_split_lo(1)
            dve.wait_ge(s["h_new"], 4)
            input_lo(2, g, 0)
            input_lo(3, g, 0)
            split_lo(1)
            l0 = vec[:, VEC["lb_logits_2"]:VEC["lb_logits_2"] + DC]
            l1 = vec[:, VEC["lb_logits_2"] + DC:VEC["lb_logits_2"] + 2 * DC]
            seq(nc.vector.tensor_tensor(lb[:, 0, :], l0, l1, ALU.max))
            seq(nc.vector.tensor_tensor(lb[:, 1, :], l0, lb[:, 0, :], ALU.subtract))
            nc.vector.tensor_tensor(lb[:, 2, :], l1, lb[:, 0, :], ALU.subtract).then_inc(s["lb_ready"], 1)
            nc.vector.tensor_tensor(gfp[:], vec[:, VEC["final_norm"]:VEC["final_norm"] + DC],
                                    vec[:, VEC["mix_pre_g_2"]:VEC["mix_pre_g_2"] + DC], ALU.mult).then_inc(s["gfp_ready"], 1)
            split_lo(2)
            ffn(0, 1)
            ffn_residual(0, vec[:, VEC["mix_norm"]:], 8)
            split_lo(N_MIX1 + 2)
            mixer1_dve(dve, split_lo, seq, input_lo, residual, inverse)
            ffn(1, 5)
            ffn_residual(1, gfp, 24, add_squares2)
            add_squares2(3)
            split_lo(N_MIX2 + 2)
            mixer2_dve(dve, split_lo, seq, inverse, input_lo)
            ffn(2, 9, lookahead=False)
            inverse(10, rcol[:, 1, 0:2], rcol[:, 0, 0:2])
            dve.wait_ge(s["rstd_ready"], 10)
            for i in range(NT):
                for b in range(2):
                    dve.wait_ge(s["yg_T"], 1)
                    o = out_tok[:, i, 512 * b:512 * b + 512]
                    nc.vector.scalar_tensor_tensor(out=o, in0=ps[:, 2 * i + b, :], scalar=rcol[:, 1, i:i + 1], in1=o,
                                                   op0=ALU.mult, op1=ALU.add).then_inc(s["out_copied"], 1)

        @block.tensor
        def _(pe):
            def products(o, wh, wl, xh, xl, start, stop, skip=False):
                nc.tensor.matmul(o, wl, xh, start=start, stop=False, skip_group_check=skip)
                nc.tensor.matmul(o, wh, xl, start=False, stop=False, skip_group_check=skip)
                return nc.tensor.matmul(o, wh, xh, start=False, stop=stop, skip_group_check=skip)

            def slab_ready(n, it=None):
                pe.wait_ge(s["lo_ready"], up(n + 1, it))

            def feature_slab(n, outs, src=(x_hi[:, :, X0:], x_lo[:, :, X0:]), it=None, parts_base=None, parts="xlo_done", counts=range(1, DC + 1)):
                if n == 0:
                    pe.wait_ge(s["lo0_ready"], 1)
                else:
                    slab_ready(n, it)
                wh, wl = wview(w_hi, n, DC), wview(w_lo, n, DC)
                if parts_base is not None:
                    for k in range(DC):
                        if n == 0 and k == 4:
                            slab_ready(n)
                        pe.wait_ge(s[parts], parts_base + counts[k])
                        for c in range(2):
                            last = products(outs[c], wh[:, k, P * c:P * c + P], wl[:, k, P * c:P * c + P],
                                            src[0][:, k, :], src[1][:, k, :], k == 0, k == DC - 1, skip=True)
                    last.then_inc(s["slab_used"], 1)
                    return
                for c in range(2):
                    for k in range(DC):
                        last = products(outs[c], wh[:, k, P * c:P * c + P], wl[:, k, P * c:P * c + P],
                                        src[0][:, k, :], src[1][:, k, :], k == 0, k == DC - 1)
                last.then_inc(s["slab_used"], 1)

            def first_slabs(n, outs, srcs, base, mean):
                def part(j, ks):
                    slab_ready(n + j)
                    wh, wl = wview(w_hi, n + j, DC), wview(w_lo, n + j, DC)
                    for k in ks:
                        pe.wait_ge(s["xlo_done"], base + k + 1)
                        for c in range(2):
                            last = products(outs[j][c], wh[:, k, P * c:P * c + P], wl[:, k, P * c:P * c + P],
                                            srcs[j][0][:, k, :], srcs[j][1][:, k, :], k == 0, k == DC - 1, skip=True)
                    return last

                for k in range(0, DC - 2, 2):
                    part(0, (k, k + 1))
                    part(1, (k, k + 1))
                part(0, (DC - 2, DC - 1)).then_inc(s["slab_used"], 1)
                mean()
                part(1, (DC - 2, DC - 1)).then_inc(s["slab_used"], 1)

            def down_slab(f, n, J, last_one=False, it=None):
                slab_ready(n, it)
                pe.wait_ge(s["hid_lo_done"], up(J + 1, it, 2))
                wh, wl = wview(w_hi, n, 2), wview(w_lo, n, 2)
                hh, hl = hidden_part(f, 0, J), hidden_part(f, 1, J)
                order = [(k, m) for m in range(DC) for k in range(2)] if last_one else [(k, m) for k in range(2) for m in range(DC)]
                for k, m in order:
                    o = ps[:, 4 + m // 2, SEQ * (m % 2):SEQ * (m % 2) + SEQ]
                    last = products(o, wh[:, k, P * m:P * m + P], wl[:, k, P * m:P * m + P], hh[:, k, :], hl[:, k, :],
                                    False, last_one and k == 1, skip=True)
                    if last_one and k == 1 and m in (1, 3, 5):
                        last.then_inc(s["y_bank"], 1)
                last.then_inc(s["slab_used"], 1)

            def halves(bank):
                return [ps[:, bank, 0:SEQ], ps[:, bank, SEQ:2 * SEQ]]

            def mean_mm(k, o, width=SEQ):
                pe.wait_ge(s["ss_ready"], k)
                return nc.tensor.matmul(o, ones[:], ss[:, 0, X0:], start=True, stop=True)

            def turn(src, done):
                for i in range(NT):
                    for c in range(DC):
                        last = nc.tensor.transpose(ps[:, 2 * i + c // 4, P * (c % 4):P * (c % 4) + P], src[:, c, P * i:P * i + P], ident[:])
                    last.then_inc(s[done], 1)

            def spatial_weights_and_meta():
                pe.wait_ge(s["ws_masked"], 1)
                for g in range(GG):
                    last = nc.tensor.transpose(ps[:, 4 + g // 4, P * (g % 4):P * (g % 4) + P], ws[:, g, :], ident[:])
                last.then_inc(s["ws_T"], 1)
                pe.wait_ge(s["meta_loaded"], 16)
                for c in range(DC):
                    last = nc.tensor.transpose(ps[:, 6, META * c:META * c + META], meta_tok[0:META, P * c:P * c + P], ident[0:META, 0:META])
                last.then_inc(s["meta_T"], 1)

            def late_mean(k, squares_done, o):
                pe.wait_ge(s["ss_ready"], k)
                nc.tensor.matmul(o, ones[:], ss[:, 0, X0:], start=True, stop=False)
                pe.wait_ge(s[squares_done], 4)
                nc.tensor.matmul(o, ones[:], sq[:, DC - 2, :], start=False, stop=False)
                nc.tensor.matmul(o, ones[:], sq[:, DC - 1, :], start=False, stop=True).then_inc(s["mean_done"], 1)

            def token_sums(k, squares_done):
                pe.wait_ge(s["ss_ready"], k)
                pe.wait_ge(s[squares_done], 4)
                for i in range(NT):
                    for j, v in enumerate((ss[:, 0, X0:], sq[:, DC - 2, :], sq[:, DC - 1, :])):
                        last = nc.tensor.matmul(ps[:, 4, SEQ + 2 * i:SEQ + 2 * i + 2], v[:, P * i:P * i + P], ones[:, 0:2],
                                                start=j == 0, stop=j == 2)
                last.then_inc(s["mean_done"], 1)

            def ffn(f, base, norm, rec):
                n, J0 = N_FFN[f], PAIRS * f

                def gate(J, m, it=None, first=False):
                    if J >= 1:
                        pe.wait_ge(s["gate_scaled"], up(max(J - 1, 1), it, 2))
                    outs = [ps[:, 0, 0:SEQ], ps[:, 1, 0:SEQ]] if first else halves(J % 2)
                    feature_slab(m, outs, ffn_input(f), it=it, parts_base=base if first else None)

                def upward(J, m, it=None):
                    if J >= 1:
                        pe.wait_ge(s["up_scaled"], up(max(J - 1, 1), it, 2))
                    feature_slab(m, halves(2 + J % 2), ffn_input(f), it=it)

                if f == 0:
                    gate(J0, n, first=True)
                    late_mean(norm, "sq_done", ps[:, 3, 0:SEQ])
                    spatial_weights_and_meta()
                    upward(J0, n + 1)
                    pe.wait_ge(s["std_ready"], rec)
                    pe.wait_ge(s["gate_scaled"], J0 + 1)
                else:
                    first_slabs(n, [[ps[:, 4 + 2 * j, 0:SEQ], ps[:, 5 + 2 * j, 0:SEQ]] for j in range(2)], [ffn_input(f)] * 2, base,
                                lambda: mean_mm(norm, ps[:, 2 + J0 % 2, 0:SEQ]).then_inc(s["mean_done"], 1))
                with pe.Fori(0, (PAIRS - 1) // 2) as it:
                    for b in range(2):
                        J = J0 + 1 + b
                        gate(J, n + 2 + 3 * b, it)
                        upward(J, n + 3 + 3 * b, it)
                        pe.wait_ge(s["y_zeroed"], f + 1)
                        down_slab(f, n + 4 + 3 * b, J - 1, it=it)
                if f == 2:
                    pe.wait_ge(s["hid_lo_done"], 3 * PAIRS)
                    turn(h, "hT_T")
                down_slab(f, n + FFN_SLABS - 1, J0 + PAIRS - 1, last_one=True)

            def token_slab(n, outs):
                slab_ready(n)
                wh, wl = wview(w_hi, n, DC), wview(w_lo, n, DC)
                for t in range(NT):
                    t0 = X0 + P * t
                    for k in range(DC):
                        last = products(outs[t], x_hi[:, k, t0:t0 + P], x_lo[:, k, t0:t0 + P], wh[:, k, :], wl[:, k, :],
                                        k == 0, k == DC - 1)
                last.then_inc(s["slab_used"], 1)

            def branch_slab(n, c0, banks, nk=4, parts=None):
                slab_ready(n)
                wh, wl = wview(w_hi, n, nk), wview(w_lo, n, nk)
                for c in range(4):
                    o = ps[:, banks + c // 2, SEQ * (c % 2):SEQ * (c % 2) + SEQ]
                    for k in range(nk):
                        last = products(o, wh[:, k, P * c:P * c + P], wl[:, k, P * c:P * c + P],
                                        a_hi[:, c0 + k, :], a_lo[:, c0 + k, :], k == 0, k == nk - 1)
                last.then_inc(s["slab_used"], 1)

            def mixer1():
                n = N_MIX1
                order = (0, 2, 1, 3)

                def scores(g):
                    pe.wait_ge(s["evac"], 4)
                    for o, j in enumerate(order):
                        c, r = 2 * g + j // 2, AD * (j % 2)
                        nc.tensor.matmul(ps[:, 6 + o // 2, P * (o % 2):P * (o % 2) + P], qT[r:r + AD, c, 0:P],
                                         kT[r:r + AD, c, 0:P], start=True, stop=True)
                        last = nc.tensor.matmul(ps[:, 4 + o // 2, SEQ * (o % 2):SEQ * (o % 2) + SEQ], qT[r:r + AD, c, P:],
                                                kT[r:r + AD, c, :], start=True, stop=True)
                    last.then_inc(s["s1_mm"], 1)

                def turn_probs(g):
                    pe.wait_ge(s["p1_ready"], 2 * g + 2)
                    for o in range(4):
                        for j in range(3):
                            last = nc.tensor.transpose(ps[:, 4 + o, P * j:P * j + P], S1[:, o, P * j:P * j + P], ident[:])
                        last.then_inc(s["p1_T"], 1)

                def attend(g):
                    pe.wait_ge(s["p1_copied"], 4 * g + 4)
                    for o, j in enumerate(order):
                        v = AD * (4 * g + j)
                        out_ = ps[AD * (j % 2):AD * (j % 2) + AD, 4, SEQ * (j // 2):SEQ * (j // 2) + SEQ]
                        nc.tensor.matmul(out_, V1[:, 0, v:v + AD], pT1[:, o, 0:SEQ], start=True, stop=False)
                        last = nc.tensor.matmul(out_[:, P:], V1[:, 1, v:v + AD], pT1[:, o, SEQ:], start=False, stop=True)
                    last.then_inc(s["pv1_mm"], 1)

                def spatial():
                    pe.wait_ge(s["vln_ready"], 3)
                    for g in range(GG):
                        for t in range(NT):
                            c = g // 2
                            o = ps[GD * (g % 2):GD * (g % 2) + GD, 5 + c // 2, SEQ * (c % 2) + P * t:SEQ * (c % 2) + P * t + P]
                            last = nc.tensor.matmul(o, vg[:, t, GD * g:GD * g + GD], wsT[:, g, :], start=True, stop=True)
                    last.then_inc(s["mixed_mm"], 1)

                def mean():
                    mean_mm(2, ps[:, 4, 0:SEQ])
                    for t in range(NT):
                        last = nc.tensor.matmul(ps[:, 4, SEQ + 2 * t:SEQ + 2 * t + 2], ss[:, 0, X0 + P * t:X0 + P * t + P],
                                                ones[:, 0:2], start=True, stop=True)
                    last.then_inc(s["mean_done"], 1)

                x = (x_hi[:, :, X0:], x_lo[:, :, X0:])
                first_slabs(n, [[ps[:, b, 0:SEQ] for b in (0, 1)], [ps[:, b, 0:SEQ] for b in (2, 3)]], [x, x], 8, mean)
                for i in range(2, 26):
                    if 3 <= i < 22:
                        pe.wait_ge(s["evac"], i - 1)
                    k = 6 if i == 2 else 2 * (i % 2)
                    outs = [ps[:, k, 0:SEQ], ps[:, k + 1, 0:SEQ]]
                    if i in (4, 5, 8, 9):
                        token_slab(n + i, outs)
                    elif i < 18:
                        feature_slab(n + i, outs)
                    elif i < 22:
                        if i == 18:
                            pe.wait_ge(s["attn_lo"], 2)
                        if i == 19:
                            pe.wait_ge(s["gm_lo"], 1)
                        branch_slab(n + i, 4 * (i % 2), k)
                    else:
                        o = mixer_out(i - 22)
                        feature_slab(n + i, [o[:, 0, :], o[:, 1, :]], parts_base=0 if i == 22 else None, parts="m_lo", counts=(1, 1, 1, 1, 2, 2, 3, 3))
                    if i == 4:
                        pe.wait_ge(s["std_ready"], 3)
                        scores(0)
                    if i == 8:
                        turn_probs(0)
                    if i == 9:
                        attend(0)
                    if i == 10:
                        pe.wait_ge(s["attn_lo"], 1)
                        scores(1)
                    if i == 13:
                        turn_probs(1)
                    if i == 14:
                        attend(1)
                    if i == 15:
                        spatial()

            def mixer2():
                n = N_MIX2
                xs, xf = (x_hi[:, :, X0:], x_lo[:, :, X0:]), (x_hi, x_lo)

                def one_chunk_slab(n, o):
                    slab_ready(n)
                    wh, wl = wview(w_hi, n, DC, P), wview(w_lo, n, DC, P)
                    for k in range(DC):
                        last = products(o, wh[:, k, :], wl[:, k, :], x_hi[:, k, :], x_lo[:, k, :], k == 0, k == DC - 1)
                    last.then_inc(s["slab_used"], 1)

                def q_slab(n, banks, rope_bank):
                    slab_ready(n)
                    wh, wl = wview(w_hi, n, 2, 768), wview(w_lo, n, 2, 768)
                    for j in range(4):
                        o = ps[:, banks + j // 2, SEQ * (j % 2):SEQ * (j % 2) + SEQ]
                        for k in range(2):
                            c = NOPE * j
                            products(o, wh[:, k, c:c + NOPE], wl[:, k, c:c + NOPE], a_hi[:, k, :], a_lo[:, k, :], k == 0, k == 1)
                    for j in range(2):
                        for k in range(2):
                            c = 4 * NOPE + 2 * ROPE * j
                            last = products(ps[:, rope_bank, SEQ * j:SEQ * j + SEQ], wh[:, k, c:c + P], wl[:, k, c:c + P], a_hi[:, k, :], a_lo[:, k, :], k == 0, k == 1)
                    last.then_inc(s["slab_used"], 1)

                def kv_slab(n, banks, spare, i):
                    slab_ready(n)
                    wh, wl = wview(w_hi, n, 2), wview(w_lo, n, 2)
                    ch, cl = kv_part(a_hi), kv_part(a_lo)
                    for j in (1, 0, 2, 3):
                        if i == 8 and j in (0, 2):
                            pe.wait_ge(s["kv_left"], j // 2 + 1)
                        o = ps[:, (banks + j) if j < 2 else 2 + j, 0:L2]
                        for k in range(2):
                            c = (NOPE + VH) * j
                            products(o, wh[:, k, c:c + NOPE], wl[:, k, c:c + NOPE], ch[:, k, :], cl[:, k, :], k == 0, k == 1)
                    if i == 7:
                        pe.wait_ge(s["evac"], E2 + 7)
                    else:
                        pe.wait_ge(s["evac"], E2 + 8)
                    for t, bank in zip(TILES, (spare, 6, 7)):
                        for k in range(2):
                            vh, vl = (v[:, k, :].rearrange("p (h c) -> p h c", h=4)[:, :, NOPE:] for v in (wh, wl))
                            o = ps[:, bank, :].rearrange("p (h c) -> p h c", h=4)
                            last = products(o, ch[:, k, t:t + P], cl[:, k, t:t + P], vh, vl, k == 0, k == 1)
                    last.then_inc(s["slab_used"], 1)

                def scores(p):
                    for hh in range(2):
                        hd, r = 2 * p + hh, ROPE * hh
                        for o, t, nk in ((ps[:, 5 + hh, 0:K0], 0, K0), (ps[:, 5 + hh, K0:K0 + L2], P, L2)):
                            nc.tensor.matmul(o, qn[:, hd, t:t + P], kn[:, hd, 0:nk], start=True, stop=False)
                            last = nc.tensor.matmul(o, q_pe[r:r + ROPE, p, t:t + P], k_pe[r:r + ROPE, 0:nk], start=False, stop=True)
                    last.then_inc(s["s2_mm"], 1)

                def turn_probs(p):
                    pe.wait_ge(s["p2_ready"], 2 * p + 2)
                    for hh in range(2):
                        for j, c in enumerate((META, K0 + META, K0 + META + P)):
                            nc.tensor.transpose(ps[:, 5 + hh, P * j:P * j + P], S2[:, hh, c:c + P], ident[:])
                        for t in range(NT):
                            last = nc.tensor.transpose(ps[0:META, 4, SEQ * hh + P * t:SEQ * hh + P * t + P],
                                                       S2[:, hh, K0 * t:K0 * t + META], ident[:])
                    last.then_inc(s["p2_T"], 1)

                def attend(p):
                    pe.wait_ge(s["p2_copied"], 2 * p + 2)
                    if p:
                        pe.wait_ge(s["mla_lo"], p)
                    for hh in range(2):
                        v = VH * (2 * p + hh)
                        o = ps[:, 7, SEQ * hh:SEQ * hh + SEQ]
                        nc.tensor.matmul(o, V2[:, 0, v:v + VH], pT2[:, hh, 0:SEQ], start=True, stop=False)
                        nc.tensor.matmul(o[:, P:], V2[:, 1, v:v + VH], pT2[:, hh, SEQ:], start=False, stop=False)
                        last = nc.tensor.matmul(o, V2m[0:META, v:v + VH], pT2m[0:META, hh, :], start=False, stop=True)
                    last.then_inc(s["pv2_mm"], 1)

                def level(l):
                    if l == 0:
                        pe.wait_ge(s["f_ready"], 4)
                        pe.wait_ge(s["silu2_done"], 4)
                        pe.wait_ge(s["mla_lo"], 4)
                    else:
                        pe.wait_ge(s["hg_ready"], l)
                        pe.wait_ge(s["lvl_done"], 4 * l)
                    if l == 5:
                        pe.wait_ge(s["v_copied"], 2)
                    size = LEVELS[l]
                    for hd in range(HH):
                        for t in range(NT):
                            o = ps[:, 4 + hd // 2, SEQ * (hd % 2) + P * t:SEQ * (hd % 2) + P * t + P]
                            q = q2[:, hd, P * t:P * t + P]
                            if size:
                                o, q = (v.rearrange("p (b two s) -> p b two s", two=2, s=size)[:, :, 1, :] for v in (o, q))
                            last = nc.tensor.matmul(o, k2[:, hd, X0 + P * t:X0 + P * t + P], q, start=True, stop=True)
                    last.then_inc(s["lvl_mm"], 1)

                def turn_v():
                    pe.wait_ge(s["evac"], E2 + 23)
                    for hd in range(HH):
                        last = nc.tensor.transpose(ps[0:META, hd // 4, P * (hd % 4):P * (hd % 4) + P], hiT[:, hd, 0:META], ident[:])
                    last.then_inc(s["vm_T"], 1)
                    pe.wait_ge(s["lvl_done"], 20)
                    for t in range(NT):
                        for hd in range(HH):
                            last = nc.tensor.transpose(ps[:, 4 + 2 * t + hd // 4, P * (hd % 4):P * (hd % 4) + P],
                                                       hiT[:, hd, X0 + P * t:X0 + P * t + P], ident[:])
                    last.then_inc(s["vT"], 1)

                def meta_scores(hd, bank):
                    for t, km in enumerate((k2[:, hd, 0:META], meta[:, 0, hd, :])):
                        c = SEQ * (hd % 2) + P * t
                        last = nc.tensor.matmul(ps[0:META, bank, c:c + P], km, q2[:, hd, P * t:P * t + P], start=True, stop=True)
                    return last

                def cross():
                    pe.wait_ge(s["hg_ready"], 8)
                    pe.wait_ge(s["lvl_done"], 32)
                    for hd in range(HH):
                        nc.tensor.matmul(ps[:, 4 + hd // 4, P * (hd % 4):P * (hd % 4) + P], k2[:, hd, X0:X0 + P],
                                         q2[:, hd, P:], start=True, stop=True)
                    for hd in range(4):
                        last = meta_scores(hd, 6 + hd // 2)
                    last.then_inc(s["cross_mm"], 1)

                def recurrence_out():
                    pe.wait_ge(s["am_copied"], 1)
                    for hd in range(HH):
                        o = ps[:, 4 + hd // 2, SEQ * (hd % 2):SEQ * (hd % 2) + SEQ]
                        v = P * hd
                        nc.tensor.matmul(o, V2[:, 0, v:v + P], AT[:, hd, 0:2, :].rearrange("p j t -> p (j t)"), start=True, stop=False)
                        nc.tensor.matmul(o[:, P:], V2[:, 1, v:v + P], AT[:, hd, 2, :], start=False, stop=False)
                        last = nc.tensor.matmul(o, V2m[0:META, v:v + P], Am[0:META, hd, :], start=False, stop=True)
                        if hd % 2:
                            last.then_inc(s["o_mm"], 1)

                def means():
                    pe.wait_ge(s["ss_ready"], 4)
                    pe.wait_ge(s["ss2_ready"], 1)
                    nc.tensor.matmul(ps[:, 4, 0:SEQ], ones[:], ss[:, 0, X0:], start=True, stop=True)
                    nc.tensor.matmul(ps[:, 5, 0:L2], ones[:], ss[:, 1, :], start=True, stop=True).then_inc(s["mean_done"], 1)

                first_slabs(n, [[ps[:, 0, 0:SEQ], ps[:, 1, 0:SEQ]], [ps[:, 2, 0:L2], ps[:, 3, 0:L2]]], [xs, xf], 24, means)
                for i in range(2, 43):
                    if 3 <= i < 39:
                        pe.wait_ge(s["evac"], E2 + i - 1)
                    if i == 9:
                        pe.wait_ge(s["kv_left"], 5)
                    k = 2 * (i % 2)
                    if i in FULL:
                        feature_slab(n + i, [ps[:, k, 0:L2], ps[:, k + 1, 0:L2]], xf)
                    elif i == 2:
                        one_chunk_slab(n + i, ps[:, 7, 0:L2])
                    elif i in (5, 6):
                        if i == 5:
                            pe.wait_ge(s["ac_lo"], 4)
                        else:
                            pe.wait_ge(s["cstd_ready"], 3)
                        q_slab(n + i, k, 12 - i)
                    elif i in (7, 8):
                        kv_slab(n + i, k, 2 - k, i)
                    elif i < 39:
                        if i == 23:
                            pe.wait_ge(s["mla_lo"], 4)
                        if i == 24:
                            pe.wait_ge(s["vm_copied"], 1)
                        if i == 35:
                            pe.wait_ge(s["o_lo"], 2)
                        src = (a_hi, a_lo) if 23 <= i < 27 or i >= 35 else xs
                        feature_slab(n + i, [ps[:, k, 0:SEQ], ps[:, k + 1, 0:SEQ]], src)
                    else:
                        o = mixer_out(i - 39)
                        feature_slab(n + i, [o[:, 0, :], o[:, 1, :]], parts_base=0 if i == 39 else None, parts="m2_lo", counts=(1, 1, 2, 2, 3, 3, 4, 4))
                    if i == 3:
                        pe.wait_ge(s["css_ready"], 2)
                        pe.wait_ge(s["std_ready"], 7)
                        nc.tensor.matmul(ps[:, 4, 0:SEQ], ones[:], ss[:, 0, X0:], start=True, stop=True)
                        nc.tensor.matmul(ps[:, 5, 0:L2], ones[:], ss[:, 1, :], start=True, stop=True)
                        for j, t in enumerate(TILES):
                            last = nc.tensor.matmul(ps[:, 6, 2 * j:2 * j + 2], ss[:, 1, t:t + P], ones[:, 0:2], start=True, stop=True)
                        last.then_inc(s["cmean_mm"], 1)
                    if i in MLA_T:
                        turn_probs(MLA_T[i])
                    if i in MLA_PV:
                        attend(MLA_PV[i])
                    if i in MLA_S:
                        p = MLA_S[i]
                        if p == 0:
                            pe.wait_ge(s["evac"], E2 + 9)
                            pe.wait_ge(s["rope_done"], 3)
                        scores(p)
                    if i in LSLOT:
                        level(LSLOT[i])
                    if i == 23:
                        turn_v()
                    if i == 27:
                        cross()
                    if i == 28:
                        pe.wait_ge(s["cross_copied"], 2)
                        for hd in range(4, 8):
                            last = meta_scores(hd, 4 + (hd - 4) // 2)
                        last.then_inc(s["am_mm"], 1)
                    if i == 29:
                        recurrence_out()
                    if i == 30:
                        for hd in range(HH):
                            if hd % 4 == 0:
                                pe.wait_ge(s["osq_done"], hd // 4 + 1)
                            last = nc.tensor.matmul(ps[0:HH, 4, 0:SEQ], pick[:, HH - 1 - hd:2 * HH - 1 - hd], k2[:, hd, 0:SEQ],
                                                    start=hd == 0, stop=hd == HH - 1)
                        last.then_inc(s["osum_mm"], 1)
                    if i == 31:
                        pe.wait_ge(s["orec_ready"], 1)
                        pe.wait_ge(s["o_ready"], 2)
                        for hd in range(HH):
                            last = nc.tensor.matmul(ps[:, 4 + hd // 2, SEQ * (hd % 2):SEQ * (hd % 2) + SEQ],
                                                    ident[0:HH, hd:hd + 1].to_broadcast([HH, P]), std[0:HH, 0, 0:SEQ], start=True, stop=True)
                        last.then_inc(s["obc_mm"], 1)
                token_sums(5, "msq_done")
                pe.wait_ge(s["rstd_ready"], 8)
                for i in range(NT):
                    last = nc.tensor.matmul(ps[:, 0, P * i:P * i + P], rcol[:, 1, i:i + 1].to_broadcast([P, P]), ident[:], start=True, stop=True)
                last.then_inc(s["spread"], 1)

            pe.wait_ge(s["id_loaded"], 16)
            pe.wait_ge(s["vec_loaded"], 16)
            nc.tensor.transpose(ps[:, 0, 0:NVEC], vrows[0:NVEC, :], ident[0:NVEC, 0:NVEC]).then_inc(s["vec_T"], 1)
            for c in range(DC):
                pe.wait_ge(s[f"x_loaded{c // 4}"], 16)
                for i in range(NT):
                    last = nc.tensor.transpose(ps[:, 4 + c // 2, SEQ * (c % 2) + P * i:SEQ * (c % 2) + P * i + P],
                                               x_tok[:, i, P * c:P * c + P], ident[:])
                if c % 2:
                    last.then_inc(s["x_T"], 1)
            pe.wait_ge(s["ones_ready"], 1)
            pe.wait_ge(s["vec_ready"], 1)
            ffn(0, 0, 1, 1)
            mixer1()
            ffn(1, 16, 3, 5)
            mixer2()
            ffn(2, 32, 6, 9)
            for k in range(4):
                if k == 3:
                    token_sums(7, "ysq_done")
                pe.wait_ge(s["yg_done"], 2 * k + 2)
                if k == 0:
                    pe.wait_ge(s["hT_copied"], 2)
                for c in (2 * k, 2 * k + 1):
                    for i in range(NT):
                        last = nc.tensor.transpose(ps[:, 2 * i + c // 4, P * (c % 4):P * (c % 4) + P], yg[:, c, P * i:P * i + P], ident[:])
            last.then_inc(s["yg_T"], 1)


_INS = [
    "x", "ffn1_norm", "ffn1_w_gate", "ffn1_w_up", "ffn1_w_down", "mix_norm", "w_in", "gmlp_ln_g", "gmlp_ln_b",
    "gmlp_w_s", "gmlp_b_s", "w_branch_attn", "w_branch_gmlp", "w_gate", "b_gate", "w_out", "ffn2_norm",
    "ffn2_w_gate", "ffn2_w_up", "ffn2_w_down", "final_norm", "meta_tokens_2", "w_in_2", "b_gate_2",
    "lb_logits_2", "hg_norm_g_2", "w_hg_o_2", "q_a_norm_g_2", "w_q_b_2", "kv_a_norm_g_2", "w_kv_b_2",
    "w_mla_o_2", "w_out_2", "mix_pre_g_2", "mix_post_g_2", "ffn_pre_g_2", "ffn_post_g_2", "w_ffn_in_2",
    "w_ffn_out_2"]


def kernel(**inputs):
    import concourse.bacc as _bacc
    from concourse.bass_utils import run_bass_kernel_spmd as _run

    nc = _bacc.Bacc("TRN2", target_bir_lowering=False, num_devices=1)
    arrays, args = {}, {}

    def give(name, value):
        v = np.ascontiguousarray(value)
        arrays[f"in_{name}_dram"] = v
        return nc.dram_tensor(f"in_{name}_dram", v.shape, mybir.dt.from_np(v.dtype), kind="ExternalInput").ap()

    packed = [name for name, _ in VEC_ROWS]
    for name in _INS:
        if name in packed:
            continue
        args[name] = give(name, inputs[name])
    vec_d = give("vectors", np.concatenate([np.asarray(inputs[name]).reshape(-1, P) for name, _ in VEC_ROWS]))
    id_d = give("identity", np.eye(P, dtype=np.float32))
    tab_d = give("tables", constants())
    out = nc.dram_tensor("out_0_dram", (1, SEQ, D), F32, kind="ExternalOutput").ap()
    program(nc, args, vec_d, id_d, tab_d, out)
    r = _run(nc, [arrays], core_ids=[0])
    return r.results[0]["out_0_dram"]
```
